# Optimizing a Trainium2 kernel written in Bass

```python
import math
import jax
import jax.numpy as jnp
from jax import lax
import numpy as np
import jax, jax.numpy as jnp

D_MODEL = 1024
BATCH = 1
SEQ = 512
DEPTH = 4

N_MIXERS = 3
N_FOX_LAYERS = (DEPTH + 2) // 3
N_GLA_LAYERS = (DEPTH + 1) // 3
N_GDN_LAYERS = DEPTH // 3
RMS_EPS = 1e-6

FOX_HEADS = 8
FOX_HEAD_DIM = D_MODEL // FOX_HEADS
FOX_WIDTH = FOX_HEADS * FOX_HEAD_DIM
FOX_BLOCK = 128
FOX_FGATE_BIAS = 3.0
FOX_IN_DIM = 4 * FOX_WIDTH + FOX_HEADS

GLA_HEADS = 4
GLA_KEY_DIM = D_MODEL // 2 // GLA_HEADS
GLA_VAL_DIM = D_MODEL // GLA_HEADS
GLA_WIDTH = GLA_HEADS * GLA_VAL_DIM
GLA_RANK = 16
GLA_TAU = 16.0
GLA_CHUNK = 64
GLA_IN_DIM = 2 * GLA_HEADS * GLA_KEY_DIM + 2 * GLA_WIDTH + GLA_RANK

GDN_QK_HEADS = 4
GDN_V_HEADS = 8
GDN_HEAD_DIM = D_MODEL // GDN_V_HEADS
GDN_WIDTH = GDN_V_HEADS * GDN_HEAD_DIM
GDN_CONV = 4
GDN_CHUNK = 64
GDN_CONV_DIM = 2 * GDN_QK_HEADS * GDN_HEAD_DIM + GDN_WIDTH
GDN_IN_DIM = GDN_CONV_DIM + GDN_WIDTH + 2 * GDN_V_HEADS


def rms_norm(x, w):
    xf = x.astype(jnp.float32)
    y = xf * lax.rsqrt(jnp.mean(xf * xf, axis=-1, keepdims=True) + RMS_EPS)
    return (y * w.astype(jnp.float32)).astype(x.dtype)

def l2_norm(x):
    xf = x.astype(jnp.float32)
    return xf * lax.rsqrt(jnp.sum(xf * xf, axis=-1, keepdims=True) + RMS_EPS)

def to_chunks(t, chunk):
    b, s, h = t.shape[:3]
    t = t.reshape((b, s // chunk, chunk, h) + t.shape[3:])
    return jnp.moveaxis(t, 3, 1)

def from_chunks(t):
    b, h, nc, l, d = t.shape
    return jnp.moveaxis(t, 1, 3).reshape(b, nc * l, h, d)

def causal_conv(u, w):
    k, c = w.shape
    return lax.conv_general_dilated(u, w[:, None, :].astype(u.dtype), window_strides=(1,), padding=[(k - 1, 0)], dimension_numbers=('NWC', 'WIO', 'NWC'), feature_group_count=c)

def fox_mixer(xn, w_in, b_f, q_gain, k_gain, w_out):
    bsz, s, _ = xn.shape
    h, dh = FOX_HEADS, FOX_HEAD_DIM
    q, k, v, z, f_logit = jnp.split(xn @ w_in, [FOX_WIDTH, 2 * FOX_WIDTH, 3 * FOX_WIDTH, 4 * FOX_WIDTH], axis=-1)
    q = rms_norm(q.reshape(bsz, s, h, dh), q_gain).transpose(0, 2, 1, 3)
    k = rms_norm(k.reshape(bsz, s, h, dh), k_gain).transpose(0, 2, 1, 3)
    v = v.reshape(bsz, s, h, dh).transpose(0, 2, 1, 3)
    log_f = jax.nn.log_sigmoid((f_logit + b_f).astype(jnp.float32))
    cum = jnp.cumsum(log_f, axis=1).transpose(0, 2, 1)
    nb = s // FOX_BLOCK
    q_blocks = q.reshape(bsz, h, nb, FOX_BLOCK, dh).transpose(2, 0, 1, 3, 4)
    c_blocks = cum.reshape(bsz, h, nb, FOX_BLOCK).transpose(2, 0, 1, 3)
    pos_blocks = jnp.arange(s).reshape(nb, FOX_BLOCK)
    key_pos = jnp.arange(s)
    scale = dh ** -0.5

    def attend_block(blk):
        qb, cb, pb = blk
        logits = jnp.einsum('bhqd,bhkd->bhqk', qb, k).astype(jnp.float32) * scale + (cb[..., :, None] - cum[..., None, :])
        logits = jnp.where(pb[:, None] >= key_pos[None, :], logits, -jnp.inf)
        p = jax.nn.softmax(logits, axis=-1).astype(v.dtype)
        return jnp.einsum('bhqk,bhkd->bhqd', p, v)

    o = lax.map(attend_block, (q_blocks, c_blocks, pos_blocks))
    o = o.transpose(1, 0, 3, 2, 4).reshape(bsz, s, FOX_WIDTH)
    return (o * jax.nn.silu(z)) @ w_out

def gla_mixer(xn, w_in, w_gate_up, b_gate, o_gain, w_out):
    bsz, s, _ = xn.shape
    h, dk, dv, L = GLA_HEADS, GLA_KEY_DIM, GLA_VAL_DIM, GLA_CHUNK
    f32 = jnp.float32
    qk_w = h * dk
    q, k, v, z, g_low = jnp.split(xn @ w_in, [qk_w, 2 * qk_w, 2 * qk_w + GLA_WIDTH, 2 * qk_w + 2 * GLA_WIDTH], axis=-1)
    log_a = jax.nn.log_sigmoid((g_low @ w_gate_up + b_gate).astype(f32)) / GLA_TAU
    qc = to_chunks(q.reshape(bsz, s, h, dk).astype(f32) * dk ** -0.5, L)
    kc = to_chunks(k.reshape(bsz, s, h, dk).astype(f32), L)
    vc = to_chunks(v.reshape(bsz, s, h, dv).astype(f32), L)
    ac = to_chunks(log_a.reshape(bsz, s, h, dk), L)
    bcum = jnp.cumsum(ac, axis=3)
    b_last = bcum[..., -1:, :]
    q_dec = qc * jnp.exp(bcum)
    k_inv = kc * jnp.exp(-bcum)
    k_dec = kc * jnp.exp(b_last - bcum)
    causal = jnp.tril(jnp.ones((L, L), dtype=bool))
    attn = jnp.where(causal, jnp.einsum('bhnld,bhnmd->bhnlm', q_dec, k_inv), 0.0)
    o_intra = jnp.einsum('bhnlm,bhnmv->bhnlv', attn, vc)

    def step(state, inp):
        qd, kd, vv, dec = inp
        o = jnp.einsum('bhld,bhdv->bhlv', qd, state)
        state = state * dec[..., :, None] + jnp.einsum('bhld,bhlv->bhdv', kd, vv)
        return state, o

    xs = (jnp.moveaxis(q_dec, 2, 0), jnp.moveaxis(k_dec, 2, 0), jnp.moveaxis(vc, 2, 0), jnp.moveaxis(jnp.exp(b_last[..., 0, :]), 2, 0))
    state0 = jnp.zeros((bsz, h, dk, dv), f32)
    _, o_inter = lax.scan(step, state0, xs)
    o = o_intra + jnp.moveaxis(o_inter, 0, 2)
    o = rms_norm(from_chunks(o), o_gain).reshape(bsz, s, GLA_WIDTH).astype(xn.dtype)
    return (o * jax.nn.silu(z)) @ w_out

def gdn_mixer(xn, w_in, conv_w, a_log, dt_bias, o_gain, w_out):
    bsz, s, _ = xn.shape
    hq, hv, d, L = GDN_QK_HEADS, GDN_V_HEADS, GDN_HEAD_DIM, GDN_CHUNK
    f32 = jnp.float32
    qkv, z, a, b = jnp.split(xn @ w_in, [GDN_CONV_DIM, GDN_CONV_DIM + GDN_WIDTH, GDN_CONV_DIM + GDN_WIDTH + hv], axis=-1)
    qkv = jax.nn.silu(causal_conv(qkv, conv_w))
    q, k, v = jnp.split(qkv, [hq * d, 2 * hq * d], axis=-1)
    rep = hv // hq
    q = jnp.repeat(l2_norm(q.reshape(bsz, s, hq, d)), rep, axis=2) * d ** -0.5
    k = jnp.repeat(l2_norm(k.reshape(bsz, s, hq, d)), rep, axis=2)
    v = v.reshape(bsz, s, hv, d).astype(f32)
    beta = jax.nn.sigmoid(b.astype(f32))
    g = -jnp.exp(a_log) * jax.nn.softplus(a.astype(f32) + dt_bias)
    qc, kc, vc = to_chunks(q, L), to_chunks(k, L), to_chunks(v, L)
    bc = to_chunks(beta, L)
    gc = jnp.cumsum(to_chunks(g, L), axis=-1)
    causal = jnp.tril(jnp.ones((L, L), dtype=bool))
    strict = jnp.tril(jnp.ones((L, L), dtype=bool), k=-1)
    diff = gc[..., :, None] - gc[..., None, :]
    decay = jnp.where(causal, jnp.exp(jnp.where(causal, diff, 0.0)), 0.0)
    kb = kc * bc[..., None]
    vb = vc * bc[..., None]
    tri = jnp.where(strict, jnp.einsum('bhnld,bhnmd->bhnlm', kb, kc) * decay, 0.0) + jnp.eye(L, dtype=f32)
    u = lax.linalg.triangular_solve(tri, vb, left_side=True, lower=True)
    w = lax.linalg.triangular_solve(tri, kb * jnp.exp(gc)[..., None], left_side=True, lower=True)
    qk = jnp.einsum('bhnld,bhnmd->bhnlm', qc, kc) * decay
    q_dec = qc * jnp.exp(gc)[..., None]
    g_last = gc[..., -1]
    k_dec = kc * jnp.exp(g_last[..., None] - gc)[..., None]

    def step(state, inp):
        uu, ww, qkk, qd, kd, dec = inp
        v_new = uu - jnp.einsum('bhld,bhdv->bhlv', ww, state)
        o = jnp.einsum('bhld,bhdv->bhlv', qd, state) + jnp.einsum('bhlm,bhmv->bhlv', qkk, v_new)
        state = state * dec[..., None, None] + jnp.einsum('bhld,bhlv->bhdv', kd, v_new)
        return state, o

    xs = tuple(jnp.moveaxis(t, 2, 0) for t in (u, w, qk, q_dec, k_dec, jnp.exp(g_last)))
    state0 = jnp.zeros((bsz, hv, d, d), f32)
    _, o_inter = lax.scan(step, state0, xs)
    o = from_chunks(jnp.moveaxis(o_inter, 0, 2))
    o = rms_norm(o, o_gain).reshape(bsz, s, GDN_WIDTH).astype(xn.dtype)
    return (o * jax.nn.silu(z)) @ w_out

def first_inputs(seed: int = 0) -> dict:
    key = jax.random.key(seed)
    ks = jax.random.split(key, 20)
    f32 = jnp.float32

    def nrm(k, shape, scale):
        return jax.random.normal(k, shape, f32) * scale

    x = nrm(ks[0], (BATCH, SEQ, D_MODEL), 1.0)
    norm_w = 1.0 + nrm(ks[1], (DEPTH, D_MODEL), 0.02)
    fox_w_in = nrm(ks[2], (N_FOX_LAYERS, D_MODEL, FOX_IN_DIM), D_MODEL ** -0.5)
    fox_b_f = FOX_FGATE_BIAS + nrm(ks[3], (N_FOX_LAYERS, FOX_HEADS), 0.5)
    fox_q_gain = 1.0 + nrm(ks[4], (N_FOX_LAYERS, FOX_HEAD_DIM), 0.02)
    fox_k_gain = 1.0 + nrm(ks[5], (N_FOX_LAYERS, FOX_HEAD_DIM), 0.02)
    fox_w_out = nrm(ks[6], (N_FOX_LAYERS, FOX_WIDTH, D_MODEL), FOX_WIDTH ** -0.5)
    gla_w_in = nrm(ks[7], (N_GLA_LAYERS, D_MODEL, GLA_IN_DIM), D_MODEL ** -0.5)
    gla_w_gate_up = nrm(ks[8], (N_GLA_LAYERS, GLA_RANK, GLA_HEADS * GLA_KEY_DIM), GLA_RANK ** -0.5)
    gla_b_gate = nrm(ks[9], (N_GLA_LAYERS, GLA_HEADS * GLA_KEY_DIM), 0.1)
    gla_o_gain = 1.0 + nrm(ks[10], (N_GLA_LAYERS, GLA_VAL_DIM), 0.02)
    gla_w_out = nrm(ks[11], (N_GLA_LAYERS, GLA_WIDTH, D_MODEL), GLA_WIDTH ** -0.5)
    gdn_w_in = nrm(ks[12], (N_GDN_LAYERS, D_MODEL, GDN_IN_DIM), D_MODEL ** -0.5)
    gdn_conv_w = nrm(ks[13], (N_GDN_LAYERS, GDN_CONV, GDN_CONV_DIM), GDN_CONV ** -0.5)
    gdn_a_log = jnp.log(jax.random.uniform(ks[14], (N_GDN_LAYERS, GDN_V_HEADS), f32, minval=1.0, maxval=16.0))
    dt = jnp.exp(jax.random.uniform(ks[15], (N_GDN_LAYERS, GDN_V_HEADS), f32, minval=math.log(1e-3), maxval=math.log(1e-1)))
    gdn_dt_bias = dt + jnp.log(-jnp.expm1(-dt))
    gdn_o_gain = 1.0 + nrm(ks[16], (N_GDN_LAYERS, GDN_HEAD_DIM), 0.02)
    gdn_w_out = nrm(ks[17], (N_GDN_LAYERS, GDN_WIDTH, D_MODEL), GDN_WIDTH ** -0.5)
    return {'x': x, 'norm_w': norm_w,
            'fox_w_in': fox_w_in, 'fox_b_f': fox_b_f, 'fox_q_gain': fox_q_gain, 'fox_k_gain': fox_k_gain, 'fox_w_out': fox_w_out,
            'gla_w_in': gla_w_in, 'gla_w_gate_up': gla_w_gate_up, 'gla_b_gate': gla_b_gate, 'gla_o_gain': gla_o_gain, 'gla_w_out': gla_w_out,
            'gdn_w_in': gdn_w_in, 'gdn_conv_w': gdn_conv_w, 'gdn_a_log': gdn_a_log, 'gdn_dt_bias': gdn_dt_bias, 'gdn_o_gain': gdn_o_gain, 'gdn_w_out': gdn_w_out}

def first_block(x, norm_w, fox_w_in, fox_b_f, fox_q_gain, fox_k_gain, fox_w_out, gla_w_in, gla_w_gate_up, gla_b_gate, gla_o_gain, gla_w_out, gdn_w_in, gdn_conv_w, gdn_a_log, gdn_dt_bias, gdn_o_gain, gdn_w_out):
    for layer in range(DEPTH):
        xn = rms_norm(x, norm_w[layer])
        kind, idx = layer % N_MIXERS, layer // N_MIXERS
        if kind == 0:
            y = fox_mixer(xn, fox_w_in[idx], fox_b_f[idx], fox_q_gain[idx], fox_k_gain[idx], fox_w_out[idx])
        elif kind == 1:
            y = gla_mixer(xn, gla_w_in[idx], gla_w_gate_up[idx], gla_b_gate[idx], gla_o_gain[idx], gla_w_out[idx])
        else:
            y = gdn_mixer(xn, gdn_w_in[idx], gdn_conv_w[idx], gdn_a_log[idx], gdn_dt_bias[idx], gdn_o_gain[idx], gdn_w_out[idx])
        x = x + y.astype(x.dtype)
    return x


DEPTH_2 = 2

CHUNK = 64
Q_BLOCK = 128
N_MIXERS_2 = 2
ATTN_HEADS = 8
ATTN_HEAD_DIM = 64
ATTN_WIDTH = ATTN_HEADS * 2 * ATTN_HEAD_DIM
ROPE_DIM = ATTN_HEAD_DIM // 4
ROPE_THETA = 500000.0
CONV_WIDTH = 3
CONV_CH = D_MODEL
D_FF = -(-8 * D_MODEL // (3 * 256)) * 256
ALPHA = (2 * DEPTH_2) ** 0.25
BETA = (8 * DEPTH_2) ** -0.25
N_ATTN_LAYERS = (DEPTH_2 + 1) // 2
N_CONV_LAYERS = DEPTH_2 // 2
LN_EPS = 1e-5
NEG_INF = -1e30


def layer_norm(x, g, b):
    xf = x.astype(jnp.float32)
    mu = jnp.mean(xf, axis=-1, keepdims=True)
    xc = xf - mu
    var = jnp.mean(xc * xc, axis=-1, keepdims=True)
    y = xc * lax.rsqrt(var + LN_EPS) * g.astype(jnp.float32) + b.astype(jnp.float32)
    return y.astype(x.dtype)

def rms_norm_2(x, g):
    xf = x.astype(jnp.float32)
    y = xf * lax.rsqrt(jnp.mean(xf * xf, axis=-1, keepdims=True) + LN_EPS) * g.astype(jnp.float32)
    return y.astype(x.dtype)

def rope_tables(seq):
    pos = jnp.arange(seq, dtype=jnp.float32)
    inv = ROPE_THETA ** (-jnp.arange(0, ROPE_DIM, 2, dtype=jnp.float32) / ROPE_DIM)
    ang = pos[:, None] * inv[None, :]
    return jnp.cos(ang), jnp.sin(ang)

def partial_rotary(x, cos, sin):
    half = ROPE_DIM // 2
    c = cos[None, :, None, None, :].astype(x.dtype)
    s = sin[None, :, None, None, :].astype(x.dtype)
    x1 = x[..., :half]
    x2 = x[..., half:ROPE_DIM]
    rot = jnp.concatenate([x1 * c - x2 * s, x2 * c + x1 * s], axis=-1)
    return jnp.concatenate([rot, x[..., ROPE_DIM:]], axis=-1)

def lambda_init_fn(layer_idx):
    return 0.8 - 0.6 * math.exp(-0.3 * layer_idx)

def diff_attention(x, w_qkv, w_o, lq1, lk1, lq2, lk2, g_sub, lam_init):
    B, S, _ = x.shape
    H, Dh = ATTN_HEADS, ATTN_HEAD_DIM
    qkv = jnp.einsum('bsd,de->bse', x, w_qkv)
    q = qkv[..., :ATTN_WIDTH].reshape(B, S, H, 2, Dh)
    k = qkv[..., ATTN_WIDTH:2 * ATTN_WIDTH].reshape(B, S, H, 2, Dh)
    v = qkv[..., 2 * ATTN_WIDTH:].reshape(B, S, H, 2 * Dh)
    cos, sin = rope_tables(S)
    q = partial_rotary(q, cos, sin) * (Dh ** -0.5)
    k = partial_rotary(k, cos, sin)
    f32 = jnp.float32
    lam = (jnp.exp(jnp.sum(lq1.astype(f32) * lk1.astype(f32)))
           - jnp.exp(jnp.sum(lq2.astype(f32) * lk2.astype(f32))) + lam_init)
    nb = S // Q_BLOCK
    q_blocks = jnp.moveaxis(q.reshape(B, nb, Q_BLOCK, H, 2, Dh), 1, 0)
    key_chunk = jnp.arange(S) // CHUNK

    def one_block(args):
        q_blk, bi = args
        s = jnp.einsum('bqhcd,bkhcd->bhcqk', q_blk, k).astype(f32)
        q_chunk = (bi * Q_BLOCK + jnp.arange(Q_BLOCK)) // CHUNK
        mask = key_chunk[None, :] <= q_chunk[:, None]
        s = jnp.where(mask, s, NEG_INF)
        p = jax.nn.softmax(s, axis=-1)
        a = p[:, :, 0] - lam * p[:, :, 1]
        return jnp.einsum('bhqk,bkhe->bqhe', a.astype(v.dtype), v)

    o = lax.map(one_block, (q_blocks, jnp.arange(nb)))
    o = jnp.moveaxis(o, 0, 1).reshape(B, S, H, 2 * Dh)
    o = rms_norm_2(o, g_sub) * (1.0 - lam_init)
    return jnp.einsum('bse,ed->bsd', o.reshape(B, S, ATTN_WIDTH), w_o)

def short_gated_conv(x, w_in, w_conv, w_out):
    bcx = jnp.einsum('bsd,de->bse', x, w_in)
    b_gate = bcx[..., :CONV_CH]
    c_gate = bcx[..., CONV_CH:2 * CONV_CH]
    xt = bcx[..., 2 * CONV_CH:]
    u = c_gate * xt
    y = lax.conv_general_dilated(
        u, w_conv[:, None, :], window_strides=(1,),
        padding=[(CONV_WIDTH - 1, 0)],
        dimension_numbers=('NWC', 'WIO', 'NWC'),
        feature_group_count=CONV_CH)
    return jnp.einsum('bsc,cd->bsd', b_gate * y, w_out)

def swiglu(x, w_gate, w_up, w_down):
    h = jax.nn.silu(jnp.einsum('bsd,df->bsf', x, w_gate)) * jnp.einsum('bsd,df->bsf', x, w_up)
    return jnp.einsum('bsf,fd->bsd', h, w_down)

def second_inputs(seed: int = 0) -> dict:
    key = jax.random.key(seed)
    ks = jax.random.split(key, 18)
    f32 = jnp.float32

    def nrm(k, shape, scale):
        return jax.random.normal(k, shape, f32) * scale

    NA, NC, Dh = N_ATTN_LAYERS, N_CONV_LAYERS, ATTN_HEAD_DIM
    return {
        'x': nrm(ks[0], (BATCH, SEQ, D_MODEL), 1.0),
        'attn_w_qkv': nrm(ks[1], (NA, D_MODEL, 3 * ATTN_WIDTH), D_MODEL ** -0.5),
        'attn_w_o': nrm(ks[2], (NA, ATTN_WIDTH, D_MODEL), ATTN_WIDTH ** -0.5 * BETA),
        'attn_lambda_q1': nrm(ks[3], (NA, Dh), 0.1),
        'attn_lambda_k1': nrm(ks[4], (NA, Dh), 0.1),
        'attn_lambda_q2': nrm(ks[5], (NA, Dh), 0.1),
        'attn_lambda_k2': nrm(ks[6], (NA, Dh), 0.1),
        'attn_subln_g': 1.0 + nrm(ks[7], (NA, 2 * Dh), 0.02),
        'conv_w_in': nrm(ks[8], (NC, D_MODEL, 3 * CONV_CH), D_MODEL ** -0.5),
        'conv_w': nrm(ks[9], (NC, CONV_WIDTH, CONV_CH), CONV_WIDTH ** -0.5),
        'conv_w_out': nrm(ks[10], (NC, CONV_CH, D_MODEL), CONV_CH ** -0.5 * BETA),
        'ffn_w_gate': nrm(ks[11], (DEPTH_2, D_MODEL, D_FF), D_MODEL ** -0.5),
        'ffn_w_up': nrm(ks[12], (DEPTH_2, D_MODEL, D_FF), D_MODEL ** -0.5),
        'ffn_w_down': nrm(ks[13], (DEPTH_2, D_FF, D_MODEL), D_FF ** -0.5 * BETA),
        'ln1_g': 1.0 + nrm(ks[14], (DEPTH_2, D_MODEL), 0.02),
        'ln1_b': nrm(ks[15], (DEPTH_2, D_MODEL), 0.02),
        'ln2_g': 1.0 + nrm(ks[16], (DEPTH_2, D_MODEL), 0.02),
        'ln2_b': nrm(ks[17], (DEPTH_2, D_MODEL), 0.02),
    }

def second_block(x, attn_w_qkv, attn_w_o, attn_lambda_q1, attn_lambda_k1, attn_lambda_q2,
              attn_lambda_k2, attn_subln_g, conv_w_in, conv_w, conv_w_out,
              ffn_w_gate, ffn_w_up, ffn_w_down, ln1_g, ln1_b, ln2_g, ln2_b):
    h = x
    for i in range(DEPTH_2):
        j = i // N_MIXERS_2
        if i % N_MIXERS_2 == 0:
            m = diff_attention(h, attn_w_qkv[j], attn_w_o[j], attn_lambda_q1[j],
                               attn_lambda_k1[j], attn_lambda_q2[j], attn_lambda_k2[j],
                               attn_subln_g[j], lambda_init_fn(i))
        else:
            m = short_gated_conv(h, conv_w_in[j], conv_w[j], conv_w_out[j])
        h = layer_norm(ALPHA * h + m, ln1_g[i], ln1_b[i])
        h = layer_norm(ALPHA * h + swiglu(h, ffn_w_gate[i], ffn_w_up[i], ffn_w_down[i]),
                       ln2_g[i], ln2_b[i])
    return h


def setup_inputs(seed=0):
    out = dict(first_inputs(seed))
    for name, value in second_inputs(seed + 1).items():
        if name != "x":
            out[name + "_2"] = value
    return out


def reference(
    x, norm_w, fox_w_in, fox_b_f, fox_q_gain, fox_k_gain, fox_w_out, gla_w_in, gla_w_gate_up,
    gla_b_gate, gla_o_gain, gla_w_out, gdn_w_in, gdn_conv_w, gdn_a_log, gdn_dt_bias, gdn_o_gain,
    gdn_w_out, attn_w_qkv_2, attn_w_o_2, attn_lambda_q1_2, attn_lambda_k1_2, attn_lambda_q2_2,
    attn_lambda_k2_2, attn_subln_g_2, conv_w_in_2, conv_w_2, conv_w_out_2, ffn_w_gate_2,
    ffn_w_up_2, ffn_w_down_2, ln1_g_2, ln1_b_2, ln2_g_2, ln2_b_2,
):
    x = first_block(
        x, norm_w, fox_w_in, fox_b_f, fox_q_gain, fox_k_gain, fox_w_out, gla_w_in,
        gla_w_gate_up, gla_b_gate, gla_o_gain, gla_w_out, gdn_w_in, gdn_conv_w, gdn_a_log,
        gdn_dt_bias, gdn_o_gain, gdn_w_out,
    )
    return second_block(
        x, attn_w_qkv_2, attn_w_o_2, attn_lambda_q1_2, attn_lambda_k1_2, attn_lambda_q2_2,
        attn_lambda_k2_2, attn_subln_g_2, conv_w_in_2, conv_w_2, conv_w_out_2, ffn_w_gate_2,
        ffn_w_up_2, ffn_w_down_2, ln1_g_2, ln1_b_2, ln2_g_2, ln2_b_2,
    )


_drawn_inputs = setup_inputs


def setup_inputs(seed=0):
    import zlib

    import numpy as np

    out = dict(_drawn_inputs(seed))
    spreads = {}
    factors = {'fox_q_gain': 8.0,
     'fox_k_gain': 8.0,
     'gla_o_gain': 3.705,
     'gdn_o_gain': 5.068,
     'attn_lambda_q1_2': 171.264,
     'attn_lambda_q2_2': 8.0,
     'attn_lambda_k2_2': 8.0,
     'attn_subln_g_2': 126.862,
     'attn_lambda_k1_2': 8.0}
    for name, (base, spread) in spreads.items():
        noise = np.random.default_rng([zlib.crc32(name.encode()), seed]).standard_normal(out[name].shape)
        drawn = base * np.exp(spread * noise) if base else spread * noise
        out[name] = jnp.asarray(drawn.astype(out[name].dtype))
    for name, factor in factors.items():
        out[name] = (out[name] * factor).astype(out[name].dtype)
    return out
```

```python
from contextlib import ExitStack

import concourse.bass as bass
import numpy as np
from concourse import mybir

F32 = mybir.dt.float32
F32R = mybir.dt.float32r
BF16 = mybir.dt.bfloat16
ALU = mybir.AluOpType
ACT = mybir.ActivationFunctionType
AX = mybir.AxisListType.X

P = 128
SEQ = 512
D = 1024
TT = SEQ // P
KT = D // P
COLS = 512
HALF = 4
D_FF = 2816
FT = D_FF // P
FOX_HEADS = 8
GLA_HEADS = 4
GLA_RANK = 16
GDN_QK = 4
GDN_V = 8
ATTN_HEADS = 8
CHUNK = 64
RMS_EPS = 1e-6
LN_EPS = 1e-5
ALPHA = 4 ** 0.25
NEG = -1e30
LAM_INIT = 0.8 - 0.6
LAYERS = ("fox", "gla", "gdn", "fox", "attn", "ffn", "conv", "ffn")
SWAP = [*range(8, 16), *range(8), *range(16, 32)]
ACT_STEPS = (1, 2, 3, 5, 6, 8, 10, 11, 12, 13, 15, 16)
DVE_STEPS = (1, 4, 7, 9, 11, 14, 17)
LAST_STEP = 17
RECURRENCE_AFTER = (3, 7, 11, 15)


def rotary_tables():
    half = 8
    inv = np.power(np.float32(500000.0), -np.arange(0, 2 * half, 2, dtype=np.float32) / np.float32(2 * half))
    angle = np.arange(SEQ, dtype=np.float32)[None, :] * inv[:, None].astype(np.float32)
    table = np.zeros((2, P, SEQ), np.float32)
    table[0] = 1.0
    for c in range(0, P, P // 2):
        for m, sign in enumerate((-1.0, 1.0)):
            table[0, c + half * m:c + half * m + half] = np.cos(angle)
            table[1, c + half * m:c + half * m + half] = sign * np.sin(angle)
    return table


def block_masks():
    row, col = np.arange(P)[:, None], np.arange(P)[None, :]
    same = row // CHUNK == col // CHUNK
    block = row // 16 == col // 16
    return np.stack([block & (col < row), same & ~block & (col < row), same]).astype(np.float32)


PREP_LOADS = {"fox": 4, "gla": 4, "gdn": 9, "attn": 7, "conv": 3}


def plan(layers):
    stages = []
    at = dict(pair=0, full=0, filled=0, act=0, dve=0, gated=0, small=0, loads=0, rms=0, roots=0,
              squares=0, norms=0, mixer={})

    def stage(kind, pairs=0, panels=0, full=0, filled=0, act=0, dve=0, gated=0,
              small=0, loads=0, rms=0, roots=0, squares=0, norms=0, **more):
        st = dict(kind=kind, panels=panels, n_full=full, n_act=act, n_dve=dve, **{k: at[k] for k in at if k != "mixer"})
        st.update(more)
        st["nth"] = at["mixer"].get(kind, 0)
        at["mixer"][kind] = st["nth"] + 1
        before = stages[-1] if stages else None
        st["free0"] = (st["act"], st["dve"])
        if before and before["kind"] in ("project", "ffn_up") and kind in ("project", "ffn_up", "ffn_down"):
            st["free0"] = (st["act"] - before["n_act"] // before["panels"], st["dve"] - before["n_dve"] // before["panels"])
        stages.append(st)
        for key, n in (("pair", pairs), ("full", full), ("filled", filled), ("act", act), ("dve", dve),
                       ("gated", gated), ("small", small), ("loads", loads), ("rms", rms),
                       ("roots", roots), ("squares", squares), ("norms", norms)):
            at[key] += n

    def fill(norm, which=0):
        stage("fill", filled=8, dve=8, norm=norm, which=which, rms=int(norm == "rms"),
              roots=TT * (norm != "plain"))

    def project(weights, layer, col, panels, rows, by, to, gated=0):
        stage("project", pairs=panels, panels=panels, full=3 * panels, weights=weights, layer=layer, col=col,
              rows=rows, by=by, to=to, act=4 * panels * (by == "act"), dve=4 * panels * (by == "dve"), gated=gated,
              keep=ALPHA if weights in ("attn_w_o_2", "conv_w_out_2") else 1.0)

    n_fox = n_ffn = 0
    for n, name in enumerate(layers):
        if n == 0 and name in ("ffn", "conv"):
            fill("plain")
        if name == "fox":
            fill("rms", n)
            stage("prep", layer_kind="fox", layer=n_fox, small=1, loads=PREP_LOADS["fox"])
            project("fox_w_in", n_fox, 0, 2, False, "dve", "A")
            project("fox_w_in", n_fox, D, 2, False, "dve", "B")
            project("fox_w_in", n_fox, 3 * D, 2, False, "act", "silu D")
            project("fox_w_in", n_fox, 2 * D, 2, True, "dve", "C")
            stage("fox", layer=n_fox, gated=KT, squares=16, norms=1, roots=1)
            project("fox_w_out", n_fox, 0, 2, True, "dve", "residual")
            n_fox += 1
        if name == "gla":
            fill("rms", n)
            stage("prep", layer_kind="gla", layer=0, small=1, loads=PREP_LOADS["gla"])
            project("gla_w_in", 0, 2 * D, 2, False, "act", "silu D")
            project("gla_w_in", 0, 0, 2, False, "dve", "A")
            project("gla_w_in", 0, D, 2, True, "dve", "C")
            stage("gla", gated=KT, squares=8, norms=1, roots=1)
            project("gla_w_out", 0, 0, 2, True, "dve", "residual")
        if name == "gdn":
            fill("rms", n)
            stage("prep", layer_kind="gdn", layer=0, small=1, loads=PREP_LOADS["gdn"])
            project("gdn_w_in", 0, 0, 4, False, "dve", "conv")
            project("gdn_w_in", 0, 2 * D, 2, False, "act", "silu D")
            stage("gdn", gated=KT, squares=16, norms=2, roots=2)
            project("gdn_w_out", 0, 0, 2, True, "dve", "residual")
        if name == "attn":
            fill("plain")
            stage("prep", layer_kind="attn", layer=0, small=0, loads=PREP_LOADS["attn"])
            project("attn_w_qkv_2", 0, 0, 2, False, "dve", "rotary A")
            project("attn_w_qkv_2", 0, D, 2, False, "dve", "rotary B")
            project("attn_w_qkv_2", 0, 2 * D, 2, True, "act", "copy C")
            stage("attn", gated=KT, squares=8, norms=1, roots=1)
            project("attn_w_o_2", 0, 0, 2, True, "dve", "residual")
            fill("ln1", n_ffn)
        if name == "conv":
            stage("prep", layer_kind="conv", layer=0, small=0, loads=PREP_LOADS["conv"])
            project("conv_w_in_2", 0, D, 2, False, "act", "copy A")
            project("conv_w_in_2", 0, 2 * D, 2, False, "dve", "gated conv")
            project("conv_w_in_2", 0, 0, 2, False, "dve", "gate G", gated=KT)
            project("conv_w_out_2", 0, 0, 2, True, "dve", "residual")
            fill("ln1", n_ffn)
        if name == "ffn":
            stage("ffn_up", pairs=11, panels=11, full=33, act=22, dve=22, layer=n_ffn)
            stage("ffn_down", pairs=6, panels=2, full=6, dve=8, layer=n_ffn)
            if n == len(layers) - 1:
                stage("last_norm", layer=n_ffn)
            else:
                fill("ln2", n_ffn)
            n_ffn += 1
    if layers[-1] != "ffn":
        stage("store")
    return stages, at


def six_mixer_stack(nc, t, out):
    stages, total = plan(LAYERS)
    n_pairs = total["pair"]
    ctx = ExitStack()
    with ctx:
        base = -(-nc.sbuf_base // 64) * 64
        KB = 1024

        def sb(name, offset_kb, shape, dt=F32):
            return nc.alloc_sbuf_tensor_at(name, shape, dt, offset=base + int(offset_kb * KB))

        raw = sb("weights_raw", 0, [P, 2, HALF, COLS])
        w_hi = sb("weights_high", 16, [P, 2, HALF, COLS], F32R)
        w_lo = sb("weights_low", 32, [P, 2, HALF, COLS], F32R)
        x = sb("x", 48, [P, TT, D])
        xt_hi = sb("xt_high", 64, [P, KT, SEQ], F32R)
        xt_lo = sb("xt_low", 80, [P, KT, SEQ], F32R)
        buf_a = sb("A", 96, [P, 8, SEQ])
        buf_b = sb("B", 112, [P, 8, SEQ])
        buf_c = sb("C", 128, [P, 8, SEQ])
        buf_d = sb("D", 144, [P, 8, SEQ])
        c_rows = buf_c[:].rearrange("p (t c) n -> p t (c n)", t=TT)
        g_hi = sb("gated_high", 160, [P, KT, SEQ], F32R)
        g_lo = sb("gated_low", 176, [P, KT, SEQ], F32R)
        xn = sb("x_normalised", 96, [P, TT, D])
        h_hi = sb("hidden_high", 96, [P, FT, SEQ], F32R)
        h_lo = sb("hidden_low", 140, [P, FT, SEQ], F32R)
        gate_act = sb("gate_activated", 184, [P, 2, SEQ])
        hidden = sb("hidden", 188, [P, 2, SEQ])
        norm_w = sb("norm_weight_rows", 192, [P, D])
        norm_b = sb("norm_bias_rows", 196, [P, D])
        C0 = 200
        N_CONSTS = 8
        ident = sb("identity", C0, [P, P])
        ones = sb("ones", C0 + .5, [P, P])
        tri = sb("triangle", C0 + 1, [P, P])
        chunk_tri = sb("chunk_triangle", C0 + 1.5, [P, P])
        ident_b = sb("identity_bf16", C0 + 2, [P, P], BF16)
        mask_b = sb("causal_mask", C0 + 2.25, [P, P], BF16)
        mask2_b = sb("chunk_mask", C0 + 2.5, [P, P], BF16)
        stat = sb("row_statistics", C0 + 2.75, [P, 32])
        soft = sb("softmax_statistics", C0 + 2.875, [P, 32])
        s_raw = sb("small_raw", C0 + 3, [P, KT, 16])
        s_hi = sb("small_high", C0 + 3.5, [P, KT, 16], F32R)
        s_lo = sb("small_low", C0 + 4, [P, KT, 16], F32R)
        cols = sb("columns", C0 + 4.5, [P, 96])
        vec = sb("vectors", C0 + 4.875, [P, 64])
        logf = sb("log_forget", C0 + 5.125, [P, 32])
        logf_e = sb("log_forget_part", C0 + 5.25, [P, 32])
        cum_rows = sb("cumulated_rows", C0 + 5.375, [P, SEQ])
        pick = sb("column_pick", C0 + 7.375, [P, 31])
        q_n = sb("q_normalised", 64, [P, 2, SEQ])
        k_n = sb("k_normalised", 68, [P, 2, SEQ])
        squares = sb("squares", 72, [P, 2, SEQ])
        probs = sb("probs", 76, [P, 2, SEQ])
        probs_t = sb("probs_transposed", 80, [P, 2, TT, SEQ])
        pair_probs = sb("pair_probs", 64, [P, 2, 2, SEQ])
        rotary = sb("rotary_tables", 192, [P, 2, SEQ])
        rotary_in = sb("rotary_source", 196, [P, SEQ])
        rotary_sin = sb("rotary_shuffled", 198, [P, SEQ])
        lam_rows = sb("lambda_vectors", C0 + 5.375, [P, 4, 64])
        lam_work = sb("lambda_work", C0 + 6.375, [P, 64])
        low_rank = sb("gate_low_rank", 64, [P, SEQ])
        resets = sb("chunk_resets", 66, [P, SEQ])
        gate_abs = sb("gate_absolute", 68, [P, 2, SEQ])
        gate_log = sb("gate_logarithm", 72, [P, 2, SEQ])
        grown = sb("inverse_decay", 76, [P, 2, SEQ])
        decayed = sb("decay", 80, [P, GLA_HEADS, SEQ])
        gla_state = sb("gla_state", 88, [P, 2, GLA_HEADS * 256])
        k_rows = sb("keys_decayed_rows", 64, [P, TT, GLA_HEADS * P])
        inner = sb("scores_in_chunks", 72, [P, 2, GLA_HEADS, P])
        up_rows = sb("gate_up_weights", C0 + 5.375, [P, SEQ])
        def heads(name, offset_kb):
            return sb(name, offset_kb, [P, GDN_V, P])

        key_rows = sb("key_rows", 64, [P, TT, GDN_QK * P])
        w_t = [heads(f"w_transposed_{m}", 80 + 4 * m) for m in range(2)]
        k_dec = [heads(f"keys_decayed_{m}", 88 + 4 * m) for m in range(2)]
        q_dec = [heads(f"queries_decayed_{m}", 112 + 4 * m) for m in range(2)]
        qk_dec = [heads(f"scores_decayed_{m}", 120 + 4 * m) for m in range(2)]
        cross, inverse, x1, x2, x3, x4 = [heads(n, 160 + 4 * m) for m, n in enumerate(
            ("cross_blocks", "inverse_transposed", "solve_1", "solve_2", "solve_3", "solve_4"))]
        delta_state = heads("delta_state", 184)
        v_new = heads("values_new", 188)
        u_rows = buf_c[:].rearrange("p (t c) (a n) -> p t (c a) n", t=TT, n=P)
        masks = sb("block_masks", 196, [P, 3, P])
        in_block, across_blocks, same_chunk = masks[:, 0], masks[:, 1], masks[:, 2]
        small = sb("gate_columns", 197.5, [P, 8, 32])
        chunk_decay = sb("chunk_decay", 198.5, [P, TT, GDN_V, 2])
        selector = sb("row_selector", 192, [P, 16, P])
        gated_conv = sb("gated_convolution", 198, [P, SEQ])
        gated = sb("gated", 72, [P, SEQ])
        norm_r = sb("norm_reciprocals", 74, [P, SEQ])
        norm_u = sb("norm_mean_squares", 76, [P, SEQ])
        norm_t = sb("norm_newton", 78, [P, SEQ])

        bank = [ctx.enter_context(nc.psum_tensor(f"bank{n}", [P, SEQ], F32)) for n in range(8)]

        def sem(name):
            return ctx.enter_context(nc.semaphore(name))

        w_loaded = [sem("even_slot_loaded"), sem("odd_slot_loaded")]
        w_high = sem("slot_high_done")
        w_split = sem("slot_split")
        w_used = [sem("even_slot_used"), sem("odd_slot_used")]
        bank_full = sem("bank_full")
        fill_full = sem("fill_bank_full")
        act_freed = sem("banks_freed_by_act")
        dve_freed = sem("banks_freed_by_dve")
        x_loaded = [sem(f"x_tile_{tt}_loaded") for tt in range(TT)]
        rows_loaded = sem("norm_rows_loaded")
        rows_ready = sem("token_tile_normalised")
        out_rows = sem("output_tile_normalised")
        sumsq = sem("sum_of_squares")
        xt_high = sem("xt_high_done")
        dve_step = sem("dve_own_step")
        act_step = sem("act_own_step")
        pool_step = sem("pool_own_step")
        consts = sem("constants_ready")
        gated_raw = sem("gated_raw_done")
        gated_high = sem("gated_high_done")
        gated_low = sem("gated_low_done")
        h_high = sem("hidden_high_done")
        h_low = sem("hidden_low_done")
        stored = sem("stored")
        mixer_loaded = sem("mixer_vectors_loaded")
        small_split = sem("small_weights_split")
        small_full = sem("small_logits_full")
        squares_done = sem("squares_done")
        squares_used = sem("squares_used")
        sums_full = sem("norm_sums_full")
        root_in = sem("root_wanted")
        root_out = sem("root_done")
        rows_r = sem("norm_rows_done")
        fox = {n: sem("fox_" + n) for n in (
            "consts", "logits", "log", "cum_in", "cum_full", "cum_rows", "norm_full", "qk_ready", "scores",
            "exps", "normed", "max", "turned", "turned_used", "out_full")}

        diff = {n: sem("attn_" + n) for n in (
            "selector", "lam_in", "lam_out", "scores", "max", "exps", "mixed", "turned", "turned_used", "out_full",
            "out_taken", "spread")}

        gla = {n: sem("gla_" + n) for n in (
            "low", "low_turned", "low_rows", "gates", "abs", "log", "sums", "decays", "keys", "keys_turned", "keys_rows",
            "inner_full", "inner", "out_full", "out_taken", "update", "state", "spread")}

        gdn = {n: sem("gdn_" + n) for n in (
            "silu", "logits", "logs", "g", "sums", "columns", "exps", "factors", "spread", "qk_ready", "keys_full",
            "keys_rows", "values_full", "values_rows", "ws", "v_new", "update", "state", "out_full", "out_taken",
            "norm_spread")}
        solve = {n: [sem(f"gdn_{n}_{g}") for g in range(2)] for n in (
            "build_full", "differences", "decays", "lower", "full", "act", "dve", "kbg")}

        def solved(eng, g, tt, n, also=("act", "dve")):
            for name, steps in (("act", ACT_STEPS), ("dve", DVE_STEPS)):
                if n in steps and name in also:
                    eng.wait_ge(solve[name][g], len(steps) * tt + steps.index(n) + 1)

        def small_columns(name, layer, c0, n):
            return s_raw[:, :, 0:n], t[name][layer].rearrange("(kt p) n -> p kt n", p=P)[:, :, c0:c0 + n]

        def column(ap):
            return ap.rearrange("(p a) -> p a", a=1)

        def across(ap, times=1):
            return bass.AP(tensor=ap.tensor, offset=ap.offset, ap=[[0, P], [0, times]] + [list(d) for d in ap.ap])

        def prep_loads(st):
            kind, layer = st["layer_kind"], st["layer"]
            if kind == "fox":
                return [small_columns("fox_w_in", layer, 4 * D, FOX_HEADS),
                        (cols[:, 0:1], column(t["fox_q_gain"][layer])),
                        (cols[:, 1:2], column(t["fox_k_gain"][layer])),
                        (vec[:, 0:32].rearrange("p (t n) -> p t n", n=8), across(t["fox_b_f"][layer], TT))]
            if kind == "gla":
                return [small_columns("gla_w_in", 0, 3 * D, GLA_RANK), (up_rows[0:GLA_RANK], t["gla_w_gate_up"][0]),
                        (cols[:, 0:4], t["gla_b_gate"][0].rearrange("(n p) -> p n", p=P)),
                        (cols[:, 4:6], t["gla_o_gain"][0].rearrange("(n p) -> p n", p=P))]
            if kind == "attn":
                return [(rotary[:, m], t["rotary"][m]) for m in range(2)] + [
                    (lam_rows[:, m:m + 1], across(t[f"attn_lambda_{n}_2"][0]))
                    for m, n in enumerate(("q1", "k1", "q2", "k2"))] + [(cols[:, 0:1], column(t["attn_subln_g_2"][0]))]
            if kind == "conv":
                return [(cols[:, 8 * k:8 * k + 8], t["conv_w_2"][0][k].rearrange("(n p) -> p n", p=P))
                        for k in range(3)]
            if kind == "gdn":
                return [small_columns("gdn_w_in", 0, 3 * D, 2 * GDN_V)] + [
                    (cols[:, 16 * k:16 * k + 16], t["gdn_conv_w"][0][k].rearrange("(n p) -> p n", p=P))
                    for k in range(4)] + [
                    (vec[:, 32 * m:32 * m + 32].rearrange("p (t n) -> p t n", n=GDN_V), across(t[name][0], TT))
                    for m, name in enumerate(("gdn_a_log", "gdn_dt_bias"))] + [
                    (cols[:, 64:65], column(t["gdn_o_gain"][0])),
                    (masks[:], t["block_masks"].rearrange("m p n -> p m n"))]

        def wait_all(eng, *needs):
            for _, v in needs:
                if not isinstance(v, int):
                    eng.compute_val(v)
            eng.wait_ge(consts, N_CONSTS)
            for s, v in needs:
                eng.wait_ge(s, v)

        def wait_bank(eng, st, j, b):
            if b < 3:
                eng.wait_ge(bank_full, st["full"] + 3 * j + b + 1)
            else:
                eng.wait_ge(w_used[1], st["pair"] + (3 * j + 3 if st["kind"] == "ffn_down" else j + 1))

        block = ctx.enter_context(nc.Block())

        @block.sync
        def _(sp):
            for tt in range(TT):
                sp.dma_start(x[:, tt], t["x"][0, tt * P:tt * P + P]).then_inc(x_loaded[tt], 16)

            def load_slot(pair, odd, parts):
                if not (isinstance(pair, int) and pair == 0):
                    sp.wait_ge(w_split, 2 * pair - 1 + odd)
                for dst, src in parts:
                    sp.dma_start(raw[:, odd][dst], src).then_inc(w_loaded[odd], 16)

            for st in stages:
                if st["kind"] == "project":
                    w = t[st["weights"]][st["layer"]].rearrange("(kt p) n -> p kt n", p=P)

                    def panel(pair, col):
                        for odd in range(2):
                            load_slot(pair, odd, [
                                ((slice(None), slice(2 * m, 2 * m + 2)),
                                 w[:, HALF * odd + 2 * m:HALF * odd + 2 * m + 2, col])
                                for m in range(2)])

                    panel(st["pair"], slice(st["col"], st["col"] + COLS))
                    if st["panels"] > 2:
                        with sp.Fori(1, st["panels"]) as j:
                            panel(st["pair"] + j, bass.ds(st["col"] + COLS * j, COLS))
                    else:
                        panel(st["pair"] + 1, slice(st["col"] + COLS, st["col"] + 2 * COLS))
                if st["kind"] == "ffn_up":
                    half = COLS // 2
                    ws = [t[n][st["layer"]].rearrange("(kt p) n -> p kt n", p=P) for n in ("ffn_w_gate_2", "ffn_w_up_2")]

                    def up_panel(pair, col):
                        for odd in range(2):
                            load_slot(pair, odd, [
                                ((slice(None), slice(None), slice(half * m, half * m + half)),
                                 ws[m][:, HALF * odd:HALF * odd + HALF, col]) for m in range(2)])

                    up_panel(st["pair"], slice(0, half))
                    with sp.Fori(1, 11) as j:
                        up_panel(st["pair"] + j, bass.ds(half * j, half))
                if st["kind"] == "ffn_down":
                    w = t["ffn_w_down_2"][st["layer"]].rearrange("(kt p) n -> p kt n", p=P)
                    for chunk in range(2):
                        for slot in range(6):
                            k0 = HALF * slot
                            k = min(HALF, FT - k0) // 2
                            load_slot(st["pair"] + 3 * chunk + slot // 2, slot % 2, [
                                ((slice(None), slice(k * m, k * m + k)),
                                 w[:, k0 + k * m:k0 + k * m + k, COLS * chunk:COLS * chunk + COLS])
                                for m in range(2)])
                if st["kind"] in ("store", "last_norm"):
                    for tt in range(TT):
                        if st["kind"] == "store":
                            sp.wait_ge(dve_freed, st["dve"] - TT + tt + 1)
                        else:
                            sp.wait_ge(out_rows, tt + 1)
                        sp.dma_start(out[0].rearrange("(t p) d -> p t d", p=P)[:, tt], x[:, tt]).then_inc(stored, 16)
                    sp.wait_ge(stored, 16 * TT)

        @block.gpsimd
        def _(pool):
            pool.memset(ident[:], 0.0).then_inc(pool_step, 1)
            pool.memset(mask_b[:], 0.0).then_inc(pool_step, 1)
            pool.memset(mask2_b[:], 0.0).then_inc(pool_step, 1)
            pool.memset(tri[:], 1.0).then_inc(pool_step, 1)
            pool.memset(pick[:], 0.0).then_inc(pool_step, 1)
            pool.memset(ones[:], 1.0).then_inc(consts, 1)
            pool.wait_ge(pool_step, 5)
            pool.affine_select(out=ident[:], in_=ident[:], compare_op=ALU.not_equal, fill=1.0, base=0,
                               pattern=[[-1, P]], channel_multiplier=1).then_inc(consts, 1)
            pool.affine_select(out=mask_b[:], in_=mask_b[:], compare_op=ALU.is_ge, fill=NEG, base=0,
                               pattern=[[-1, P]], channel_multiplier=1).then_inc(consts, 1)
            pool.affine_select(out=mask2_b[0:CHUNK], in_=mask2_b[0:CHUNK], compare_op=ALU.is_ge, fill=NEG,
                               base=CHUNK - 1, pattern=[[-1, P]], channel_multiplier=0).then_inc(consts, 1)
            pool.affine_select(out=tri[:], in_=tri[:], compare_op=ALU.is_ge, fill=0.0, base=0,
                               pattern=[[1, P]], channel_multiplier=-1).then_inc(consts, 1)
            pool.wait_ge(consts, 5)
            pool.tensor_copy(ident_b[:], ident[:]).then_inc(consts, 1)
            pool.memset(pick[:, 15:16], 1.0).then_inc(consts, 1)
            pool.tensor_copy(chunk_tri[:], tri[:]).then_inc(pool_step, 1)
            pool.wait_ge(pool_step, 6)
            pool.memset(chunk_tri[0:CHUNK, CHUNK:], 0.0).then_inc(consts, 1)

            def split(pair, odd):
                pool.wait_ge(w_high, 2 * pair + odd + 1)
                pool.tensor_tensor(w_lo[:, odd], raw[:, odd], w_hi[:, odd].bitcast(F32), ALU.subtract)\
                    .then_inc(w_split, 1)

            for odd in range(2):
                split(0, odd)
            with pool.Fori(1, n_pairs) as n:
                for odd in range(2):
                    split(n, odd)

        @block.tensor
        def _(pe):
            pe.wait_ge(consts, N_CONSTS)

            def all_free(st):
                for s, n in ((act_freed, st["act"]), (dve_freed, st["dve"])):
                    if n:
                        pe.wait_ge(s, n)

            def three(out_ap, left, right, first, last):
                lh, ll = left
                rh, rl = right
                pe.matmul(out_ap, lh, rh, start=first, stop=False)
                pe.matmul(out_ap, lh, rl, start=False, stop=False)
                return pe.matmul(out_ap, ll, rh, start=False, stop=last)

            def panel(pair, four, hi, lo, rows, wait_set):
                for odd in range(2):
                    pe.wait_ge(w_split, 2 * pair + odd + 1)
                    if odd == 0:
                        wait_set()
                    for b in range(4):
                        for k in range(HALF):
                            kt = HALF * odd + k
                            act_side = [v[:, kt, b * P:b * P + P] if rows else v[:, kt] for v in (hi, lo)]
                            w_side = [v[:, odd, k] if rows else v[:, odd, k, b * P:b * P + P] for v in (w_hi, w_lo)]
                            ins = three(bank[4 * four + b][:], *((act_side, w_side) if rows else (w_side, act_side)),
                                        odd == 0 and k == 0, odd == 1 and k == HALF - 1)
                        if odd == 1 and b < 3:
                            ins.then_inc(bank_full, 1)
                    ins.then_inc(w_used[odd], 1)

            def panels(st, hi, lo, rows):
                n = st["panels"]
                per_act, per_dve = st["n_act"] // n, st["n_dve"] // n

                def set_is_free(j):
                    if isinstance(j, int) and j < 2:
                        for s, v in ((act_freed, (st["free0"][0], st["act"])[j]), (dve_freed, (st["free0"][1], st["dve"])[j])):
                            if v:
                                pe.wait_ge(s, v)
                        return
                    if per_act:
                        pe.wait_ge(act_freed, st["act"] + per_act * (j - 1))
                    if per_dve:
                        pe.wait_ge(dve_freed, st["dve"] + per_dve * (j - 1))

                def one(j, four):
                    panel(st["pair"] + j, four, hi, lo, rows, lambda: set_is_free(j))

                one(0, 0)
                one(1, 1)
                if n == 4:
                    one(2, 0)
                    one(3, 1)
                elif n > 4:
                    with pe.Fori(1, n // 2) as i:
                        for j in range(2):
                            one(2 * i + j, j)
                    if n % 2:
                        one(n - 1, 0)

            def small_logits(st, n, dst):
                pe.wait_ge(small_split, st["small"])
                for tt in range(TT):
                    for kt in range(KT):
                        ins = three(dst[:, tt * n:tt * n + n],
                                    [v[:, kt, tt * P:tt * P + P] for v in (xt_hi, xt_lo)],
                                    [v[:, kt, 0:n] for v in (s_hi, s_lo)], kt == 0, kt == KT - 1)
                ins.then_inc(small_full, 1)

            def norm_sums(st, rows, n_rows, dst, base=0, norm=0):
                for k, row in enumerate(rows):
                    pe.wait_ge(squares_done, st["squares"] + base + k + 1)
                    ins = pe.matmul(dst[0:n_rows], pick[:, 15 - row:15 - row + n_rows], squares[:, k % 2],
                                    start=k == 0, stop=k == len(rows) - 1)
                    ins.then_inc(squares_used, 1)

            def spread(st, n, counter, freed, n_rows, dst):
                if n >= 2:
                    pe.wait_ge(gated_raw, st["gated"] + freed(n))
                pe.matmul(dst[:], selector[0:n_rows, n], norm_r[0:n_rows], start=True, stop=True).then_inc(counter, 1)

            for st in stages:
                kind, nth = st["kind"], st["nth"]
                if kind == "fill":
                    all_free(st)
                    src = xn if st["norm"] == "rms" else x
                    for tt in range(TT):
                        pe.wait_ge(rows_ready, TT * nth + tt + 1)
                        for g in range(2):
                            for k in range(4):
                                kt = 4 * g + k
                                ins = pe.transpose(bank[2 * tt + g][:, k * P:k * P + P],
                                                   src[:, tt, kt * P:kt * P + P], ident[:])
                            ins.then_inc(fill_full, 1)
                    pe.wait_ge(dve_freed, st["dve"] + 8)
                if kind == "project":
                    if st["to"] == "residual":
                        pe.wait_ge(gated_low, st["gated"])
                        panels(st, g_hi, g_lo, True)
                    else:
                        panels(st, xt_hi, xt_lo, st["rows"])
                if kind == "ffn_up":
                    panels(st, xt_hi, xt_lo, False)
                if kind == "ffn_down":
                    for chunk in range(2):
                        four = (1 + chunk) % 2
                        for slot in range(6):
                            odd, pair = slot % 2, st["pair"] + 3 * chunk + slot // 2
                            k0 = HALF * slot
                            n = min(HALF, FT - k0)
                            pe.wait_ge(w_split, 2 * pair + odd + 1)
                            if slot == 0:
                                if chunk == 0:
                                    pe.wait_ge(act_freed, st["free0"][0])
                                    pe.wait_ge(dve_freed, st["free0"][1])
                                else:
                                    all_free(st)
                            if chunk == 0:
                                pe.wait_ge(h_low, FT * nth + k0 + n)
                            for b in range(4):
                                for k in range(n):
                                    ins = three(bank[4 * four + b][:],
                                                [v[:, k0 + k, b * P:b * P + P] for v in (h_hi, h_lo)],
                                                [v[:, odd, k] for v in (w_hi, w_lo)],
                                                slot == 0 and k == 0, slot == 5 and k == n - 1)
                                if slot == 5 and b < 3:
                                    ins.then_inc(bank_full, 1)
                            ins.then_inc(w_used[odd], 1)
                if kind == "fox":
                    all_free(st)
                    small_logits(st, FOX_HEADS, bank[0])
                    pe.wait_ge(fox["cum_in"], nth + 1)
                    pe.wait_ge(fox["consts"], nth + 1)
                    for jt in range(TT):
                        for tt in range(jt + 1):
                            ins = pe.matmul(bank[1][0:8, jt * P:jt * P + P], logf[:, 8 * tt:8 * tt + 8],
                                            (tri if tt == jt else ones)[:], start=tt == 0, stop=tt == jt)
                    ins.then_inc(fox["cum_full"], 1)

                    def spread_norms(h):
                        if h:
                            pe.wait_ge(fox["qk_ready"], 16 * nth + 2 * h)
                        for m in range(2):
                            pe.matmul(bank[m][:], selector[0:16, 8 * m + h], norm_r[0:16], start=True, stop=True)\
                                .then_inc(fox["norm_full"], 1)

                    def scores(n):
                        h, i = divmod(n, TT)
                        pe.wait_ge(fox["qk_ready"], 16 * nth + 2 * h + 2)
                        if n >= 3:
                            pe.wait_ge(fox["exps"], 32 * nth + n - 2)
                        dst, keys = bank[2 + n % 3], (i + 1) * P
                        pe.matmul(dst[:, 0:keys], q_n[:, h % 2, i * P:i * P + P], k_n[:, h % 2, 0:keys],
                                  start=True, stop=False)
                        pe.matmul(dst[:, 0:keys], selector[0:8, h], cum_rows[0:8, 0:keys], start=False, stop=False)
                        pe.matmul(dst[:, i * P:keys], ident_b[:], mask_b[:], start=False, stop=True)\
                            .then_inc(fox["scores"], 1)

                    def turn(n):
                        h, i = divmod(n, TT)
                        pe.wait_ge(fox["normed"], 32 * nth + n + 1)
                        if n >= 2:
                            pe.wait_ge(fox["turned_used"], 32 * nth + n - 1)
                        for k in range(i + 1):
                            ins = pe.transpose(bank[5 + n % 2][:, k * P:k * P + P], probs[:, n % 2, k * P:k * P + P],
                                               ident[:])
                        ins.then_inc(fox["turned"], 1)

                    def weigh(h):
                        pe.wait_ge(fox["turned_used"], 32 * nth + TT * (h + 1))
                        if h:
                            pe.wait_ge(gated_raw, st["gated"] + h)
                        for k in range(TT):
                            ins = pe.matmul(bank[7][:, k * P:], c_rows[:, k, h * P:h * P + P],
                                            probs_t[:, h % 2, k, k * P:], start=k == 0, stop=k == TT - 1)
                        ins.then_inc(fox["out_full"], 1)

                    pe.wait_ge(fox["cum_rows"], nth + 1)
                    norm_sums(st, [8 * m + h for h in range(FOX_HEADS) for m in range(2)], 16, bank[2])
                    pe.wait_ge(rows_r, st["norms"] + 1)
                    spread_norms(0)
                    n_all = FOX_HEADS * TT
                    scores(0)
                    scores(1)
                    for n in range(n_all):
                        if n % TT == 0 and n // TT + 1 < FOX_HEADS:
                            spread_norms(n // TT + 1)
                        if n + 2 < n_all:
                            scores(n + 2)
                        turn(n)
                        if n % TT == 1 and n > TT:
                            weigh(n // TT - 1)
                    weigh(FOX_HEADS - 1)

                if kind == "attn":
                    all_free(st)

                    def pair_scores(n):
                        h, i = divmod(n, TT)
                        if n >= 3:
                            pe.wait_ge(diff["exps"], 2 * n - 4)
                        keys = (i + 1) * P
                        for c in range(2):
                            dst, rows = bank[2 * (n % 3) + c], slice(CHUNK * c, CHUNK * c + CHUNK)
                            pe.matmul(dst[:, 0:keys], buf_a[rows, h, i * P:i * P + P], buf_b[rows, h, 0:keys],
                                      start=True, stop=False)
                            pe.matmul(dst[:, i * P:keys], ident_b[:], mask2_b[:], start=False, stop=True)\
                                .then_inc(diff["scores"], 1)

                    def turn_pair(n):
                        i = n % TT
                        pe.wait_ge(diff["mixed"], n + 1)
                        if n:
                            pe.wait_ge(diff["turned_used"], n)
                        for k in range(i + 1):
                            ins = pe.transpose(bank[6][:, k * P:k * P + P],
                                               pair_probs[:, n % 2, 0, k * P:k * P + P], ident[:])
                        ins.then_inc(diff["turned"], 1)

                    def weigh_values(h):
                        pe.wait_ge(diff["turned_used"], TT * (h + 1))
                        if h:
                            pe.wait_ge(diff["out_taken"], h)
                        for k in range(TT):
                            ins = pe.matmul(bank[7][:, k * P:], c_rows[:, k, h * P:h * P + P],
                                            probs_t[:, h % 2, k, k * P:], start=k == 0, stop=k == TT - 1)
                        ins.then_inc(diff["out_full"], 1)

                    n_all = ATTN_HEADS * TT
                    pair_scores(0)
                    pair_scores(1)
                    for n in range(n_all):
                        if n + 2 < n_all:
                            pair_scores(n + 2)
                        turn_pair(n)
                        if n % TT == 1 and n > TT:
                            weigh_values(n // TT - 1)
                    weigh_values(ATTN_HEADS - 1)
                    norm_sums(st, list(range(8)), 8, bank[2])
                    pe.wait_ge(diff["selector"], 1)
                    pe.wait_ge(rows_r, st["norms"] + 1)
                    for h in range(ATTN_HEADS):
                        spread(st, h, diff["spread"], lambda n: n - 1, 8, bank[h % 2])
                if kind == "gla":
                    all_free(st)
                    small_logits(st, GLA_RANK, bank[0])
                    pe.wait_ge(gla["low"], 1)
                    for tt in range(TT):
                        ins = pe.transpose(bank[1][0:GLA_RANK, tt * P:tt * P + P],
                                           vec[:, tt * GLA_RANK:(tt + 1) * GLA_RANK], ident[:])
                    ins.then_inc(gla["low_turned"], 1)
                    pe.wait_ge(gla["low_rows"], 1)
                    for h in range(GLA_HEADS):
                        pe.matmul(bank[2 + h][:], up_rows[0:GLA_RANK, h * P:h * P + P], low_rank[0:GLA_RANK],
                                  start=True, stop=True).then_inc(gla["gates"], 1)
                    pe.wait_ge(gla["keys"], GLA_HEADS)
                    for tt in range(TT):
                        if tt >= 2:
                            pe.wait_ge(gla["keys_rows"], tt - 1)
                        for h in range(GLA_HEADS):
                            ins = pe.transpose(bank[tt % 2][:, h * P:h * P + P], buf_a[:, 4 + h, tt * P:tt * P + P],
                                               ident[:])
                        ins.then_inc(gla["keys_turned"], 1)

                    def inside(tt):
                        if tt >= 2:
                            pe.wait_ge(gla["inner"], tt - 1)
                        for h in range(GLA_HEADS):
                            ins = pe.matmul(bank[2 + tt % 2][:, h * P:h * P + P], buf_b[:, 4 + h, tt * P:tt * P + P],
                                            buf_b[:, h, tt * P:tt * P + P], start=True, stop=True)
                        ins.then_inc(gla["inner_full"], 1)

                    inside(0)
                    pe.wait_ge(gla["keys_rows"], TT)
                    for tt in range(TT):
                        if tt + 1 < TT:
                            inside(tt + 1)
                        pe.wait_ge(gla["inner"], tt + 1)
                        if tt:
                            pe.wait_ge(gla["out_taken"], 2 * tt)
                        for h in range(GLA_HEADS):
                            for m in range(2):
                                at = (h % 2) * 256 + m * P
                                pe.matmul(bank[4 + h // 2][:, at:at + P],
                                          c_rows[:, tt, h * 256 + m * P:h * 256 + m * P + P], inner[:, tt % 2, h],
                                          start=h % 2 == 0 and m == 0, stop=False, skip_group_check=True)
                        for half in range(2):
                            c = 2 * tt + half
                            rows = slice(CHUNK * half, CHUNK * half + CHUNK)
                            if c:
                                pe.wait_ge(gla["state"], c)
                            for h in range(GLA_HEADS if c else 0):
                                for m in range(2):
                                    at = (h % 2) * 256 + m * P + CHUNK * half
                                    ins = pe.matmul(bank[4 + h // 2][:, at:at + CHUNK],
                                                    gla_state[:, c % 2, h * 256 + m * P:h * 256 + m * P + P],
                                                    buf_b[:, h, CHUNK * c:CHUNK * c + CHUNK],
                                                    start=False, stop=half == 1 and h % 2 == 1 and m == 1,
                                                    skip_group_check=True)
                                if half == 1 and h % 2 == 1:
                                    ins.then_inc(gla["out_full"], 1)
                            if c < 7:
                                for h in range(GLA_HEADS):
                                    ins = pe.matmul(bank[6 + h // 2][:, (h % 2) * 256:(h % 2) * 256 + 256],
                                                    k_rows[rows, tt, h * P:h * P + P],
                                                    c_rows[rows, tt, h * 256:h * 256 + 256], start=True, stop=True)
                                    if h % 2:
                                        ins.then_inc(gla["update"], 1)
                    norm_sums(st, [n // 2 for n in range(8)], GLA_HEADS, bank[0])
                    pe.wait_ge(gla["state"], 8)
                    pe.wait_ge(rows_r, st["norms"] + 1)
                    for h in range(GLA_HEADS):
                        spread(st, h, gla["spread"], lambda n: 2 * n - 2, GLA_HEADS, bank[2 + h % 2])
                if kind == "gdn":
                    all_free(st)
                    small_logits(st, 2 * GDN_V, bank[0])
                    pe.wait_ge(gdn["silu"], 16)
                    norm_sums(st, list(range(8)), 8, bank[1])
                    pe.wait_ge(gdn["g"], 1)
                    pe.matmul(bank[2][:, 0:32], chunk_tri[:], small[:, 0], start=True, stop=True)
                    pe.matmul(bank[2][:, 32:64], same_chunk, small[:, 0], start=True, stop=True)
                    for tt in range(TT):
                        ins = pe.matmul(bank[3][0:GDN_V, tt * P:tt * P + P], small[:, 0, tt * GDN_V:(tt + 1) * GDN_V],
                                        chunk_tri[:], start=True, stop=True)
                    ins.then_inc(gdn["sums"], 1)
                    pe.wait_ge(rows_r, st["norms"] + 1)
                    for n in range(8):
                        if n >= 2:
                            pe.wait_ge(gdn["qk_ready"], n - 1)
                        pe.matmul(bank[4 + n % 2][:], selector[0:8, n], norm_r[0:8], start=True, stop=True)\
                            .then_inc(gdn["spread"], 1)
                    pe.wait_ge(gdn["qk_ready"], 8)
                    for tt in range(TT):
                        if tt >= 2:
                            pe.wait_ge(gdn["keys_rows"], tt - 1)
                        for h in range(GDN_QK):
                            ins = pe.transpose(bank[6 + tt % 2][:, h * P:h * P + P],
                                               buf_a[:, GDN_QK + h, tt * P:tt * P + P], ident[:])
                        ins.then_inc(gdn["keys_full"], 1)
                    for n in range(2 * TT):
                        tt, g = divmod(n, 2)
                        if n >= 2:
                            pe.wait_ge(gdn["values_rows"], n - 1)
                        for i in range(4):
                            ins = pe.transpose(bank[4 + g][:, i * P:i * P + P],
                                               buf_b[:, 4 * g + i, tt * P:tt * P + P], ident[:])
                        ins.then_inc(gdn["values_full"], 1)
                    pe.wait_ge(gdn["factors"], 1)

                    def build(tt, g):
                        if tt:
                            solved(pe, g, tt - 1, LAST_STEP - 1)
                            solved(pe, g, tt - 1, LAST_STEP)
                        at = slice(tt * P, tt * P + P)
                        for i in range(4):
                            pe.matmul(bank[2 * g][:, i * P:i * P + P], selector[0:GDN_V, 4 * g + i], cum_rows[0:GDN_V, at],
                                      start=True, stop=True)
                        for i in range(2):
                            k = buf_a[:, GDN_QK + 2 * g + i, at]
                            pe.matmul(bank[2 * g + 1][:, i * P:i * P + P], k, k, start=True, stop=True)
                        for i in range(2):
                            ins = pe.matmul(bank[2 * g + 1][:, (2 + i) * P:(3 + i) * P], buf_a[:, GDN_QK + 2 * g + i, at],
                                            buf_a[:, 2 * g + i, at], start=True, stop=True)
                        ins.then_inc(solve["build_full"][g], 1)

                    def step(g, n, left, right, flip=False):
                        for i in range(4):
                            h, o = 4 * g + i, bank[2 * g + n % 2][:, i * P:i * P + P]
                            ins = pe.transpose(o, left[:, h], ident[:]) if flip else \
                                pe.matmul(o, left[:, h], right[:, h], start=True, stop=True)
                        ins.then_inc(solve["full"][g], 1)

                    def solve_step(tt, g, n):
                        def after(*earlier):
                            for e in earlier:
                                solved(pe, g, tt, e)
                        if n == 1:
                            pe.wait_ge(solve["lower"][g], tt + 1)
                            step(g, n, x1, None, True)
                        if n == 2:
                            after(1)
                            step(g, n, x2, x1)
                        if n == 3:
                            step(g, n, x1, x2)
                        if n == 4:
                            after(2)
                            step(g, n, x3, inverse)
                        if n == 5:
                            after(3)
                            step(g, n, x4, x3)
                        if n == 6:
                            after(4)
                            step(g, n, x3, x4)
                        if n == 7:
                            after(5)
                            step(g, n, x1, inverse)
                        if n == 8:
                            after(6)
                            step(g, n, x2, x1)
                        if n == 9:
                            after(8, 7)
                            step(g, n, x3, inverse)
                        if n == 10:
                            after(9)
                            step(g, n, inverse, cross)
                        if n == 11:
                            step(g, n, cross, inverse)
                        if n == 12:
                            after(10, 11)
                            step(g, n, x1, x4)
                        if n == 13:
                            step(g, n, inverse, None, True)
                        if n == 14:
                            after(12)
                            step(g, n, x3, x2)
                        if n == 15:
                            after(13, 14)
                            step(g, n, x4, x2)
                        if n == 16:
                            after(15)
                            pe.wait_ge(solve["kbg"][g], tt + 1)
                            step(g, n, x3, x1)
                        if n == 17:
                            step(g, n, x1, u_rows[:, tt])

                    def read_state(c):
                        tt, rows = c // 2, slice(CHUNK * (c % 2), CHUNK * (c % 2) + CHUNK)
                        solved(pe, 0, tt, 16)
                        solved(pe, 1, tt, 16)
                        for g in range(2):
                            pe.wait_ge(gdn["state"], max(1, 2 * c + g))
                            for i in range(4):
                                ins = pe.matmul(bank[4 + g][:, i * P:i * P + P], w_t[tt % 2][:, 4 * g + i],
                                                delta_state[:, 4 * g + i], start=True, stop=True)
                            ins.then_inc(gdn["ws"], 1)
                        if c % 2 == 0 and tt:
                            pe.wait_ge(gdn["out_taken"], 2 * tt)
                        for h in range(GDN_V):
                            at = (h % 4) * P
                            pe.matmul(bank[6 + h // 4][:, at + rows.start:at + rows.stop], delta_state[:, h],
                                      q_dec[tt % 2][:, h, rows], start=c % 2 == 0 and h % 4 == 0, stop=False,
                                      skip_group_check=True)

                    def write_state(c):
                        tt, rows = c // 2, slice(CHUNK * (c % 2), CHUNK * (c % 2) + CHUNK)
                        for g in range(2):
                            pe.wait_ge(gdn["v_new"], 2 * c + g + 1)
                            for i in range(4 if c < 2 * TT - 1 else 0):
                                h = 4 * g + i
                                ins = pe.matmul(bank[4 + g][:, i * P:i * P + P], k_dec[tt % 2][rows, h],
                                                v_new[rows, h], start=True, stop=True)
                            if c < 2 * TT - 1:
                                ins.then_inc(gdn["update"], 1)
                            for i in range(4):
                                h = 4 * g + i
                                ins = pe.matmul(bank[6 + g][:, i * P + rows.start:i * P + rows.stop], v_new[rows, h],
                                                qk_dec[tt % 2][rows, h, rows], start=False,
                                                stop=c % 2 == 1 and i == 3, skip_group_check=True)
                            if c % 2:
                                ins.then_inc(gdn["out_full"], 1)

                    for tt in range(TT + 1):
                        for g in range(2 if tt < TT else 0):
                            build(tt, g)
                        for n in range(1, LAST_STEP + 1):
                            for g in range(2 if tt < TT else 0):
                                solve_step(tt, g, n)
                            if tt and n in RECURRENCE_AFTER:
                                part = RECURRENCE_AFTER.index(n)
                                (write_state if part % 2 else read_state)(2 * (tt - 1) + part // 2)
                    norm_sums(st, list(range(8)), 8, bank[0], base=8)
                    pe.wait_ge(rows_r, st["norms"] + 2)
                    for h in range(GDN_V):
                        spread(st, h, gdn["norm_spread"], lambda n: n - 1, 8, bank[2 + h % 2])
        @block.scalar
        def _(act):
            steps = [0]

            def link(ins):
                steps[0] += 1
                ins.then_inc(act_step, 1)
                act.wait_ge(act_step, steps[0])

            def load_norm(norm, which):
                w, b = (("norm_w", "norm_w") if norm == "rms" else (norm + "_g_2", norm + "_b_2"))
                act.dma_start(norm_w[:], across(t[w][which])).then_inc(rows_loaded, 16)
                act.dma_start(norm_b[:], across(t[b][which])).then_inc(rows_loaded, 16)

            def weights_high(pair, odd):
                if isinstance(pair, int) and pair >= n_pairs:
                    return
                used = [] if isinstance(pair, int) and pair == 0 else [(w_used[odd], pair)]
                wait_all(act, (w_loaded[odd], 32 * (pair + 1)), *used)
                act.activation(w_hi[:, odd], raw[:, odd], ACT.Copy).then_inc(w_high, 1)

            def high(st, h):
                if st["kind"] == "project":
                    act.wait_ge(dve_freed, st["dve"] + h + 1)
                else:
                    act.wait_ge(gated_raw, st["gated"] + h + 1)
                src = gated_conv if st["kind"] == "project" else gated
                act.activation(g_hi[:, h], src[:], ACT.Copy).then_inc(gated_high, 1)

            def root(st, n, ap):
                act.wait_ge(root_in, st["roots"] + n + 1)
                act.activation(ap, ap, ACT.Sqrt).then_inc(root_out, 1)

            def square_tiles(st, tiles, base=0):
                for k, src in enumerate(tiles):
                    n = st["squares"] + base + k
                    if k >= 2:
                        act.wait_ge(squares_used, n - 1)
                    o = squares[:, k % 2] if len(src.shape) == 2 else \
                        squares[:, k % 2].rearrange("p (t n) -> p t n", t=TT)
                    act.activation(o, src, ACT.Square).then_inc(squares_done, 1)

            def behind(st, n):
                if st["to"] == "gate G":
                    high(st, n)
                else:
                    act.wait_ge(dve_freed, st["dve"] + n + 1)
                    dst = buf_a[:, n] if n < 8 else buf_b[:, n - 8]
                    act.activation(dst, dst, ACT.Silu).then_inc(gdn["silu"], 1)

            for odd in range(2):
                weights_high(0, odd)
            for st in stages:
                kind, nth = st["kind"], st["nth"]
                if kind == "last_norm":
                    load_norm("ln2", st["layer"])
                    for tt in range(TT):
                        root(st, tt, stat[:, 12 + tt:13 + tt])
                if kind == "fill":
                    if nth:
                        act.wait_ge(rows_ready, TT * nth)
                    if st["norm"] != "plain":
                        if st["gated"]:
                            act.wait_ge(gated_low, st["gated"])
                        load_norm(st["norm"], st["which"])
                    def squares_of(tt):
                        if st["norm"] != "rms":
                            return
                        if nth:
                            act.wait_ge(dve_freed, st["dve"] - TT + tt + 1)
                        else:
                            act.wait_ge(x_loaded[tt], 16)
                        act.activation(xn[:, tt], x[:, tt], ACT.Square, accum_out=stat[:, tt:tt + 1]).then_inc(sumsq, 1)

                    def transposed_high(tt):
                        for g in range(2):
                            act.wait_ge(fill_full, 8 * nth + 2 * tt + g + 1)
                            act.activation(xt_hi[:, 4 * g:4 * g + 4, tt * P:tt * P + P],
                                           bank[2 * tt + g][:].rearrange("p (k n) -> p k n", k=4), ACT.Copy)\
                                .then_inc(xt_high, 1)

                    squares_of(0)
                    squares_of(1)
                    for tt in range(TT):
                        if st["norm"] != "plain":
                            root(st, tt, stat[:, 12 + tt:13 + tt])
                        if tt + 2 < TT:
                            squares_of(tt + 2)
                        if tt:
                            transposed_high(tt - 1)
                    transposed_high(TT - 1)
                if kind == "prep":
                    for dst, src in prep_loads(st):
                        with nc.allow_non_contiguous_dma(reason="a few kilobytes of small vectors"):
                            act.dma_start(dst, src).then_inc(mixer_loaded, 16)
                if kind == "ffn_down":
                    for slot in range(2, 14):
                        weights_high(st["pair"] + slot // 2, slot % 2)
                if kind == "project":
                    func, name = (ACT.Silu if "silu" in st["to"] else ACT.Copy), st["to"].split()[-1]
                    dst = {"A": buf_a, "B": buf_b, "C": buf_c, "D": buf_d}.get(name)
                    for j in range(st["panels"]):
                        weights_high(st["pair"] + j + 1, 0)
                        for b in range(4):
                            if b == 3:
                                weights_high(st["pair"] + j + 1, 1)
                            if st["to"] in ("conv", "gate G") and b > 0:
                                behind(st, 4 * j + b - 1)
                            if st["by"] != "act":
                                continue
                            wait_bank(act, st, j, b)
                            o = c_rows[:, b, COLS * j:COLS * j + COLS] if st["rows"] else dst[:, 4 * j + b]
                            act.activation(o, bank[4 * (j % 2) + b][:], func).then_inc(act_freed, 1)
                        if st["to"] in ("conv", "gate G"):
                            behind(st, 4 * j + 3)
                if kind == "ffn_up":
                    def up(j, four, first=False):
                        weights_high(st["pair"] + j + 1, 0)
                        for m in range(2):
                            full = (bank_full, st["full"] + 3 * j + m + 1)
                            wait_all(act, full, *([] if first else [(dve_freed, st["dve"] + 2 * j + m - 1)]))
                            act.activation(gate_act[:, m], bank[4 * four + m][:], ACT.Silu).then_inc(act_freed, 1)
                        weights_high(st["pair"] + j + 1, 1)
                        for m in range(2):
                            wait_all(act, (dve_freed, st["dve"] + 2 * j + m + 1))
                            at = 2 * j + m
                            o = h_hi[:, at] if first else h_hi[:, bass.ds(at, 1)].rearrange("p a n -> p (a n)")
                            act.activation(o, hidden[:, m], ACT.Copy).then_inc(h_high, 1)

                    up(0, 0, True)
                    with act.Fori(0, 5) as i:
                        for j in range(2):
                            up(2 * i + j + 1, 1 - j)
                if kind == "fox":
                    act.wait_ge(fox["logits"], nth + 1)
                    link(act.activation(logf_e[:], logf_e[:], ACT.Exp, scale=-1.0))
                    act.activation(logf_e[:], logf_e[:], ACT.Ln, bias=1.0).then_inc(fox["log"], 1)
                    act.wait_ge(small_full, st["small"])
                    act.wait_ge(dve_freed, st["dve"])
                    square_tiles(st, [b[:, h] for h in range(FOX_HEADS) for b in (buf_a, buf_b)])
                    root(st, 0, norm_t[0:16])

                    def exponentials(n):
                        i = n % TT
                        act.wait_ge(fox["max"], 32 * nth + n + 1)
                        if n >= 2:
                            act.wait_ge(fox["turned"], 32 * nth + n - 1)
                        keys = (i + 1) * P
                        act.activation(probs[:, n % 2, 0:keys], bank[2 + n % 3][:, 0:keys], ACT.Exp,
                                       bias=soft[:, n % 4:n % 4 + 1], accum_out=soft[:, 4 + n % 4:5 + n % 4])\
                            .then_inc(fox["exps"], 1)

                    def take_turned(n):
                        h, i = divmod(n, TT)
                        act.wait_ge(fox["turned"], 32 * nth + n + 1)
                        if h >= 2 and i == 0:
                            act.wait_ge(fox["out_full"], 8 * nth + h - 1)
                        act.activation(probs_t[:, h % 2, 0:i + 1, i * P:i * P + P],
                                       bank[5 + n % 2][:, 0:(i + 1) * P].rearrange("p (k n) -> p k n", n=P), ACT.Copy)\
                            .then_inc(fox["turned_used"], 1)

                    n_all = FOX_HEADS * TT
                    for n in range(n_all):
                        exponentials(n)
                        if n:
                            take_turned(n - 1)
                        if n % TT == 2 and n > TT:
                            high(st, n // TT - 1)
                    take_turned(n_all - 1)
                    high(st, FOX_HEADS - 1)

                if kind == "attn":
                    act.wait_ge(diff["lam_in"], 1)
                    act.activation(lam_work[:, 0:2], lam_work[:, 0:2], ACT.Exp).then_inc(diff["lam_out"], 1)

                    def pair_exponentials(n):
                        i = n % TT
                        keys = (i + 1) * P
                        for c in range(2):
                            act.wait_ge(diff["max"], 2 * n + c + 1)
                            if n >= 2:
                                act.wait_ge(diff["turned"], n - 1)
                            k = 2 * (n % 2) + c
                            act.activation(pair_probs[:, n % 2, c, 0:keys], bank[2 * (n % 3) + c][:, 0:keys], ACT.Exp,
                                           bias=soft[:, k:k + 1], accum_out=soft[:, 4 + k:5 + k])\
                                .then_inc(diff["exps"], 1)

                    def take_pair(n):
                        h, i = divmod(n, TT)
                        act.wait_ge(diff["turned"], n + 1)
                        if h >= 2 and i == 0:
                            act.wait_ge(diff["out_full"], h - 1)
                        act.activation(probs_t[:, h % 2, 0:i + 1, i * P:i * P + P],
                                       bank[6][:, 0:(i + 1) * P].rearrange("p (k n) -> p k n", n=P), ACT.Copy)\
                            .then_inc(diff["turned_used"], 1)

                    def take_out(h):
                        act.wait_ge(diff["out_full"], h + 1)
                        act.activation(buf_d[:, h], bank[7][:], ACT.Copy).then_inc(diff["out_taken"], 1)

                    n_all = ATTN_HEADS * TT
                    for n in range(n_all):
                        pair_exponentials(n)
                        if n:
                            take_pair(n - 1)
                        if n % TT == 2 and n > TT:
                            take_out(n // TT - 1)
                    take_pair(n_all - 1)
                    take_out(ATTN_HEADS - 1)
                    act.wait_ge(diff["out_taken"], ATTN_HEADS)
                    square_tiles(st, [buf_d[:, h] for h in range(ATTN_HEADS)])
                    root(st, 0, norm_t[0:8])
                    for h in range(ATTN_HEADS):
                        high(st, h)
                if kind == "gla":
                    def gate_log_exp(h):
                        act.wait_ge(gla["abs"], h + 1)
                        link(act.activation(gate_abs[:, h % 2], gate_abs[:, h % 2], ACT.Exp, scale=-1.0))
                        act.activation(gate_abs[:, h % 2], gate_abs[:, h % 2], ACT.Ln, bias=1.0).then_inc(gla["log"], 1)

                    gate_log_exp(0)
                    for h in range(GLA_HEADS):
                        if h + 1 < GLA_HEADS:
                            gate_log_exp(h + 1)
                        act.wait_ge(gla["sums"], h + 1)
                        act.activation(decayed[:, h], gate_log[:, h % 2], ACT.Exp, scale=1 / 16.0)\
                            .then_inc(gla["decays"], 1)
                        act.activation(grown[:, h % 2], gate_log[:, h % 2], ACT.Exp, scale=-1 / 16.0)\
                            .then_inc(gla["decays"], 1)
                    for tt in range(TT):
                        act.wait_ge(gla["keys_turned"], tt + 1)
                        if tt == 0:
                            act.wait_ge(gla["keys"], GLA_HEADS)
                        act.activation(k_rows[:, tt], bank[tt % 2][:], ACT.Copy).then_inc(gla["keys_rows"], 1)
                    for tt in range(TT):
                        for g in range(2):
                            act.wait_ge(gla["out_full"], 2 * tt + g + 1)
                            act.activation(buf_a[:, 4 * g:4 * g + 4, tt * P:tt * P + P],
                                           bank[4 + g][:].rearrange("p (n l) -> p n l", l=P), ACT.Copy)\
                                .then_inc(gla["out_taken"], 1)
                    act.wait_ge(gla["out_taken"], 2 * TT)
                    square_tiles(st, [buf_a[:, n] for n in range(8)])
                    root(st, 0, norm_t[0:GLA_HEADS])
                    for n in range(8):
                        high(st, n)
                if kind == "gdn":
                    act.wait_ge(gdn["logits"], 1)
                    link(act.activation(small[:, 1], small[:, 1], ACT.Exp, scale=-1.0))
                    act.activation(small[:, 1], small[:, 1], ACT.Ln, bias=1.0).then_inc(gdn["logs"], 1)
                    act.activation(vec[:, 0:32], vec[:, 0:32], ACT.Exp).then_inc(gdn["logs"], 1)
                    act.activation(small[:, 5], small[:, 5], ACT.Sigmoid).then_inc(gdn["logs"], 1)
                    act.wait_ge(small_full, st["small"])
                    square_tiles(st, [buf_a[:, n] for n in range(8)])
                    act.wait_ge(gdn["columns"], 1)
                    act.activation(small[:, 4], small[:, 2], ACT.Exp).then_inc(gdn["exps"], 1)
                    act.activation(small[:, 3], small[:, 3], ACT.Exp).then_inc(gdn["exps"], 1)
                    root(st, 0, norm_t[0:8])
                    for tt in range(TT):
                        act.wait_ge(gdn["keys_full"], tt + 1)
                        act.activation(key_rows[:, tt], bank[6 + tt % 2][:], ACT.Copy).then_inc(gdn["keys_rows"], 1)

                    def decays(tt, g):
                        s, four = solve["decays"][g], slice(4 * g, 4 * g + 4)
                        act.wait_ge(solve["differences"][g], 2 * tt + 1)
                        act.activation(x3[:, four], bank[2 * g][:].rearrange("p (a n) -> p a n", n=P), ACT.Exp)\
                            .then_inc(s, 1)
                        act.activation(x2[:, four], x2[:, four], ACT.Exp, scale=-1.0).then_inc(s, 1)
                        act.wait_ge(solve["differences"][g], 2 * tt + 2)
                        o = qk_dec[tt % 2][:, four]
                        act.activation(o, o, ACT.Exp).then_inc(s, 1)

                    def take_step(tt, g, n):
                        four = slice(4 * g, 4 * g + 4)
                        act.wait_ge(solve["full"][g], LAST_STEP * tt + n)
                        dst = {1: x2, 2: x3, 3: x4, 5: x1, 6: x2, 8: x3, 10: x4, 11: x1, 12: x3, 13: x4, 15: x1,
                               16: w_t[tt % 2]}[n]
                        act.activation(dst[:, four], bank[2 * g + n % 2][:].rearrange("p (a n) -> p a n", n=P), ACT.Copy)\
                            .then_inc(solve["act"][g], 1)

                    for tt in range(TT + 1):
                        for g in range(2 if tt < TT else 0):
                            decays(tt, g)
                        for n in ACT_STEPS if tt < TT else ():
                            for g in range(2):
                                take_step(tt, g, n)
                        for g in range(2 if tt else 0):
                            act.wait_ge(gdn["out_full"], 2 * tt - 1 + g)
                            act.activation(u_rows[:, tt - 1, 4 * g:4 * g + 4],
                                           bank[6 + g][:].rearrange("p (a n) -> p a n", n=P), ACT.Copy)\
                                .then_inc(gdn["out_taken"], 1)
                    act.wait_ge(gdn["out_taken"], 2 * TT)
                    square_tiles(st, [u_rows[:, :, h] for h in range(GDN_V)], base=8)
                    root(st, 1, norm_t[0:8])
                    for h in range(GDN_V):
                        high(st, h)
        @block.vector
        def _(dve):
            steps = [0]

            def link(ins):
                steps[0] += 1
                ins.then_inc(dve_step, 1)
                dve.wait_ge(dve_step, steps[0])

            def low(st, h):
                dve.wait_ge(gated_high, st["gated"] + h + 1)
                src = gated_conv if st["kind"] == "project" else gated
                dve.tensor_tensor(g_lo[:, h], src[:], g_hi[:, h].bitcast(F32), ALU.subtract).then_inc(gated_low, 1)

            def newton(u, y, t):
                link(dve.tensor_tensor(t, y, y, ALU.mult))
                link(dve.scalar_tensor_tensor(t, t, -0.5, u, ALU.mult, ALU.mult))
                return dve.scalar_tensor_tensor(y, t, 1.5, y, ALU.add, ALU.mult)

            def rsqrt(st, n, u, root_of, y, t):
                dve.tensor_copy(root_of, u).then_inc(root_in, 1)
                dve.wait_ge(root_out, st["roots"] + n + 1)
                link(dve.reciprocal(y, root_of))
                return newton(u, y, t)

            def norm_rows(st, src, n_rows, count, eps, norm=0, base=0, n_squares=16):
                dve.wait_ge(squares_used, st["squares"] + base + n_squares)
                u, y, t = norm_u[0:n_rows], norm_r[0:n_rows], norm_t[0:n_rows]
                link(dve.tensor_scalar(u, src[0:n_rows], 1.0 / count, eps, ALU.mult, ALU.add))
                rsqrt(st, norm, u, t, y, t).then_inc(rows_r, 1)

            def make_selector(counter, n=16):
                dve.tensor_copy(selector[:, 0:n], ident[:, 0:n].unsqueeze(2).to_broadcast([P, n, P]))\
                    .then_inc(counter, 1)

            def taps(y, u, weights):
                last = len(weights) - 1
                link(dve.tensor_scalar(y, u, weights[last], None, ALU.mult))
                for k in range(last):
                    s = last - k
                    link(dve.scalar_tensor_tensor(y[:, s:], u[:, :SEQ - s], weights[k], y[:, s:], ALU.mult, ALU.add))

            def prep(st):
                dve.wait_ge(mixer_loaded, 16 * (st["loads"] + PREP_LOADS[st["layer_kind"]]))
                n = {"fox": FOX_HEADS, "gla": GLA_RANK, "gdn": 2 * GDN_V}.get(st["layer_kind"])
                if n:
                    link(dve.tensor_copy(s_hi[:, :, 0:n], s_raw[:, :, 0:n]))
                    dve.tensor_tensor(s_lo[:, :, 0:n], s_raw[:, :, 0:n], s_hi[:, :, 0:n].bitcast(F32), ALU.subtract)\
                        .then_inc(small_split, 1)
                if st["layer_kind"] == "attn":
                    for m in range(2):
                        link(dve.tensor_tensor(lam_rows[:, 2 * m], lam_rows[:, 2 * m], lam_rows[:, 2 * m + 1], ALU.mult))
                        ins = dve.reduce_sum(lam_work[:, m:m + 1], lam_rows[:, 2 * m], AX)
                        if m == 0:
                            link(ins)
                    ins.then_inc(diff["lam_in"], 1)
                    link(dve.tensor_scalar(cols[:, 1:2], cols[:, 0:1], 1.0 - LAM_INIT, None, ALU.mult))
                if st["layer_kind"] == "fox":
                    link(dve.scalar_tensor_tensor(cols[:, 2:3], cols[:, 0:1], float(P) ** -.5, cols[:, 1:2],
                                                  ALU.mult, ALU.mult))
                    make_selector(fox["consts"])

            norms = 0
            dve.wait_ge(consts, N_CONSTS)
            for st in stages:
                kind, nth = st["kind"], st["nth"]
                if kind in ("fill", "last_norm"):
                    norm = st.get("norm", "ln2")
                    signal, s0 = (rows_ready, TT * nth) if kind == "fill" else (out_rows, 0)
                    if norm != "plain":
                        norms += 1
                        dve.wait_ge(rows_loaded, 32 * norms)
                    def statistics(tt):
                        if norm == "rms":
                            dve.wait_ge(sumsq, TT * st["rms"] + tt + 1)
                            s = stat[:, tt:tt + 1]
                            link(dve.tensor_scalar(s, s, 1.0 / D, RMS_EPS, ALU.mult, ALU.add))
                            dve.tensor_copy(stat[:, 12 + tt:13 + tt], s).then_inc(root_in, 1)
                        if norm in ("ln1", "ln2"):
                            dve.wait_ge(dve_freed, st["dve"] - TT + tt + 1)
                            sums, mv = stat[:, 16:28], soft[:, 2 * tt:2 * tt + 2]
                            for m in range(2):
                                link(dve.bn_stats(sums[:, 6 * m:6 * m + 6], x[:, tt, COLS * m:COLS * m + COLS]))
                            link(dve.bn_aggr(mv, sums))
                            link(dve.tensor_scalar(stat[:, tt:tt + 1], mv[:, 1:2], LN_EPS, None, ALU.add))
                            dve.tensor_copy(stat[:, 12 + tt:13 + tt], stat[:, tt:tt + 1]).then_inc(root_in, 1)

                    def normalise_rows(tt):
                        if norm == "plain":
                            if st["dve"]:
                                dve.wait_ge(dve_freed, st["dve"] - TT + tt + 1)
                            else:
                                dve.wait_ge(x_loaded[tt], 16)
                            dve.tensor_copy(stat[:, 8 + tt:9 + tt], x[:, tt, 0:1]).then_inc(signal, 1)
                            return
                        y, work = stat[:, 8 + tt:9 + tt], stat[:, 4 + tt:5 + tt]
                        dve.wait_ge(root_out, st["roots"] + tt + 1)
                        link(dve.reciprocal(y, stat[:, 12 + tt:13 + tt]))
                        link(newton(stat[:, tt:tt + 1], y, work))
                        if norm == "rms":
                            dve.scalar_tensor_tensor(xn[:, tt], x[:, tt], y, norm_w[:], ALU.mult, ALU.mult)\
                                .then_inc(signal, 1)
                        else:
                            link(dve.scalar_tensor_tensor(x[:, tt], x[:, tt], soft[:, 2 * tt:2 * tt + 1],
                                                          norm_w[:], ALU.subtract, ALU.mult))
                            dve.scalar_tensor_tensor(x[:, tt], x[:, tt], y, norm_b[:], ALU.mult, ALU.add)\
                                .then_inc(signal, 1)

                    def transposed_low(tt):
                        for n in (2 * tt, 2 * tt + 1):
                            g = n % 2
                            dve.wait_ge(xt_high, 8 * nth + n + 1)
                            at = (slice(None), slice(4 * g, 4 * g + 4), slice(tt * P, tt * P + P))
                            dve.tensor_tensor(xt_lo[at], bank[n][:].rearrange("p (k n) -> p k n", k=4),
                                              xt_hi[at].bitcast(F32), ALU.subtract).then_inc(dve_freed, 1)

                    statistics(0)
                    for tt in range(TT):
                        if tt + 1 < TT:
                            statistics(tt + 1)
                        normalise_rows(tt)
                        if kind == "fill" and tt:
                            transposed_low(tt - 1)
                    if kind == "fill":
                        transposed_low(TT - 1)
                if kind == "prep":
                    prep(st)
                if kind == "project" and st["by"] == "dve" or kind == "ffn_down":
                    to = st.get("to", "residual")
                    keep = st.get("keep", ALPHA)
                    for j in range(st["panels"]):
                        for b in range(4):
                            wait_bank(dve, st, j, b)
                            four = (j + 1) % 2 if kind == "ffn_down" else j % 2
                            src = bank[4 * four + b]
                            n = 4 * j + b
                            if to in ("A", "B", "C"):
                                dst = {"A": buf_a, "B": buf_b, "C": buf_c}[to]
                                o = c_rows[:, b, COLS * j:COLS * j + COLS] if st["rows"] else dst[:, n]
                                dve.tensor_copy(o, src[:]).then_inc(dve_freed, 1)
                            if to == "residual":
                                o = x[:, b, COLS * j:COLS * j + COLS]
                                dve.scalar_tensor_tensor(o, o, keep, src[:], ALU.mult, ALU.add).then_inc(dve_freed, 1)
                            if to.startswith("rotary"):
                                scale = 64 ** -.5 if to[-1] == "A" else 1.0
                                dst = (buf_a if to[-1] == "A" else buf_b)[:, n]
                                dve.tensor_copy(rotary_in[:], src[:]).then_inc(dve_freed, 1)
                                dve.wait_ge(dve_freed, st["dve"] + n + 1)
                                link(dve.stream_shuffle(rotary_sin[:], rotary_in[:], SWAP))
                                link(dve.scalar_tensor_tensor(dst, rotary_in[:], scale, rotary[:, 0], ALU.mult, ALU.mult))
                                link(dve.scalar_tensor_tensor(rotary_sin[:], rotary_sin[:], scale, rotary[:, 1],
                                                              ALU.mult, ALU.mult))
                                link(dve.tensor_tensor(dst, dst, rotary_sin[:], ALU.add))
                            if to == "conv":
                                y = buf_a[:, n] if n < 8 else buf_b[:, n - 8]
                                link(dve.tensor_scalar(y, src[:], cols[:, 48 + n:49 + n], None, ALU.mult))
                                for k in range(3):
                                    s = 3 - k
                                    ins = dve.scalar_tensor_tensor(y[:, s:], src[:, :SEQ - s],
                                                                   cols[:, 16 * k + n:16 * k + n + 1], y[:, s:],
                                                                   ALU.mult, ALU.add)
                                    if k < 2:
                                        link(ins)
                                ins.then_inc(dve_freed, 1)
                            if to == "gated conv":
                                if n == 0:
                                    dve.wait_ge(act_freed, st["act"])
                                    dve.wait_ge(mixer_loaded, 16 * st["loads"])
                                dve.tensor_tensor(buf_a[:, n], buf_a[:, n], src[:], ALU.mult).then_inc(dve_freed, 1)
                                dve.wait_ge(dve_freed, st["dve"] + n + 1)
                                taps(buf_b[:, n], buf_a[:, n], [cols[:, 8 * k + n:8 * k + n + 1] for k in range(3)])
                            if to == "gate G":
                                if n:
                                    low(st, n - 1)
                                    dve.wait_ge(gated_low, st["gated"] + n)
                                dve.tensor_tensor(gated_conv[:], buf_b[:, n], src[:], ALU.mult).then_inc(dve_freed, 1)
                    if to == "gate G":
                        low(st, KT - 1)
                if kind == "ffn_up":
                    def up(j, four, first=False):
                        for m in range(2):
                            if m == 0:
                                dve.wait_ge(bank_full, st["full"] + 3 * j + 3)
                            else:
                                dve.wait_ge(w_used[1], st["pair"] + j + 1)
                            dve.wait_ge(act_freed, st["act"] + 2 * j + m + 1)
                            if not first:
                                dve.wait_ge(h_low, FT * nth + 2 * j + m - 1)
                            dve.tensor_tensor(hidden[:, m], gate_act[:, m], bank[4 * four + 2 + m][:], ALU.mult)\
                                .then_inc(dve_freed, 1)
                        for m in range(2):
                            dve.wait_ge(h_high, FT * nth + 2 * j + m + 1)
                            at = 2 * j + m
                            o, hi = [v[:, at] if first else v[:, bass.ds(at, 1)].rearrange("p a n -> p (a n)")
                                     for v in (h_lo, h_hi)]
                            dve.tensor_tensor(o, hidden[:, m], hi.bitcast(F32), ALU.subtract).then_inc(h_low, 1)

                    up(0, 0, True)
                    with dve.Fori(0, 5) as i:
                        for j in range(2):
                            up(2 * i + j + 1, 1 - j)
                if kind == "fox":
                    dve.wait_ge(small_full, st["small"])
                    link(dve.tensor_tensor(logf[:], bank[0][:, 0:32], vec[:, 0:32], ALU.add))
                    dve.scalar_tensor_tensor(logf_e[:], logf[:], -1.0, logf[:], ALU.mult, ALU.max).then_inc(fox["logits"], 1)
                    link(dve.tensor_scalar(logf[:], logf[:], 0.0, None, ALU.min))
                    dve.wait_ge(fox["log"], nth + 1)
                    dve.tensor_tensor(logf[:], logf_e[:], logf[:], ALU.subtract).then_inc(fox["cum_in"], 1)
                    dve.wait_ge(fox["cum_full"], nth + 1)
                    dve.tensor_copy(cum_rows[0:8], bank[1][0:8]).then_inc(fox["cum_rows"], 1)

                    norm_rows(st, bank[2], 16, P, RMS_EPS)

                    def normalise(h):
                        dve.wait_ge(fox["norm_full"], 16 * nth + 2 * h + 2)
                        dve.scalar_tensor_tensor(q_n[:, h % 2], buf_a[:, h], cols[:, 2:3], bank[0][:],
                                                 ALU.mult, ALU.mult).then_inc(fox["qk_ready"], 1)
                        dve.tensor_tensor(k_n[:, h % 2], buf_b[:, h], bank[1][:], ALU.mult)\
                            .then_inc(fox["qk_ready"], 1)

                    def row_max(n):
                        dve.wait_ge(fox["scores"], 32 * nth + n + 1)
                        dve.tensor_reduce(soft[:, n % 4:n % 4 + 1], bank[2 + n % 3][:, 0:(n % TT + 1) * P], AX,
                                          ALU.max, negate=True).then_inc(fox["max"], 1)

                    def divide(n):
                        dve.wait_ge(fox["exps"], 32 * nth + n + 1)
                        s = soft[:, 8 + n % 4:9 + n % 4]
                        link(dve.reciprocal(s, soft[:, 4 + n % 4:5 + n % 4]))
                        p = probs[:, n % 2, 0:(n % TT + 1) * P]
                        dve.tensor_scalar(p, p, s, None, ALU.mult).then_inc(fox["normed"], 1)

                    def gate(h):
                        dve.wait_ge(fox["out_full"], 8 * nth + h + 1)
                        if h == 0:
                            dve.wait_ge(act_freed, st["act"])
                        if h:
                            dve.wait_ge(gated_low, st["gated"] + h)
                        dve.tensor_tensor(gated[:], buf_d[:, h], bank[7][:], ALU.mult).then_inc(gated_raw, 1)

                    normalise(0)
                    n_all = FOX_HEADS * TT
                    row_max(0)
                    for n in range(n_all):
                        if n + 1 < n_all:
                            row_max(n + 1)
                        divide(n)
                        if n % TT == 1 and n // TT + 1 < FOX_HEADS:
                            normalise(n // TT + 1)
                        if n % TT == 2 and n > TT:
                            gate(n // TT - 1)
                        if n % TT == 3 and n > TT:
                            low(st, n // TT - 1)
                    gate(FOX_HEADS - 1)
                    low(st, FOX_HEADS - 1)

                if kind == "attn":
                    make_selector(diff["selector"])
                    dve.wait_ge(diff["lam_out"], 1)
                    link(dve.scalar_tensor_tensor(lam_work[:, 2:3], lam_work[:, 0:1], -1.0, lam_work[:, 1:2],
                                                  ALU.mult, ALU.add))
                    link(dve.tensor_scalar(lam_work[:, 2:3], lam_work[:, 2:3], LAM_INIT, None, ALU.subtract))
                    neg_lam = lam_work[:, 2:3]

                    def pair_max(n):
                        for c in range(2):
                            k = 2 * (n % 2) + c
                            dve.wait_ge(diff["scores"], 2 * n + c + 1)
                            if n >= 2:
                                dve.wait_ge(diff["exps"], 2 * (n - 2) + c + 1)
                            dve.tensor_reduce(soft[:, k:k + 1], bank[2 * (n % 3) + c][:, 0:(n % TT + 1) * P], AX,
                                              ALU.max, negate=True).then_inc(diff["max"], 1)

                    def mix(n):
                        dve.wait_ge(diff["exps"], 2 * n + 2)
                        k = 2 * (n % 2)
                        link(dve.reciprocal(soft[:, 8 + k:10 + k], soft[:, 4 + k:6 + k]))
                        link(dve.tensor_tensor(soft[:, 12 + k:13 + k], soft[:, 9 + k:10 + k], neg_lam, ALU.mult))
                        p0, p1 = [pair_probs[:, n % 2, c, 0:(n % TT + 1) * P] for c in range(2)]
                        link(dve.tensor_scalar(p1, p1, soft[:, 12 + k:13 + k], None, ALU.mult))
                        dve.scalar_tensor_tensor(p0, p0, soft[:, 8 + k:9 + k], p1, ALU.mult, ALU.add)\
                            .then_inc(diff["mixed"], 1)

                    n_all = ATTN_HEADS * TT
                    pair_max(0)
                    for n in range(n_all):
                        if n + 1 < n_all:
                            pair_max(n + 1)
                        mix(n)
                    norm_rows(st, bank[2], 8, P, LN_EPS, n_squares=8)
                    for h in range(ATTN_HEADS):
                        dve.wait_ge(diff["spread"], h + 1)
                        if h:
                            dve.wait_ge(gated_low, st["gated"] + h)
                        dve.scalar_tensor_tensor(gated[:], buf_d[:, h], cols[:, 1:2], bank[h % 2][:],
                                                 ALU.mult, ALU.mult).then_inc(gated_raw, 1)
                        low(st, h)
                if kind == "gla":
                    dve.wait_ge(small_full, st["small"])
                    dve.tensor_copy(vec[:, 0:64], bank[0][:, 0:64]).then_inc(gla["low"], 1)
                    make_resets = resets[:].rearrange("p (c l) -> p c l", l=CHUNK)
                    link(dve.memset(resets[:], 1.0))
                    link(dve.memset(make_resets[:, :, 0:1], 0.0))
                    dve.wait_ge(gla["low_turned"], 1)
                    dve.tensor_copy(low_rank[0:GLA_RANK], bank[1][0:GLA_RANK]).then_inc(gla["low_rows"], 1)

                    def gate_logits(h):
                        x_, a_ = gate_log[:, h % 2], gate_abs[:, h % 2]
                        dve.wait_ge(gla["gates"], h + 1)
                        link(dve.tensor_scalar(x_, bank[2 + h][:], cols[:, h:h + 1], None, ALU.add))
                        dve.scalar_tensor_tensor(a_, x_, -1.0, x_, ALU.mult, ALU.max).then_inc(gla["abs"], 1)

                    def gate_log_sigmoid(h):
                        x_, a_ = gate_log[:, h % 2], gate_abs[:, h % 2]
                        link(dve.tensor_scalar(x_, x_, 0.0, None, ALU.min))
                        dve.wait_ge(gla["log"], h + 1)
                        link(dve.tensor_tensor(a_, x_, a_, ALU.subtract))
                        dve.tensor_tensor_scan(x_, resets[:], a_, 0.0, ALU.mult, ALU.add).then_inc(gla["sums"], 1)

                    gate_logits(0)
                    for h in range(GLA_HEADS):
                        if h + 1 < GLA_HEADS:
                            gate_logits(h + 1)
                        gate_log_sigmoid(h)
                        dve.wait_ge(gla["decays"], 2 * h + 2)
                        link(dve.scalar_tensor_tensor(buf_b[:, h], buf_a[:, h], float(P) ** -.5, decayed[:, h],
                                                      ALU.mult, ALU.mult))
                        link(dve.tensor_tensor(buf_b[:, 4 + h], buf_a[:, 4 + h], grown[:, h % 2], ALU.mult))
                        o, k, d_ = [v.rearrange("p (c l) -> p c l", l=CHUNK)
                                    for v in (buf_a[:, 4 + h], buf_b[:, 4 + h], decayed[:, h])]
                        dve.tensor_tensor(o, k, d_[:, :, CHUNK - 1:CHUNK].to_broadcast([P, 8, CHUNK]), ALU.mult)\
                            .then_inc(gla["keys"], 1)

                    def mask(tt):
                        dve.wait_ge(gla["inner_full"], tt + 1)
                        dve.tensor_tensor(inner[:, tt % 2], bank[2 + tt % 2][:].rearrange("p (h l) -> p h l", l=P),
                                          chunk_tri[:].unsqueeze(1).to_broadcast([P, GLA_HEADS, P]), ALU.mult)\
                            .then_inc(gla["inner"], 1)

                    mask(0)
                    for c in range(7):
                        if c % 2 == 0 and c // 2 + 1 < TT:
                            if c >= 2:
                                dve.wait_ge(gla["out_full"], c - 2)
                            mask(c // 2 + 1)
                        new, old = gla_state[:, (c + 1) % 2], gla_state[:, c % 2]
                        for g in range(2):
                            dve.wait_ge(gla["update"], 2 * c + g + 1)
                            for h in (2 * g, 2 * g + 1):
                                o = slice(h * 256, h * 256 + 256)
                                src = bank[6 + g][:, (h % 2) * 256:(h % 2) * 256 + 256]
                                if c == 0:
                                    ins = dve.tensor_copy(new[:, o], src)
                                else:
                                    ins = dve.scalar_tensor_tensor(
                                        new[:, o], old[:, o], decayed[:, h, CHUNK * (c + 1) - 1:CHUNK * (c + 1)], src,
                                        ALU.mult, ALU.add)
                                if h < 3:
                                    link(ins)
                        ins.then_inc(gla["state"], 1)
                        dve.wait_ge(gla["state"], c + 1)
                    make_selector(gla["state"])
                    norm_rows(st, bank[0], GLA_HEADS, 2 * P, RMS_EPS, n_squares=8)
                    for n in range(8):
                        h = n // 2
                        dve.wait_ge(gla["spread"], h + 1)
                        if n:
                            dve.wait_ge(gated_low, st["gated"] + n)
                        link(dve.scalar_tensor_tensor(gated[:], buf_a[:, n], cols[:, 4 + n % 2:5 + n % 2],
                                                      bank[2 + h % 2][:], ALU.mult, ALU.mult))
                        dve.tensor_tensor(gated[:], gated[:], buf_d[:, n], ALU.mult).then_inc(gated_raw, 1)
                        low(st, n)
                if kind == "gdn":
                    def by_tile(ap):
                        return ap.rearrange("p (t n) -> p t n", t=TT)

                    def wide(ap, n=P):
                        return ap.unsqueeze(2).to_broadcast([P, ap.shape[1], n])

                    def four_of(b):
                        return bank[b][:].rearrange("p (a n) -> p a n", n=P)

                    a, b = [bank[0][:, 0:64].rearrange("p (t m n) -> p m t n", t=TT, m=2)[:, m] for m in range(2)]
                    dve.wait_ge(small_full, st["small"])
                    link(dve.tensor_tensor(by_tile(small[:, 0]), a, by_tile(vec[:, 32:64]), ALU.add))
                    link(dve.tensor_copy(by_tile(small[:, 5]), b))
                    dve.scalar_tensor_tensor(small[:, 1], small[:, 0], -1.0, small[:, 0], ALU.mult, ALU.max)\
                        .then_inc(gdn["logits"], 1)
                    dve.wait_ge(gdn["logs"], 3)
                    link(dve.scalar_tensor_tensor(small[:, 0], small[:, 0], 0.0, small[:, 1], ALU.max, ALU.add))
                    dve.scalar_tensor_tensor(small[:, 0], small[:, 0], -1.0, vec[:, 0:32], ALU.mult, ALU.mult)\
                        .then_inc(gdn["g"], 1)
                    link(dve.tensor_scalar(small[:, 6], small[:, 5], -1.0, None, ALU.mult))
                    dve.wait_ge(gdn["sums"], 1)
                    link(dve.tensor_copy(small[:, 2], bank[2][:, 0:32]))
                    link(dve.tensor_copy(cum_rows[0:GDN_V], bank[3][0:GDN_V]))
                    dve.tensor_tensor(small[:, 3], bank[2][:, 32:64], small[:, 2], ALU.subtract)\
                        .then_inc(gdn["columns"], 1)
                    dve.wait_ge(gdn["exps"], 2)
                    link(dve.tensor_tensor(small[:, 4], small[:, 4], small[:, 5], ALU.mult))
                    link(dve.memset(delta_state[:], 0.0))
                    make_selector(gdn["state"], GDN_V)
                    norm_rows(st, bank[1], 8, 1, RMS_EPS, n_squares=8)
                    for n in range(8):
                        dve.wait_ge(gdn["spread"], n + 1)
                        dve.scalar_tensor_tensor(buf_a[:, n], buf_a[:, n], float(P) ** -.5 if n < GDN_QK else 1.0,
                                                 bank[4 + n % 2][:], ALU.mult, ALU.mult).then_inc(gdn["qk_ready"], 1)
                    for n in range(2 * TT):
                        tt, g = divmod(n, 2)
                        dve.wait_ge(gdn["values_full"], n + 1)
                        dve.tensor_tensor(u_rows[:, tt, 4 * g:4 * g + 4], four_of(4 + g),
                                          wide(small[:, 5, tt * GDN_V + 4 * g:tt * GDN_V + 4 * g + 4]), ALU.mult)\
                            .then_inc(gdn["values_rows"], 1)
                    dve.wait_ge(gdn["keys_rows"], TT)
                    dve.tensor_copy(small[:, 7], small[:, 4]).then_inc(gdn["factors"], 1)
                    dve.wait_ge(gdn["values_rows"], 2 * TT)

                    def paired(ap):
                        return ap.unsqueeze(2).to_broadcast([P, 2, 2, P])

                    def by_pair(ap):
                        return ap.rearrange("p (a b) n -> p a b n", b=2)

                    def masked(mask):
                        return mask.unsqueeze(1).to_broadcast([P, 4, P])

                    def build(tt, g):
                        four, at = slice(4 * g, 4 * g + 4), slice(tt * GDN_V + 4 * g, tt * GDN_V + 4 * g + 4)
                        kq, m = bank[2 * g + 1][:].rearrange("p (c a n) -> p c a n", c=2, n=P), tt % 2
                        dve.wait_ge(solve["build_full"][g], tt + 1)
                        if tt >= 2:
                            dve.wait_ge(gdn["out_full"], 2 * tt - 2)
                        link(dve.tensor_tensor(x1[:, four], four_of(2 * g), wide(small[:, 2, at]), ALU.subtract))
                        dve.tensor_scalar(x2[:, four], x1[:, four], 0.0, None, ALU.max)\
                            .then_inc(solve["differences"][g], 1)
                        dve.tensor_scalar(qk_dec[m][:, four], x1[:, four], 0.0, None, ALU.min)\
                            .then_inc(solve["differences"][g], 1)
                        keys = key_rows[:, tt, 2 * g * P:(2 * g + 2) * P].rearrange("p (a n) -> p a n", n=P)
                        link(dve.tensor_tensor(by_pair(k_dec[m][:, four]), paired(keys),
                                               by_pair(wide(small[:, 3, at])), ALU.mult))
                        dve.wait_ge(solve["decays"][g], 3 * tt + 1)
                        link(dve.tensor_copy(chunk_decay[:, tt, four], x3[:, four, CHUNK - 1::CHUNK]))
                        link(dve.tensor_tensor(by_pair(q_dec[m][:, four]), paired(buf_a[:, 2 * g:2 * g + 2, tt * P:tt * P + P]),
                                               by_pair(x3[:, four]), ALU.mult))
                        dve.wait_ge(solve["decays"][g], 3 * tt + 2)
                        link(dve.tensor_tensor(by_pair(x2[:, four]), by_pair(x2[:, four]), paired(kq[:, 0]), ALU.mult))
                        link(dve.tensor_tensor(x2[:, four], x2[:, four], wide(small[:, 6, at]), ALU.mult))
                        dve.wait_ge(solve["decays"][g], 3 * tt + 3)
                        link(dve.tensor_tensor(by_pair(qk_dec[m][:, four]), by_pair(qk_dec[m][:, four]), paired(kq[:, 1]),
                                               ALU.mult))
                        link(dve.tensor_tensor(qk_dec[m][:, four], qk_dec[m][:, four], masked(chunk_tri[:]), ALU.mult))
                        link(dve.tensor_tensor(cross[:, four], x2[:, four], masked(across_blocks), ALU.mult))
                        dve.tensor_tensor(x1[:, four], x2[:, four], masked(in_block), ALU.mult)\
                            .then_inc(solve["lower"][g], 1)

                    def take_step(tt, g, n):
                        four = slice(4 * g, 4 * g + 4)
                        src = four_of(2 * g + n % 2)
                        dve.wait_ge(solve["full"][g], LAST_STEP * tt + n)
                        if n in ACT_STEPS:
                            solved(dve, g, tt, n, ("act",))
                        if n in (1, 11):
                            o, other = (inverse if n == 1 else x2)[:, four], masked(ident[:])
                        elif n == 14:
                            o = other = x2[:, four]
                        else:
                            o = other = inverse[:, four]
                        if n == 17:
                            ins = dve.tensor_copy(u_rows[:, tt, four], src)
                        else:
                            ins = dve.tensor_tensor(o, other, src, ALU.add)
                        ins.then_inc(solve["dve"][g], 1)
                        if n == 14:
                            at = slice(tt * GDN_V + 4 * g, tt * GDN_V + 4 * g + 4)
                            keys = key_rows[:, tt, 2 * g * P:(2 * g + 2) * P].rearrange("p (a n) -> p a n", n=P)
                            dve.tensor_tensor(by_pair(x3[:, four]), paired(keys), by_pair(wide(small[:, 4, at])), ALU.mult)\
                                .then_inc(solve["kbg"][g], 1)

                    def new_values(c):
                        tt, rows = c // 2, slice(CHUNK * (c % 2), CHUNK * (c % 2) + CHUNK)
                        for g in range(2):
                            four = slice(4 * g, 4 * g + 4)
                            solved(dve, g, tt, LAST_STEP)
                            dve.wait_ge(gdn["ws"], 2 * c + g + 1)
                            dve.tensor_tensor(v_new[rows, four], u_rows[rows, tt, four], four_of(4 + g)[rows], ALU.subtract)\
                                .then_inc(gdn["v_new"], 1)

                    def update(c):
                        tt = c // 2
                        for g in range(2):
                            dve.wait_ge(gdn["update"], 2 * c + g + 1)
                            for i in range(4):
                                h = 4 * g + i
                                ins = dve.scalar_tensor_tensor(
                                    delta_state[:, h], delta_state[:, h], chunk_decay[:, tt, h, c % 2:c % 2 + 1],
                                    bank[4 + g][:, i * P:i * P + P], ALU.mult, ALU.add)
                                if i < 3:
                                    link(ins)
                            ins.then_inc(gdn["state"], 1)

                    for tt in range(TT + 1):
                        for g in range(2 if tt < TT else 0):
                            build(tt, g)
                        for n in range(1, LAST_STEP + 1):
                            for g in range(2 if tt < TT and n in DVE_STEPS else 0):
                                take_step(tt, g, n)
                            if tt and n in RECURRENCE_AFTER:
                                part = RECURRENCE_AFTER.index(n)
                                c = 2 * (tt - 1) + part // 2
                                if part % 2 == 0:
                                    new_values(c)
                                elif c < 2 * TT - 1:
                                    update(c)
                    norm_rows(st, bank[0], 8, P, RMS_EPS, norm=1, base=8, n_squares=8)
                    for h in range(GDN_V):
                        dve.wait_ge(gdn["norm_spread"], h + 1)
                        if h:
                            dve.wait_ge(gated_low, st["gated"] + h)
                        link(dve.scalar_tensor_tensor(by_tile(gated[:]), u_rows[:, :, h], cols[:, 64:65],
                                                      by_tile(bank[2 + h % 2][:]), ALU.mult, ALU.mult))
                        dve.tensor_tensor(gated[:], gated[:], buf_d[:, h], ALU.mult).then_inc(gated_raw, 1)
                        low(st, h)


_INS = ["x", "norm_w", "fox_w_in", "fox_b_f", "fox_q_gain", "fox_k_gain", "fox_w_out", "gla_w_in", "gla_w_gate_up",
        "gla_b_gate", "gla_o_gain", "gla_w_out", "gdn_w_in", "gdn_conv_w", "gdn_a_log", "gdn_dt_bias", "gdn_o_gain",
        "gdn_w_out", "attn_w_qkv_2", "attn_w_o_2", "attn_lambda_q1_2", "attn_lambda_k1_2", "attn_lambda_q2_2",
        "attn_lambda_k2_2", "attn_subln_g_2", "conv_w_in_2", "conv_w_2", "conv_w_out_2", "ffn_w_gate_2",
        "ffn_w_up_2", "ffn_w_down_2", "ln1_g_2", "ln1_b_2", "ln2_g_2", "ln2_b_2"]


def kernel(**inputs):
    import concourse.bacc as _bacc
    from concourse.bass_utils import run_bass_kernel_spmd as _run

    nc = _bacc.Bacc("TRN2", target_bir_lowering=False, num_devices=1)
    arrays = {f"in_{name}_dram": np.ascontiguousarray(inputs[name]) for name in _INS}
    arrays["rotary_dram"] = rotary_tables()
    arrays["block_masks_dram"] = block_masks()
    t = {name: nc.dram_tensor(f"in_{name}_dram", arrays[f"in_{name}_dram"].shape, F32, kind="ExternalInput").ap()
         for name in _INS}
    t["rotary"] = nc.dram_tensor("rotary_dram", arrays["rotary_dram"].shape, F32, kind="ExternalInput").ap()
    t["block_masks"] = nc.dram_tensor("block_masks_dram", (3, P, P), F32, kind="ExternalInput").ap()
    out = nc.dram_tensor("out_0_dram", (1, SEQ, D), F32, kind="ExternalOutput").ap()
    six_mixer_stack(nc, t, out)
    r = _run(nc, [arrays], core_ids=[0])
    return r.results[0]["out_0_dram"]
```

```python
from contextlib import ExitStack

import concourse.bass as bass
import numpy as np
from concourse import mybir

F32 = mybir.dt.float32
F32R = mybir.dt.float32r
BF16 = mybir.dt.bfloat16
ALU = mybir.AluOpType
ACT = mybir.ActivationFunctionType
AX = mybir.AxisListType.X

P = 128
SEQ = 512
D = 1024
TT = SEQ // P
KT = D // P
COLS = 512
HALF = 4
D_FF = 2816
FT = D_FF // P
FOX_HEADS = 8
GLA_HEADS = 4
GLA_RANK = 16
GDN_QK = 4
GDN_V = 8
ATTN_HEADS = 8
CHUNK = 64
RMS_EPS = 1e-6
LN_EPS = 1e-5
ALPHA = 4 ** 0.25
NEG = -1e30
LAM_INIT = 0.8 - 0.6
LAYERS = ("fox", "gla", "gdn", "fox", "attn", "ffn", "conv", "ffn")
SWAP = [*range(8, 16), *range(8), *range(16, 32)]
ACT_STEPS = (1, 2, 3, 5, 6, 8, 10, 11, 12, 13, 15, 16)
DVE_STEPS = (1, 4, 7, 9, 11, 14, 17)
LAST_STEP = 17
BUILD_TURNS = 5
TURNS = BUILD_TURNS + LAST_STEP
RECURRENCE_TURNS = (1, 3, 6, 9)


def staggered():
    for n in range((TT + 1) * TURNS + TURNS // 2):
        for g in range(2):
            at = n - g * (TURNS // 2)
            if 0 <= at < (TT + 1) * TURNS:
                yield at // TURNS, g, at % TURNS


def rotary_tables():
    half = 8
    inv = np.power(np.float32(500000.0), -np.arange(0, 2 * half, 2, dtype=np.float32) / np.float32(2 * half))
    angle = np.arange(SEQ, dtype=np.float32)[None, :] * inv[:, None].astype(np.float32)
    table = np.zeros((2, P, SEQ), np.float32)
    table[0] = 1.0
    for c in range(0, P, P // 2):
        for m, sign in enumerate((-1.0, 1.0)):
            table[0, c + half * m:c + half * m + half] = np.cos(angle)
            table[1, c + half * m:c + half * m + half] = sign * np.sin(angle)
    return table


def block_masks():
    row, col = np.arange(P)[:, None], np.arange(P)[None, :]
    same = row // CHUNK == col // CHUNK
    block = row // 16 == col // 16
    return np.stack([block & (col < row), same & ~block & (col < row), same]).astype(np.float32)


PREP_LOADS = {"fox": 4, "gla": 4, "gdn": 9, "attn": 7, "conv": 3}


def plan(layers):
    stages = []
    at = dict(pair=0, full=0, filled=0, act=0, dve=0, gated=0, small=0, loads=0, rms=0, roots=0,
              squares=0, norms=0, mixer={})

    def stage(kind, pairs=0, panels=0, full=0, filled=0, act=0, dve=0, gated=0,
              small=0, loads=0, rms=0, roots=0, squares=0, norms=0, **more):
        st = dict(kind=kind, panels=panels, n_full=full, n_act=act, n_dve=dve, **{k: at[k] for k in at if k != "mixer"})
        st.update(more)
        st["nth"] = at["mixer"].get(kind, 0)
        at["mixer"][kind] = st["nth"] + 1
        before = stages[-1] if stages else None
        st["free0"] = (st["act"], st["dve"])
        if before and before["kind"] in ("project", "ffn_up") and kind in ("project", "ffn_up", "ffn_down"):
            st["free0"] = (st["act"] - before["n_act"] // before["panels"], st["dve"] - before["n_dve"] // before["panels"])
        st["after_fill"] = [s["kind"] for s in stages if s["kind"] not in ("prep", "loads")][-1:] == ["fill"]
        stages.append(st)
        for key, n in (("pair", pairs), ("full", full), ("filled", filled), ("act", act), ("dve", dve),
                       ("gated", gated), ("small", small), ("loads", loads), ("rms", rms),
                       ("roots", roots), ("squares", squares), ("norms", norms)):
            at[key] += n

    def fill(norm, which=0):
        stage("fill", filled=8, dve=8, norm=norm, which=which, rms=int(norm == "rms"),
              roots=TT * (norm != "plain"))

    def loads(n):
        if n < len(layers) and layers[n] in PREP_LOADS:
            stage("loads", layer_kind=layers[n], layer=layers[:n].count(layers[n]), loads=PREP_LOADS[layers[n]])

    def project(weights, layer, col, panels, rows, by, to, gated=0, sides=()):
        stage("project", pairs=panels, panels=panels, full=3 * panels, weights=weights, layer=layer, col=col,
              rows=rows, by=by, to=to, sides=sides, nth_layer=n_fox if weights.startswith("fox") else 0, act=4 * panels * (by == "act"), dve=4 * panels * (by == "dve"), gated=gated,
              keep=ALPHA if weights in ("attn_w_o_2", "conv_w_out_2") else 1.0)

    n_fox = n_ffn = 0
    loads(0)
    for n, name in enumerate(layers):
        if name == "fox":
            fill("rms", n)
            stage("prep", layer_kind="fox", layer=n_fox, small=1)
            project("fox_w_in", n_fox, 0, 2, False, "dve", "A", sides=(None, "fox logits"))
            project("fox_w_in", n_fox, D, 2, False, "dve", "B", sides=("fox sums",))
            project("fox_w_in", n_fox, 3 * D, 2, False, "act", "silu D")
            project("fox_w_in", n_fox, 2 * D, 2, True, "dve", "C")
            stage("fox", layer=n_fox, gated=KT, squares=16, norms=1, roots=1)
            loads(n + 1)
            project("fox_w_out", n_fox, 0, 2, True, "dve", "residual")
            n_fox += 1
        if name == "gla":
            fill("rms", n)
            stage("prep", layer_kind="gla", layer=0, small=1)
            project("gla_w_in", 0, 2 * D, 2, False, "act", "silu D", sides=(None, "gla logits"))
            project("gla_w_in", 0, 0, 2, False, "dve", "A", sides=("gla gate 0", "gla gate 1"))
            project("gla_w_in", 0, D, 2, True, "dve", "C", sides=("gla gate 2", "gla gate 3"))
            stage("gla", gated=KT, squares=8, norms=1, roots=1)
            loads(n + 1)
            project("gla_w_out", 0, 0, 2, True, "dve", "residual")
        if name == "gdn":
            fill("rms", n)
            stage("prep", layer_kind="gdn", layer=0, small=1)
            project("gdn_w_in", 0, 0, 4, False, "dve", "conv", sides=(None, "gdn logits", "gdn sums"))
            project("gdn_w_in", 0, 2 * D, 2, False, "act", "silu D")
            stage("gdn", gated=KT, squares=16, norms=2, roots=2)
            loads(n + 1)
            project("gdn_w_out", 0, 0, 2, True, "dve", "residual")
        if name == "attn":
            fill("plain")
            stage("prep", layer_kind="attn", layer=0)
            project("attn_w_qkv_2", 0, 0, 2, False, "dve", "rotary A")
            project("attn_w_qkv_2", 0, D, 2, False, "dve", "rotary B")
            project("attn_w_qkv_2", 0, 2 * D, 2, True, "act", "copy C")
            stage("attn", gated=KT, squares=8, norms=1, roots=1)
            project("attn_w_o_2", 0, 0, 2, True, "dve", "residual")
            fill("ln1", n_ffn)
        if name == "conv":
            stage("prep", layer_kind="conv", layer=0)
            project("conv_w_in_2", 0, D, 2, False, "act", "copy A")
            project("conv_w_in_2", 0, 2 * D, 2, False, "dve", "gated conv")
            project("conv_w_in_2", 0, 0, 2, False, "dve", "gate G", gated=KT)
            project("conv_w_out_2", 0, 0, 2, True, "dve", "residual")
            fill("ln1", n_ffn)
        if name == "ffn":
            stage("ffn_up", pairs=11, panels=11, full=33, act=22, dve=22, layer=n_ffn)
            stage("ffn_down", pairs=6, panels=2, full=6, dve=8, layer=n_ffn)
            if n == len(layers) - 1:
                stage("last_norm", layer=n_ffn)
            else:
                loads(n + 1)
                fill("ln2", n_ffn)
            n_ffn += 1
    return stages, at


def six_mixer_stack(nc, t, out):
    stages, total = plan(LAYERS)
    n_pairs = total["pair"]
    ctx = ExitStack()
    with ctx:
        base = -(-nc.sbuf_base // 64) * 64
        KB = 1024

        def sb(name, offset_kb, shape, dt=F32):
            return nc.alloc_sbuf_tensor_at(name, shape, dt, offset=base + int(offset_kb * KB))

        raw = sb("weights_raw", 0, [P, 2, HALF, COLS])
        w_hi = sb("weights_high", 16, [P, 2, HALF, COLS], F32R)
        w_lo = sb("weights_low", 32, [P, 2, HALF, COLS], F32R)
        x = sb("x", 48, [P, TT, D])
        xt_hi = sb("xt_high", 64, [P, KT, SEQ], F32R)
        xt_lo = sb("xt_low", 80, [P, KT, SEQ], F32R)
        buf_a = sb("A", 96, [P, 8, SEQ])
        buf_b = sb("B", 112, [P, 8, SEQ])
        buf_c = sb("C", 128, [P, 8, SEQ])
        buf_d = sb("D", 144, [P, 8, SEQ])
        c_rows = buf_c[:].rearrange("p (t c) n -> p t (c n)", t=TT)
        g_hi = sb("gated_high", 160, [P, KT, SEQ], F32R)
        g_lo = sb("gated_low", 176, [P, KT, SEQ], F32R)
        xn = sb("x_normalised", 96, [P, TT, D])
        h_hi = sb("hidden_high", 96, [P, FT, SEQ], F32R)
        h_lo = sb("hidden_low", 140, [P, FT, SEQ], F32R)
        gate_act = sb("gate_activated", 184, [P, 2, SEQ])
        hidden = sb("hidden", 188, [P, 2, SEQ])
        norm_w = sb("norm_weight_rows", 192, [P, D])
        norm_b = sb("norm_bias_rows", 196, [P, D])
        C0 = 200
        N_CONSTS = 8
        ident = sb("identity", C0, [P, P])
        ones = sb("ones", C0 + .5, [P, P])
        tri = sb("triangle", C0 + 1, [P, P])
        chunk_tri = sb("chunk_triangle", C0 + 1.5, [P, P])
        ident_b = sb("identity_bf16", C0 + 2, [P, P], BF16)
        mask_b = sb("causal_mask", C0 + 2.25, [P, P], BF16)
        mask2_b = sb("chunk_mask", C0 + 2.5, [P, P], BF16)
        stat = sb("row_statistics", C0 + 2.75, [P, 32])
        soft = sb("softmax_statistics", C0 + 2.875, [P, 32])
        s_raw = sb("small_raw", C0 + 3, [P, KT, 16])
        s_hi = sb("small_high", C0 + 3.5, [P, KT, 16], F32R)
        s_lo = sb("small_low", C0 + 4, [P, KT, 16], F32R)
        cols = sb("columns", C0 + 4.5, [P, 96])
        vec = sb("vectors", C0 + 4.875, [P, 64])
        logf = sb("log_forget", C0 + 5.125, [P, 32])
        logf_e = sb("log_forget_part", C0 + 5.25, [P, 32])
        cum_rows = sb("cumulated_rows", C0 + 5.375, [P, SEQ])
        pick = sb("column_pick", C0 + 7.375, [P, 31])
        q_n = sb("q_normalised", 64, [P, 2, SEQ])
        k_n = sb("k_normalised", 68, [P, 2, SEQ])
        squares = sb("squares", 72, [P, 2, SEQ])
        probs = sb("probs", 76, [P, 2, SEQ])
        probs_t = sb("probs_transposed", 80, [P, 2, TT, SEQ])
        pair_probs = sb("pair_probs", 64, [P, 2, 2, SEQ])
        rotary = sb("rotary_tables", 192, [P, 2, SEQ])
        rotary_in = sb("rotary_source", 196, [P, SEQ])
        rotary_sin = sb("rotary_shuffled", 198, [P, SEQ])
        lam_rows = sb("lambda_vectors", C0 + 5.375, [P, 4, 64])
        lam_work = sb("lambda_work", C0 + 6.375, [P, 64])
        low_rank = sb("gate_low_rank", 160, [P, SEQ])
        resets = sb("chunk_resets", 162, [P, SEQ])
        gate_abs = sb("gate_absolute", 164, [P, 2, SEQ])
        gate_log = sb("gate_logarithm", 168, [P, 2, SEQ])
        grown = sb("inverse_decay", 184, [P, GLA_HEADS, SEQ])
        decayed = sb("decay", 176, [P, GLA_HEADS, SEQ])
        gla_state = sb("gla_state", 88, [P, 2, GLA_HEADS * 256])
        k_rows = sb("keys_decayed_rows", 64, [P, TT, GLA_HEADS * P])
        inner = sb("scores_in_chunks", 72, [P, 2, GLA_HEADS, P])
        up_rows = sb("gate_up_weights", C0 + 5.375, [P, SEQ])
        def heads(name, offset_kb):
            return sb(name, offset_kb, [P, GDN_V, P])

        key_rows = sb("key_rows", 64, [P, TT, GDN_QK * P])
        w_t = [heads(f"w_transposed_{m}", 80 + 4 * m) for m in range(2)]
        k_dec = [heads(f"keys_decayed_{m}", 88 + 4 * m) for m in range(2)]
        q_dec = [heads(f"queries_decayed_{m}", 112 + 4 * m) for m in range(2)]
        qk_dec = [heads(f"scores_decayed_{m}", 120 + 4 * m) for m in range(2)]
        cross, inverse, x1, x2, x3, x4 = [heads(n, 160 + 4 * m) for m, n in enumerate(
            ("cross_blocks", "inverse_transposed", "solve_1", "solve_2", "solve_3", "solve_4"))]
        delta_state = heads("delta_state", 184)
        v_new = heads("values_new", 188)
        u_rows = buf_c[:].rearrange("p (t c) (a n) -> p t (c a) n", t=TT, n=P)
        masks = sb("block_masks", 196, [P, 3, P])
        in_block, across_blocks, same_chunk = masks[:, 0], masks[:, 1], masks[:, 2]
        small = sb("gate_columns", 197.5, [P, 8, 32])
        chunk_decay = sb("chunk_decay", 198.5, [P, TT, GDN_V, 2])
        selector = sb("row_selector", 192, [P, 16, P])
        gated_conv = sb("gated_convolution", 198, [P, SEQ])
        gated = sb("gated", 72, [P, SEQ])
        norm_r = sb("norm_reciprocals", 74, [P, SEQ])
        norm_u = sb("norm_mean_squares", 76, [P, SEQ])
        norm_t = sb("norm_newton", 78, [P, SEQ])
        gated_2 = sb("gated_second", 78, [P, SEQ])

        bank = [ctx.enter_context(nc.psum_tensor(f"bank{n}", [P, SEQ], F32)) for n in range(8)]

        def sem(name):
            return ctx.enter_context(nc.semaphore(name))

        w_loaded = [sem("even_slot_loaded"), sem("odd_slot_loaded")]
        w_high = sem("slot_high_done")
        w_split = sem("slot_split")
        w_used = [sem("even_slot_used"), sem("odd_slot_used")]
        bank_full = sem("bank_full")
        fill_full = sem("fill_bank_full")
        act_freed = sem("banks_freed_by_act")
        dve_freed = sem("banks_freed_by_dve")
        x_loaded = [sem(f"x_tile_{tt}_loaded") for tt in range(TT)]
        rows_loaded = sem("norm_rows_loaded")
        rows_ready = sem("token_tile_normalised")
        out_rows = sem("output_tile_normalised")
        sumsq = sem("sum_of_squares")
        xt_high = sem("xt_high_done")
        dve_step = sem("dve_own_step")
        act_step = sem("act_own_step")
        pool_step = sem("pool_own_step")
        consts = sem("constants_ready")
        gated_raw = sem("gated_raw_done")
        gated_high = sem("gated_high_done")
        gated_low = sem("gated_low_done")
        h_high = sem("hidden_high_done")
        h_low = sem("hidden_low_done")
        stored = sem("stored")
        mixer_loaded = sem("mixer_vectors_loaded")
        small_split = sem("small_weights_split")
        small_full = sem("small_logits_full")
        squares_done = sem("squares_done")
        squares_used = sem("squares_used")
        root_in = sem("root_wanted")
        root_out = sem("root_done")
        rows_r = sem("norm_rows_done")
        fox = {n: sem("fox_" + n) for n in (
            "consts", "logits", "log", "cum_in", "cum_full", "cum_rows", "norm_full", "qk_ready", "scores",
            "exps", "normed", "max", "turned", "turned_used", "out_full")}

        diff = {n: sem("attn_" + n) for n in (
            "selector", "lam_in", "lam_out", "scores", "max", "exps", "mixed", "turned", "turned_used", "out_full",
            "out_taken", "spread")}

        gla = {n: sem("gla_" + n) for n in (
            "low", "low_turned", "low_rows", "gates", "abs", "log", "sums", "decays", "keys", "keys_turned", "keys_rows",
            "inner_full", "inner", "out_full", "out_taken", "update", "state", "spread")}

        gdn = {n: sem("gdn_" + n) for n in (
            "silu", "logits", "logs", "g", "sums", "columns", "exps", "factors", "spread", "qk_ready", "keys_full",
            "keys_rows", "values_full", "values_rows", "selector", "norm_spread")}
        solve = {n: [sem(f"gdn_{n}_{g}") for g in range(2)] for n in (
            "build_full", "differences", "decays", "lower", "late", "full", "act", "dve", "kbg", "ws", "v_new", "update",
            "state", "out_full", "out_free")}

        def solved(eng, g, tt, n, also=("act", "dve")):
            for name, steps in (("act", ACT_STEPS), ("dve", DVE_STEPS)):
                if n in steps and name in also:
                    eng.wait_ge(solve[name][g], len(steps) * tt + steps.index(n) + 1)

        def small_columns(name, layer, c0, n):
            return s_raw[:, :, 0:n], t[name][layer].rearrange("(kt p) n -> p kt n", p=P)[:, :, c0:c0 + n]

        def column(ap):
            return ap.rearrange("(p a) -> p a", a=1)

        def across(ap, times=1):
            return bass.AP(tensor=ap.tensor, offset=ap.offset, ap=[[0, P], [0, times]] + [list(d) for d in ap.ap])

        def prep_loads(st):
            kind, layer = st["layer_kind"], st["layer"]
            if kind == "fox":
                return [small_columns("fox_w_in", layer, 4 * D, FOX_HEADS),
                        (cols[:, 0:1], column(t["fox_q_gain"][layer])),
                        (cols[:, 1:2], column(t["fox_k_gain"][layer])),
                        (vec[:, 0:32].rearrange("p (t n) -> p t n", n=8), across(t["fox_b_f"][layer], TT))]
            if kind == "gla":
                return [small_columns("gla_w_in", 0, 3 * D, GLA_RANK), (up_rows[0:GLA_RANK], t["gla_w_gate_up"][0]),
                        (cols[:, 0:4], t["gla_b_gate"][0].rearrange("(n p) -> p n", p=P)),
                        (cols[:, 4:6], t["gla_o_gain"][0].rearrange("(n p) -> p n", p=P))]
            if kind == "attn":
                return [(rotary[:, m], t["rotary"][m]) for m in range(2)] + [
                    (lam_rows[:, m:m + 1], across(t[f"attn_lambda_{n}_2"][0]))
                    for m, n in enumerate(("q1", "k1", "q2", "k2"))] + [(cols[:, 0:1], column(t["attn_subln_g_2"][0]))]
            if kind == "conv":
                return [(cols[:, 8 * k:8 * k + 8], t["conv_w_2"][0][k].rearrange("(n p) -> p n", p=P))
                        for k in range(3)]
            if kind == "gdn":
                return [small_columns("gdn_w_in", 0, 3 * D, 2 * GDN_V)] + [
                    (cols[:, 16 * k:16 * k + 16], t["gdn_conv_w"][0][k].rearrange("(n p) -> p n", p=P))
                    for k in range(4)] + [
                    (vec[:, 32 * m:32 * m + 32].rearrange("p (t n) -> p t n", n=GDN_V), across(t[name][0], TT))
                    for m, name in enumerate(("gdn_a_log", "gdn_dt_bias"))] + [
                    (cols[:, 64:65], column(t["gdn_o_gain"][0])),
                    (masks[:], t["block_masks"].rearrange("m p n -> p m n"))]

        def gated_tile(st, h):
            if st["kind"] == "project":
                return gated_conv
            return gated if st["kind"] == "fox" or h % 2 == 0 else gated_2

        def wait_all(eng, *needs):
            for _, v in needs:
                if not isinstance(v, int):
                    eng.compute_val(v)
            eng.wait_ge(consts, N_CONSTS)
            for s, v in needs:
                eng.wait_ge(s, v)

        def wait_bank(eng, st, j, b):
            if b < 3:
                eng.wait_ge(bank_full, st["full"] + 3 * j + b + 1)
            else:
                eng.wait_ge(w_used[1], st["pair"] + (3 * j + 3 if st["kind"] == "ffn_down" else j + 1))

        block = ctx.enter_context(nc.Block())

        @block.sync
        def _(sp):
            for tt in range(TT):
                sp.dma_start(x[:, tt], t["x"][0, tt * P:tt * P + P]).then_inc(x_loaded[tt], 16)

            def load_slot(pair, odd, parts):
                if not (isinstance(pair, int) and pair == 0):
                    sp.wait_ge(w_split, 2 * pair - 1 + odd)
                for dst, src in parts:
                    sp.dma_start(raw[:, odd][dst], src).then_inc(w_loaded[odd], 16)

            for st in stages:
                if st["kind"] == "project":
                    w = t[st["weights"]][st["layer"]].rearrange("(kt p) n -> p kt n", p=P)

                    def panel(pair, col):
                        for odd in range(2):
                            load_slot(pair, odd, [
                                ((slice(None), slice(2 * m, 2 * m + 2)),
                                 w[:, HALF * odd + 2 * m:HALF * odd + 2 * m + 2, col])
                                for m in range(2)])

                    panel(st["pair"], slice(st["col"], st["col"] + COLS))
                    if st["panels"] > 2:
                        with sp.Fori(1, st["panels"]) as j:
                            panel(st["pair"] + j, bass.ds(st["col"] + COLS * j, COLS))
                    else:
                        panel(st["pair"] + 1, slice(st["col"] + COLS, st["col"] + 2 * COLS))
                if st["kind"] == "ffn_up":
                    half = COLS // 2
                    ws = [t[n][st["layer"]].rearrange("(kt p) n -> p kt n", p=P) for n in ("ffn_w_gate_2", "ffn_w_up_2")]

                    def up_panel(pair, col):
                        for odd in range(2):
                            load_slot(pair, odd, [
                                ((slice(None), slice(None), slice(half * m, half * m + half)),
                                 ws[m][:, HALF * odd:HALF * odd + HALF, col]) for m in range(2)])

                    up_panel(st["pair"], slice(0, half))
                    with sp.Fori(1, 11) as j:
                        up_panel(st["pair"] + j, bass.ds(half * j, half))
                if st["kind"] == "ffn_down":
                    w = t["ffn_w_down_2"][st["layer"]].rearrange("(kt p) n -> p kt n", p=P)
                    for chunk in range(2):
                        for slot in range(6):
                            k0 = HALF * slot
                            k = min(HALF, FT - k0) // 2
                            load_slot(st["pair"] + 3 * chunk + slot // 2, slot % 2, [
                                ((slice(None), slice(k * m, k * m + k)),
                                 w[:, k0 + k * m:k0 + k * m + k, COLS * chunk:COLS * chunk + COLS])
                                for m in range(2)])
                if st["kind"] == "last_norm":
                    for tt in range(TT):
                        sp.wait_ge(out_rows, tt + 1)
                        sp.dma_start(out[0].rearrange("(t p) d -> p t d", p=P)[:, tt], x[:, tt]).then_inc(stored, 16)
                    sp.wait_ge(stored, 16 * TT)

        @block.gpsimd
        def _(pool):
            pool.memset(ident[:], 0.0).then_inc(pool_step, 1)
            pool.memset(mask_b[:], 0.0).then_inc(pool_step, 1)
            pool.memset(mask2_b[:], 0.0).then_inc(pool_step, 1)
            pool.memset(tri[:], 1.0).then_inc(pool_step, 1)
            pool.memset(pick[:], 0.0).then_inc(pool_step, 1)
            pool.memset(ones[:], 1.0).then_inc(consts, 1)
            pool.wait_ge(pool_step, 5)
            pool.affine_select(out=ident[:], in_=ident[:], compare_op=ALU.not_equal, fill=1.0, base=0,
                               pattern=[[-1, P]], channel_multiplier=1).then_inc(consts, 1)
            pool.affine_select(out=mask_b[:], in_=mask_b[:], compare_op=ALU.is_ge, fill=NEG, base=0,
                               pattern=[[-1, P]], channel_multiplier=1).then_inc(consts, 1)
            pool.affine_select(out=mask2_b[0:CHUNK], in_=mask2_b[0:CHUNK], compare_op=ALU.is_ge, fill=NEG,
                               base=CHUNK - 1, pattern=[[-1, P]], channel_multiplier=0).then_inc(consts, 1)
            pool.affine_select(out=tri[:], in_=tri[:], compare_op=ALU.is_ge, fill=0.0, base=0,
                               pattern=[[1, P]], channel_multiplier=-1).then_inc(consts, 1)
            pool.wait_ge(consts, 5)
            pool.tensor_copy(ident_b[:], ident[:]).then_inc(consts, 1)
            pool.memset(pick[:, 15:16], 1.0).then_inc(consts, 1)
            pool.tensor_copy(chunk_tri[:], tri[:]).then_inc(pool_step, 1)
            pool.wait_ge(pool_step, 6)
            pool.memset(chunk_tri[0:CHUNK, CHUNK:], 0.0).then_inc(consts, 1)

            def split(pair, odd):
                pool.wait_ge(w_high, 2 * pair + odd + 1)
                pool.tensor_tensor(w_lo[:, odd], raw[:, odd], w_hi[:, odd].bitcast(F32), ALU.subtract)\
                    .then_inc(w_split, 1)

            for odd in range(2):
                split(0, odd)
            with pool.Fori(1, n_pairs) as n:
                for odd in range(2):
                    split(n, odd)

        @block.tensor
        def _(pe):
            pe.wait_ge(consts, N_CONSTS)

            def all_free(st):
                for s, n in ((act_freed, st["act"]), (dve_freed, st["dve"])):
                    if n:
                        pe.wait_ge(s, n)

            def three(out_ap, left, right, first, last):
                lh, ll = left
                rh, rl = right
                pe.matmul(out_ap, lh, rh, start=first, stop=False)
                pe.matmul(out_ap, lh, rl, start=False, stop=False)
                return pe.matmul(out_ap, ll, rh, start=False, stop=last)

            def side(st, name, four):
                last, nth = bank[4 * four + 3], st["nth_layer"]
                if name.endswith("logits"):
                    kind = name.split()[0]
                    n, (s, v) = {"fox": (FOX_HEADS, (fox["logits"], nth + 1)), "gla": (GLA_RANK, (gla["low"], 1)),
                                 "gdn": (2 * GDN_V, (gdn["logits"], 1))}[kind]
                    small_logits(st, n, last)
                    if kind == "gla":
                        pe.wait_ge(gla["low"], 1)
                        for tt in range(TT):
                            ins = pe.transpose(bank[4 * four + 2][0:GLA_RANK, tt * P:tt * P + P],
                                               vec[:, tt * GLA_RANK:(tt + 1) * GLA_RANK], ident[:])
                        ins.then_inc(gla["low_turned"], 1)
                        return {2: (gla["low_rows"], 1)}
                    return {3: (s, v)}
                if name == "fox sums":
                    pe.wait_ge(fox["cum_in"], nth + 1)
                    for jt in range(TT):
                        for tt in range(jt + 1):
                            ins = pe.matmul(last[0:8, jt * P:jt * P + P], logf[:, 8 * tt:8 * tt + 8],
                                            (tri if tt == jt else ones)[:], start=tt == 0, stop=tt == jt)
                    ins.then_inc(fox["cum_full"], 1)
                    return {3: (fox["cum_rows"], nth + 1)}
                if name.startswith("gla gate"):
                    h = int(name[-1])
                    pe.wait_ge(gla["low_rows"], 1)
                    pe.matmul(last[:], up_rows[0:GLA_RANK, h * P:h * P + P], low_rank[0:GLA_RANK],
                              start=True, stop=True).then_inc(gla["gates"], 1)
                    return {3: (gla["abs"], h + 1)}
                if name == "gdn sums":
                    columns = bank[4 * four + 2]
                    pe.wait_ge(gdn["g"], 1)
                    pe.matmul(columns[:, 0:32], chunk_tri[:], small[:, 0], start=True, stop=True)
                    pe.matmul(columns[:, 32:64], same_chunk, small[:, 0], start=True, stop=True)
                    for tt in range(TT):
                        ins = pe.matmul(last[0:GDN_V, tt * P:tt * P + P], small[:, 0, tt * GDN_V:(tt + 1) * GDN_V],
                                        chunk_tri[:], start=True, stop=True)
                    ins.then_inc(gdn["sums"], 1)
                    return {2: (gdn["columns"], 1)}

            def panel(pair, four, hi, lo, rows, wait_set, begin=dict, halves=1):
                n = SEQ // halves
                for half in range(halves):
                    tokens = slice(half * n, half * n + n)
                    for odd in range(2):
                        if half == 0:
                            pe.wait_ge(w_split, 2 * pair + odd + 1)
                        wait_set(odd, half)
                        taken = begin() if odd == 0 else {}
                        for b in range(4):
                            if b in taken:
                                pe.wait_ge(*taken[b])
                            for k in range(HALF):
                                kt = HALF * odd + k
                                act_side = [v[:, kt, b * P:b * P + P] if rows else v[:, kt, tokens] for v in (hi, lo)]
                                w_side = [v[:, odd, k] if rows else v[:, odd, k, b * P:b * P + P] for v in (w_hi, w_lo)]
                                ins = three(bank[4 * four + b][:, tokens], *((act_side, w_side) if rows else (w_side, act_side)),
                                            odd == 0 and k == 0, odd == 1 and k == HALF - 1)
                            if half == halves - 1 and odd == 1 and b < 3:
                                ins.then_inc(bank_full, 1)
                        if half == halves - 1:
                            ins.then_inc(w_used[odd], 1)

            def panels(st, hi, lo, rows):
                n = st["panels"]
                filled = st["after_fill"]
                per_act, per_dve = st["n_act"] // n, st["n_dve"] // n

                def set_is_free(j, odd, half):
                    first = isinstance(j, int) and j == 0
                    if hi is g_hi and first:
                        pe.wait_ge(gated_low, st["gated"] - (1 - odd) * HALF)
                    if odd:
                        return
                    if first and filled:
                        pe.wait_ge(dve_freed, st["dve"] - 4 * (1 - half))
                        if half == 0 and st["act"]:
                            pe.wait_ge(act_freed, st["act"])
                        return
                    if isinstance(j, int) and j < 2:
                        for s, v in ((act_freed, (st["free0"][0], st["act"])[j]), (dve_freed, (st["free0"][1], st["dve"])[j])):
                            if v:
                                pe.wait_ge(s, v)
                        return
                    if per_act:
                        pe.wait_ge(act_freed, st["act"] + per_act * (j - 1))
                    if per_dve:
                        pe.wait_ge(dve_freed, st["dve"] + per_dve * (j - 1))

                def one(j, four):
                    sides = st.get("sides", ())
                    begin = dict
                    if isinstance(j, int) and j < len(sides) and sides[j]:
                        begin = lambda: side(st, sides[j], four)
                    panel(st["pair"] + j, four, hi, lo, rows, lambda odd, half: set_is_free(j, odd, half), begin,
                          2 if filled and isinstance(j, int) and j == 0 else 1)

                one(0, 0)
                one(1, 1)
                if n == 4:
                    one(2, 0)
                    one(3, 1)
                elif n > 4:
                    with pe.Fori(1, n // 2) as i:
                        for j in range(2):
                            one(2 * i + j, j)
                    if n % 2:
                        one(n - 1, 0)

            def small_logits(st, n, dst):
                pe.wait_ge(small_split, st["small"])
                for tt in range(TT):
                    for kt in range(KT):
                        ins = three(dst[:, tt * n:tt * n + n],
                                    [v[:, kt, tt * P:tt * P + P] for v in (xt_hi, xt_lo)],
                                    [v[:, kt, 0:n] for v in (s_hi, s_lo)], kt == 0, kt == KT - 1)
                ins.then_inc(small_full, 1)

            def norm_sums(st, rows, n_rows, dst, base=0, norm=0):
                for k, row in enumerate(rows):
                    pe.wait_ge(squares_done, st["squares"] + base + k + 1)
                    ins = pe.matmul(dst[0:n_rows], pick[:, 15 - row:15 - row + n_rows], squares[:, k % 2],
                                    start=k == 0, stop=k == len(rows) - 1)
                    ins.then_inc(squares_used, 1)

            def spread(st, n, counter, freed, n_rows, dst):
                if n >= 4:
                    pe.wait_ge(gated_raw, st["gated"] + freed(n))
                pe.matmul(dst[:], selector[0:n_rows, n], norm_r[0:n_rows], start=True, stop=True).then_inc(counter, 1)

            for st in stages:
                kind, nth = st["kind"], st["nth"]
                if kind == "fill":
                    all_free(st)
                    src = xn if st["norm"] == "rms" else x
                    for tt in range(TT):
                        pe.wait_ge(rows_ready, TT * nth + tt + 1)
                        for g in range(2):
                            for k in range(4):
                                kt = 4 * g + k
                                ins = pe.transpose(bank[2 * tt + g][:, k * P:k * P + P],
                                                   src[:, tt, kt * P:kt * P + P], ident[:])
                            ins.then_inc(fill_full, 1)
                if kind == "project":
                    if st["to"] == "residual":
                        panels(st, g_hi, g_lo, True)
                    else:
                        panels(st, xt_hi, xt_lo, st["rows"])
                if kind == "ffn_up":
                    panels(st, xt_hi, xt_lo, False)
                if kind == "ffn_down":
                    for chunk in range(2):
                        four = (1 + chunk) % 2
                        for slot in range(6):
                            odd, pair = slot % 2, st["pair"] + 3 * chunk + slot // 2
                            k0 = HALF * slot
                            n = min(HALF, FT - k0)
                            pe.wait_ge(w_split, 2 * pair + odd + 1)
                            if slot == 0:
                                if chunk == 0:
                                    pe.wait_ge(act_freed, st["free0"][0])
                                    pe.wait_ge(dve_freed, st["free0"][1])
                                else:
                                    all_free(st)
                            if chunk == 0:
                                pe.wait_ge(h_low, FT * nth + k0 + n)
                            for b in range(4):
                                for k in range(n):
                                    ins = three(bank[4 * four + b][:],
                                                [v[:, k0 + k, b * P:b * P + P] for v in (h_hi, h_lo)],
                                                [v[:, odd, k] for v in (w_hi, w_lo)],
                                                slot == 0 and k == 0, slot == 5 and k == n - 1)
                                if slot == 5 and b < 3:
                                    ins.then_inc(bank_full, 1)
                            ins.then_inc(w_used[odd], 1)
                if kind == "fox":
                    all_free(st)
                    pe.wait_ge(fox["consts"], nth + 1)

                    def spread_norms(h):
                        if h:
                            pe.wait_ge(fox["qk_ready"], 16 * nth + 2 * h)
                        for m in range(2):
                            pe.matmul(bank[m][:], selector[0:16, 8 * m + h], norm_r[0:16], start=True, stop=True)\
                                .then_inc(fox["norm_full"], 1)

                    def scores(n):
                        h, i = divmod(n, TT)
                        pe.wait_ge(fox["qk_ready"], 16 * nth + 2 * h + 2)
                        if n >= 3:
                            pe.wait_ge(fox["exps"], 32 * nth + n - 2)
                        dst, keys = bank[2 + n % 3], (i + 1) * P
                        pe.matmul(dst[:, 0:keys], q_n[:, h % 2, i * P:i * P + P], k_n[:, h % 2, 0:keys],
                                  start=True, stop=False)
                        pe.matmul(dst[:, 0:keys], selector[0:8, h], cum_rows[0:8, 0:keys], start=False, stop=False)
                        pe.matmul(dst[:, i * P:keys], ident_b[:], mask_b[:], start=False, stop=True)\
                            .then_inc(fox["scores"], 1)

                    def turn(n):
                        h, i = divmod(n, TT)
                        pe.wait_ge(fox["normed"], 32 * nth + n + 1)
                        if n >= 2:
                            pe.wait_ge(fox["turned_used"], 32 * nth + n - 1)
                        for k in range(i + 1):
                            ins = pe.transpose(bank[5 + n % 2][:, k * P:k * P + P], probs[:, n % 2, k * P:k * P + P],
                                               ident[:])
                        ins.then_inc(fox["turned"], 1)

                    def weigh(h):
                        pe.wait_ge(fox["turned_used"], 32 * nth + TT * (h + 1))
                        if h:
                            pe.wait_ge(gated_raw, st["gated"] + h)
                        for k in range(TT):
                            ins = pe.matmul(bank[7][:, k * P:], c_rows[:, k, h * P:h * P + P],
                                            probs_t[:, h % 2, k, k * P:], start=k == 0, stop=k == TT - 1)
                        ins.then_inc(fox["out_full"], 1)

                    pe.wait_ge(fox["cum_rows"], nth + 1)
                    norm_sums(st, [8 * m + h for h in range(FOX_HEADS) for m in range(2)], 16, bank[2])
                    pe.wait_ge(rows_r, st["norms"] + 1)
                    spread_norms(0)
                    n_all = FOX_HEADS * TT
                    scores(0)
                    scores(1)
                    for n in range(n_all):
                        if n % TT == 0 and n // TT + 1 < FOX_HEADS:
                            spread_norms(n // TT + 1)
                        if n + 2 < n_all:
                            scores(n + 2)
                        turn(n)
                        if n % TT == 1 and n > TT:
                            weigh(n // TT - 1)
                    weigh(FOX_HEADS - 1)

                if kind == "attn":
                    all_free(st)

                    def pair_scores(n):
                        h, i = divmod(n, TT)
                        if n >= 3:
                            pe.wait_ge(diff["exps"], 2 * n - 4)
                        keys = (i + 1) * P
                        for c in range(2):
                            dst, rows = bank[2 * (n % 3) + c], slice(CHUNK * c, CHUNK * c + CHUNK)
                            pe.matmul(dst[:, 0:keys], buf_a[rows, h, i * P:i * P + P], buf_b[rows, h, 0:keys],
                                      start=True, stop=False)
                            pe.matmul(dst[:, i * P:keys], ident_b[:], mask2_b[:], start=False, stop=True)\
                                .then_inc(diff["scores"], 1)

                    def turn_pair(n):
                        i = n % TT
                        pe.wait_ge(diff["mixed"], n + 1)
                        if n:
                            pe.wait_ge(diff["turned_used"], n)
                        for k in range(i + 1):
                            ins = pe.transpose(bank[6][:, k * P:k * P + P],
                                               pair_probs[:, n % 2, 0, k * P:k * P + P], ident[:])
                        ins.then_inc(diff["turned"], 1)

                    def weigh_values(h):
                        pe.wait_ge(diff["turned_used"], TT * (h + 1))
                        if h:
                            pe.wait_ge(diff["out_taken"], h)
                        for k in range(TT):
                            ins = pe.matmul(bank[7][:, k * P:], c_rows[:, k, h * P:h * P + P],
                                            probs_t[:, h % 2, k, k * P:], start=k == 0, stop=k == TT - 1)
                        ins.then_inc(diff["out_full"], 1)

                    n_all = ATTN_HEADS * TT
                    pair_scores(0)
                    pair_scores(1)
                    for n in range(n_all):
                        if n + 2 < n_all:
                            pair_scores(n + 2)
                        turn_pair(n)
                        if n % TT == 1 and n > TT:
                            weigh_values(n // TT - 1)
                    weigh_values(ATTN_HEADS - 1)
                    norm_sums(st, list(range(8)), 8, bank[2])
                    pe.wait_ge(diff["selector"], 1)
                    pe.wait_ge(rows_r, st["norms"] + 1)
                    for h in range(ATTN_HEADS):
                        spread(st, h, diff["spread"], lambda n: n - 3, 8, bank[4 + h % 4])
                if kind == "gla":
                    all_free(st)
                    pe.wait_ge(gla["keys"], GLA_HEADS)
                    for tt in range(TT):
                        if tt >= 2:
                            pe.wait_ge(gla["keys_rows"], tt - 1)
                        for h in range(GLA_HEADS):
                            ins = pe.transpose(bank[tt % 2][:, h * P:h * P + P], buf_a[:, 4 + h, tt * P:tt * P + P],
                                               ident[:])
                        ins.then_inc(gla["keys_turned"], 1)

                    def inside(tt):
                        if tt >= 2:
                            pe.wait_ge(gla["inner"], tt - 1)
                        for h in range(GLA_HEADS):
                            ins = pe.matmul(bank[2 + tt % 2][:, h * P:h * P + P], buf_b[:, 4 + h, tt * P:tt * P + P],
                                            buf_b[:, h, tt * P:tt * P + P], start=True, stop=True)
                        ins.then_inc(gla["inner_full"], 1)

                    inside(0)
                    pe.wait_ge(gla["keys_rows"], TT)
                    for tt in range(TT):
                        if tt + 1 < TT:
                            inside(tt + 1)
                        pe.wait_ge(gla["inner"], tt + 1)
                        if tt:
                            pe.wait_ge(gla["out_taken"], 2 * tt)
                        for h in range(GLA_HEADS):
                            for m in range(2):
                                at = (h % 2) * 256 + m * P
                                pe.matmul(bank[4 + h // 2][:, at:at + P],
                                          c_rows[:, tt, h * 256 + m * P:h * 256 + m * P + P], inner[:, tt % 2, h],
                                          start=h % 2 == 0 and m == 0, stop=False, skip_group_check=True)
                        for half in range(2):
                            c = 2 * tt + half
                            rows = slice(CHUNK * half, CHUNK * half + CHUNK)
                            if c:
                                pe.wait_ge(gla["state"], c)
                            for h in range(GLA_HEADS if c else 0):
                                for m in range(2):
                                    at = (h % 2) * 256 + m * P + CHUNK * half
                                    ins = pe.matmul(bank[4 + h // 2][:, at:at + CHUNK],
                                                    gla_state[:, c % 2, h * 256 + m * P:h * 256 + m * P + P],
                                                    buf_b[:, h, CHUNK * c:CHUNK * c + CHUNK],
                                                    start=False, stop=half == 1 and h % 2 == 1 and m == 1,
                                                    skip_group_check=True)
                                if half == 1 and h % 2 == 1:
                                    ins.then_inc(gla["out_full"], 1)
                            if c < 7:
                                for h in range(GLA_HEADS):
                                    ins = pe.matmul(bank[6 + h // 2][:, (h % 2) * 256:(h % 2) * 256 + 256],
                                                    k_rows[rows, tt, h * P:h * P + P],
                                                    c_rows[rows, tt, h * 256:h * 256 + 256], start=True, stop=True)
                                    if h % 2:
                                        ins.then_inc(gla["update"], 1)
                    norm_sums(st, [n // 2 for n in range(8)], GLA_HEADS, bank[0])
                    pe.wait_ge(gla["state"], 8)
                    pe.wait_ge(rows_r, st["norms"] + 1)
                    for h in range(GLA_HEADS):
                        spread(st, h, gla["spread"], None, GLA_HEADS, bank[4 + h])
                if kind == "gdn":
                    all_free(st)
                    pe.wait_ge(gdn["silu"], 16)
                    norm_sums(st, list(range(8)), 8, bank[1])
                    pe.wait_ge(rows_r, st["norms"] + 1)
                    for n in range(8):
                        if n >= 2:
                            pe.wait_ge(gdn["qk_ready"], n - 1)
                        pe.matmul(bank[4 + n % 2][:], selector[0:8, n], norm_r[0:8], start=True, stop=True)\
                            .then_inc(gdn["spread"], 1)
                    pe.wait_ge(gdn["qk_ready"], 8)
                    for tt in range(TT):
                        if tt >= 2:
                            pe.wait_ge(gdn["keys_rows"], tt - 1)
                        for h in range(GDN_QK):
                            ins = pe.transpose(bank[6 + tt % 2][:, h * P:h * P + P],
                                               buf_a[:, GDN_QK + h, tt * P:tt * P + P], ident[:])
                        ins.then_inc(gdn["keys_full"], 1)
                    for n in range(2 * TT):
                        tt, g = divmod(n, 2)
                        if n >= 2:
                            pe.wait_ge(gdn["values_rows"], n - 1)
                        for i in range(4):
                            ins = pe.transpose(bank[4 + g][:, i * P:i * P + P],
                                               buf_b[:, 4 * g + i, tt * P:tt * P + P], ident[:])
                        ins.then_inc(gdn["values_full"], 1)
                    pe.wait_ge(gdn["factors"], 1)

                    def build(tt, g):
                        if tt:
                            solved(pe, g, tt - 1, LAST_STEP - 1)
                            solved(pe, g, tt - 1, LAST_STEP)
                        at = slice(tt * P, tt * P + P)
                        for i in range(4):
                            pe.matmul(bank[2 * g][:, i * P:i * P + P], selector[0:GDN_V, 4 * g + i], cum_rows[0:GDN_V, at],
                                      start=True, stop=True)
                        for i in range(2):
                            k = buf_a[:, GDN_QK + 2 * g + i, at]
                            pe.matmul(bank[2 * g + 1][:, i * P:i * P + P], k, k, start=True, stop=True)
                        for i in range(2):
                            ins = pe.matmul(bank[2 * g + 1][:, (2 + i) * P:(3 + i) * P], buf_a[:, GDN_QK + 2 * g + i, at],
                                            buf_a[:, 2 * g + i, at], start=True, stop=True)
                        ins.then_inc(solve["build_full"][g], 1)

                    def step(g, n, left, right, flip=False):
                        for i in range(4):
                            h, o = 4 * g + i, bank[2 * g + n % 2][:, i * P:i * P + P]
                            ins = pe.transpose(o, left[:, h], ident[:]) if flip else \
                                pe.matmul(o, left[:, h], right[:, h], start=True, stop=True)
                        ins.then_inc(solve["full"][g], 1)

                    def solve_step(tt, g, n):
                        def after(*earlier):
                            for e in earlier:
                                solved(pe, g, tt, e)
                        if n == 1:
                            pe.wait_ge(solve["lower"][g], tt + 1)
                            step(g, n, x1, None, True)
                        if n == 2:
                            after(1)
                            step(g, n, x2, x1)
                        if n == 3:
                            step(g, n, x1, x2)
                        if n == 4:
                            after(2)
                            step(g, n, x3, inverse)
                        if n == 5:
                            after(3)
                            step(g, n, x4, x3)
                        if n == 6:
                            after(4)
                            step(g, n, x3, x4)
                        if n == 7:
                            after(5)
                            step(g, n, x1, inverse)
                        if n == 8:
                            after(6)
                            step(g, n, x2, x1)
                        if n == 9:
                            after(8, 7)
                            step(g, n, x3, inverse)
                        if n == 10:
                            after(9)
                            step(g, n, inverse, cross)
                        if n == 11:
                            step(g, n, cross, inverse)
                        if n == 12:
                            after(10, 11)
                            step(g, n, x1, x4)
                        if n == 13:
                            step(g, n, inverse, None, True)
                        if n == 14:
                            after(12)
                            step(g, n, x3, x2)
                        if n == 15:
                            after(13, 14)
                            step(g, n, x4, x2)
                        if n == 16:
                            after(15)
                            pe.wait_ge(solve["kbg"][g], tt + 1)
                            step(g, n, x3, x1)
                        if n == 17:
                            step(g, n, x1, u_rows[:, tt])

                    def read_state(c, g):
                        tt, rows = c // 2, slice(CHUNK * (c % 2), CHUNK * (c % 2) + CHUNK)
                        solved(pe, g, tt, 16)
                        if c == 0:
                            pe.wait_ge(gdn["selector"], 1)
                        else:
                            pe.wait_ge(solve["state"][g], c)
                        for i in range(4):
                            ins = pe.matmul(bank[4 + g][:, i * P:i * P + P], w_t[tt % 2][:, 4 * g + i],
                                            delta_state[:, 4 * g + i], start=True, stop=True)
                        ins.then_inc(solve["ws"][g], 1)
                        pe.wait_ge(solve["late"][g], tt + 1)
                        if c % 2 == 0 and tt:
                            pe.wait_ge(solve["out_free"][g], tt)
                        for i in range(4):
                            pe.matmul(bank[6 + g][:, i * P + rows.start:i * P + rows.stop], delta_state[:, 4 * g + i],
                                      q_dec[tt % 2][:, 4 * g + i, rows], start=c % 2 == 0 and i == 0, stop=False,
                                      skip_group_check=True)

                    def write_state(c, g):
                        tt, rows = c // 2, slice(CHUNK * (c % 2), CHUNK * (c % 2) + CHUNK)
                        pe.wait_ge(solve["v_new"][g], c + 1)
                        if c < 2 * TT - 1:
                            for i in range(4):
                                ins = pe.matmul(bank[4 + g][:, i * P:i * P + P], k_dec[tt % 2][rows, 4 * g + i],
                                                v_new[rows, 4 * g + i], start=True, stop=True)
                            ins.then_inc(solve["update"][g], 1)
                        for i in range(4):
                            ins = pe.matmul(bank[6 + g][:, i * P + rows.start:i * P + rows.stop], v_new[rows, 4 * g + i],
                                            qk_dec[tt % 2][rows, 4 * g + i, rows], start=False,
                                            stop=c % 2 == 1 and i == 3, skip_group_check=True)
                        if c % 2:
                            ins.then_inc(solve["out_full"][g], 1)

                    for tt, g, turn in staggered():
                        if tt < TT and turn == 0:
                            build(tt, g)
                        if tt < TT and turn >= BUILD_TURNS:
                            solve_step(tt, g, turn - BUILD_TURNS + 1)
                        if tt and turn in RECURRENCE_TURNS:
                            part = RECURRENCE_TURNS.index(turn)
                            (write_state if part % 2 else read_state)(2 * (tt - 1) + part // 2, g)
                    norm_sums(st, list(range(8)), 8, bank[0], base=8)
                    pe.wait_ge(rows_r, st["norms"] + 2)
                    for h in range(GDN_V):
                        spread(st, h, gdn["norm_spread"], lambda n: n - 3, 8, bank[4 + h % 4])
        @block.scalar
        def _(act):
            steps = [0]

            def link(ins):
                steps[0] += 1
                ins.then_inc(act_step, 1)
                act.wait_ge(act_step, steps[0])

            def load_norm(norm, which):
                vectors = [(norm_w, "norm_w")] if norm == "rms" else [(norm_w, norm + "_g_2"), (norm_b, norm + "_b_2")]
                for dst, name in vectors:
                    act.dma_start(dst[:], across(t[name][which])).then_inc(rows_loaded, 16)

            def load_vectors(st):
                if st["gated"]:
                    act.wait_ge(gated_low, st["gated"])
                for dst, src in prep_loads(st):
                    with nc.allow_non_contiguous_dma(reason="a few kilobytes of small vectors"):
                        act.dma_start(dst, src).then_inc(mixer_loaded, 16)

            def weights_high(pair, odd):
                if isinstance(pair, int) and pair >= n_pairs:
                    return
                used = [] if isinstance(pair, int) and pair == 0 else [(w_used[odd], pair)]
                wait_all(act, (w_loaded[odd], 32 * (pair + 1)), *used)
                act.activation(w_hi[:, odd], raw[:, odd], ACT.Copy).then_inc(w_high, 1)

            def high(st, h):
                if st["kind"] == "project":
                    act.wait_ge(dve_freed, st["dve"] + h + 1)
                else:
                    act.wait_ge(gated_raw, st["gated"] + h + 1)
                act.activation(g_hi[:, h], gated_tile(st, h)[:], ACT.Copy).then_inc(gated_high, 1)

            def root(st, n, ap):
                act.wait_ge(root_in, st["roots"] + n + 1)
                act.activation(ap, ap, ACT.Sqrt).then_inc(root_out, 1)

            def square_tiles(st, tiles, base=0):
                for k, src in enumerate(tiles):
                    n = st["squares"] + base + k
                    if k >= 2:
                        act.wait_ge(squares_used, n - 1)
                    o = squares[:, k % 2] if len(src.shape) == 2 else \
                        squares[:, k % 2].rearrange("p (t n) -> p t n", t=TT)
                    act.activation(o, src, ACT.Square).then_inc(squares_done, 1)

            def behind(st, n):
                if st["to"] == "gate G":
                    high(st, n)
                else:
                    act.wait_ge(dve_freed, st["dve"] + n + 1)
                    dst = buf_a[:, n] if n < 8 else buf_b[:, n - 8]
                    act.activation(dst, dst, ACT.Silu).then_inc(gdn["silu"], 1)

            def side(st, name):
                nth = st["nth_layer"]
                if name == "fox logits":
                    act.wait_ge(fox["logits"], nth + 1)
                    link(act.activation(logf_e[:], logf_e[:], ACT.Exp, scale=-1.0))
                    act.activation(logf_e[:], logf_e[:], ACT.Ln, bias=1.0).then_inc(fox["log"], 1)
                if name.startswith("gla gate"):
                    h = int(name[-1])
                    act.wait_ge(gla["abs"], h + 1)
                    link(act.activation(gate_abs[:, h % 2], gate_abs[:, h % 2], ACT.Exp, scale=-1.0))
                    act.activation(gate_abs[:, h % 2], gate_abs[:, h % 2], ACT.Ln, bias=1.0).then_inc(gla["log"], 1)
                    act.wait_ge(gla["sums"], h + 1)
                    act.activation(decayed[:, h], gate_log[:, h % 2], ACT.Exp, scale=1 / 16.0)\
                        .then_inc(gla["decays"], 1)
                    act.activation(grown[:, h], gate_log[:, h % 2], ACT.Exp, scale=-1 / 16.0)\
                        .then_inc(gla["decays"], 1)
                if name == "gdn logits":
                    act.wait_ge(gdn["logits"], 1)
                    link(act.activation(small[:, 1], small[:, 1], ACT.Exp, scale=-1.0))
                    act.activation(small[:, 1], small[:, 1], ACT.Ln, bias=1.0).then_inc(gdn["logs"], 1)
                    act.activation(vec[:, 0:32], vec[:, 0:32], ACT.Exp).then_inc(gdn["logs"], 1)
                    act.activation(small[:, 5], small[:, 5], ACT.Sigmoid).then_inc(gdn["logs"], 1)
                if name == "gdn sums":
                    act.wait_ge(gdn["columns"], 1)
                    act.activation(small[:, 4], small[:, 2], ACT.Exp).then_inc(gdn["exps"], 1)
                    act.activation(small[:, 3], small[:, 3], ACT.Exp).then_inc(gdn["exps"], 1)

            for odd in range(2):
                weights_high(0, odd)
            for st in stages:
                kind, nth = st["kind"], st["nth"]
                if kind == "last_norm":
                    load_norm("ln2", st["layer"])
                    for tt in range(TT):
                        root(st, tt, stat[:, 12 + tt:13 + tt])
                if kind == "fill":
                    if nth:
                        act.wait_ge(rows_ready, TT * nth)
                    if st["norm"] != "plain":
                        if st["gated"]:
                            act.wait_ge(gated_low, st["gated"])
                        load_norm(st["norm"], st["which"])
                    def squares_of(tt):
                        if st["norm"] != "rms":
                            return
                        if nth:
                            act.wait_ge(dve_freed, st["dve"] - TT + tt + 1)
                        else:
                            act.wait_ge(x_loaded[tt], 16)
                        act.activation(xn[:, tt], x[:, tt], ACT.Square, accum_out=stat[:, tt:tt + 1]).then_inc(sumsq, 1)

                    def transposed_high(tt):
                        for g in range(2):
                            act.wait_ge(fill_full, 8 * nth + 2 * tt + g + 1)
                            act.activation(xt_hi[:, 4 * g:4 * g + 4, tt * P:tt * P + P],
                                           bank[2 * tt + g][:].rearrange("p (k n) -> p k n", k=4), ACT.Copy)\
                                .then_inc(xt_high, 1)

                    squares_of(0)
                    squares_of(1)
                    for tt in range(TT):
                        if st["norm"] != "plain":
                            root(st, tt, stat[:, 12 + tt:13 + tt])
                        if tt + 2 < TT:
                            squares_of(tt + 2)
                        if tt:
                            transposed_high(tt - 1)
                    transposed_high(TT - 1)
                if kind == "loads":
                    load_vectors(st)
                if kind == "ffn_down":
                    for slot in range(2, 14):
                        weights_high(st["pair"] + slot // 2, slot % 2)
                if kind == "project":
                    func, name = (ACT.Silu if "silu" in st["to"] else ACT.Copy), st["to"].split()[-1]
                    dst = {"A": buf_a, "B": buf_b, "C": buf_c, "D": buf_d}.get(name)
                    for j in range(st["panels"]):
                        if j < len(st["sides"]) and st["sides"][j]:
                            side(st, st["sides"][j])
                        weights_high(st["pair"] + j + 1, 0)
                        for b in range(4):
                            if b == 3:
                                weights_high(st["pair"] + j + 1, 1)
                            if st["to"] in ("conv", "gate G") and b > 0:
                                behind(st, 4 * j + b - 1)
                            if st["by"] != "act":
                                continue
                            wait_bank(act, st, j, b)
                            o = c_rows[:, b, COLS * j:COLS * j + COLS] if st["rows"] else dst[:, 4 * j + b]
                            act.activation(o, bank[4 * (j % 2) + b][:], func).then_inc(act_freed, 1)
                        if st["to"] in ("conv", "gate G"):
                            behind(st, 4 * j + 3)
                if kind == "ffn_up":
                    def up(j, four, first=False):
                        weights_high(st["pair"] + j + 1, 0)
                        for m in range(2):
                            full = (bank_full, st["full"] + 3 * j + m + 1)
                            wait_all(act, full, *([] if first else [(dve_freed, st["dve"] + 2 * j + m - 1)]))
                            act.activation(gate_act[:, m], bank[4 * four + m][:], ACT.Silu).then_inc(act_freed, 1)
                        weights_high(st["pair"] + j + 1, 1)
                        for m in range(2):
                            wait_all(act, (dve_freed, st["dve"] + 2 * j + m + 1))
                            at = 2 * j + m
                            o = h_hi[:, at] if first else h_hi[:, bass.ds(at, 1)].rearrange("p a n -> p (a n)")
                            act.activation(o, hidden[:, m], ACT.Copy).then_inc(h_high, 1)

                    up(0, 0, True)
                    with act.Fori(0, 5) as i:
                        for j in range(2):
                            up(2 * i + j + 1, 1 - j)
                if kind == "fox":
                    act.wait_ge(w_used[1], st["pair"])
                    act.wait_ge(dve_freed, st["dve"])
                    square_tiles(st, [b[:, h] for h in range(FOX_HEADS) for b in (buf_a, buf_b)])
                    root(st, 0, norm_t[0:16])

                    def exponentials(n):
                        i = n % TT
                        act.wait_ge(fox["max"], 32 * nth + n + 1)
                        if n >= 2:
                            act.wait_ge(fox["turned"], 32 * nth + n - 1)
                        keys = (i + 1) * P
                        act.activation(probs[:, n % 2, 0:keys], bank[2 + n % 3][:, 0:keys], ACT.Exp,
                                       bias=soft[:, n % 4:n % 4 + 1], accum_out=soft[:, 4 + n % 4:5 + n % 4])\
                            .then_inc(fox["exps"], 1)

                    def take_turned(n):
                        h, i = divmod(n, TT)
                        act.wait_ge(fox["turned"], 32 * nth + n + 1)
                        if h >= 2 and i == 0:
                            act.wait_ge(fox["out_full"], 8 * nth + h - 1)
                        act.activation(probs_t[:, h % 2, 0:i + 1, i * P:i * P + P],
                                       bank[5 + n % 2][:, 0:(i + 1) * P].rearrange("p (k n) -> p k n", n=P), ACT.Copy)\
                            .then_inc(fox["turned_used"], 1)

                    n_all = FOX_HEADS * TT
                    for n in range(n_all):
                        exponentials(n)
                        if n:
                            take_turned(n - 1)
                        if n % TT == 2 and n > TT:
                            high(st, n // TT - 1)
                    take_turned(n_all - 1)
                    high(st, FOX_HEADS - 1)

                if kind == "attn":
                    act.wait_ge(diff["lam_in"], 1)
                    act.activation(lam_work[:, 0:2], lam_work[:, 0:2], ACT.Exp).then_inc(diff["lam_out"], 1)

                    def pair_exponentials(n):
                        i = n % TT
                        keys = (i + 1) * P
                        for c in range(2):
                            act.wait_ge(diff["max"], 2 * n + c + 1)
                            if n >= 2:
                                act.wait_ge(diff["turned"], n - 1)
                            k = 2 * (n % 2) + c
                            act.activation(pair_probs[:, n % 2, c, 0:keys], bank[2 * (n % 3) + c][:, 0:keys], ACT.Exp,
                                           bias=soft[:, k:k + 1], accum_out=soft[:, 4 + k:5 + k])\
                                .then_inc(diff["exps"], 1)

                    def take_pair(n):
                        h, i = divmod(n, TT)
                        act.wait_ge(diff["turned"], n + 1)
                        if h >= 2 and i == 0:
                            act.wait_ge(diff["out_full"], h - 1)
                        act.activation(probs_t[:, h % 2, 0:i + 1, i * P:i * P + P],
                                       bank[6][:, 0:(i + 1) * P].rearrange("p (k n) -> p k n", n=P), ACT.Copy)\
                            .then_inc(diff["turned_used"], 1)

                    def take_out(h):
                        act.wait_ge(diff["out_full"], h + 1)
                        act.activation(buf_d[:, h], bank[7][:], ACT.Copy).then_inc(diff["out_taken"], 1)

                    n_all = ATTN_HEADS * TT
                    for n in range(n_all):
                        pair_exponentials(n)
                        if n:
                            take_pair(n - 1)
                        if n % TT == 2 and n > TT:
                            take_out(n // TT - 1)
                    take_pair(n_all - 1)
                    take_out(ATTN_HEADS - 1)
                    act.wait_ge(diff["out_taken"], ATTN_HEADS)
                    square_tiles(st, [buf_d[:, h] for h in range(ATTN_HEADS)])
                    root(st, 0, norm_t[0:8])
                    for h in range(ATTN_HEADS):
                        high(st, h)
                if kind == "gla":
                    for tt in range(TT):
                        act.wait_ge(gla["keys_turned"], tt + 1)
                        if tt == 0:
                            act.wait_ge(gla["keys"], GLA_HEADS)
                        act.activation(k_rows[:, tt], bank[tt % 2][:], ACT.Copy).then_inc(gla["keys_rows"], 1)
                    for tt in range(TT):
                        for g in range(2):
                            act.wait_ge(gla["out_full"], 2 * tt + g + 1)
                            act.activation(buf_a[:, 4 * g:4 * g + 4, tt * P:tt * P + P],
                                           bank[4 + g][:].rearrange("p (n l) -> p n l", l=P), ACT.Copy)\
                                .then_inc(gla["out_taken"], 1)
                    act.wait_ge(gla["out_taken"], 2 * TT)
                    square_tiles(st, [buf_a[:, n] for n in range(8)])
                    root(st, 0, norm_t[0:GLA_HEADS])
                    for n in range(8):
                        high(st, n)
                if kind == "gdn":
                    act.wait_ge(w_used[1], st["pair"])
                    square_tiles(st, [buf_a[:, n] for n in range(8)])
                    root(st, 0, norm_t[0:8])
                    for tt in range(TT):
                        act.wait_ge(gdn["keys_full"], tt + 1)
                        act.activation(key_rows[:, tt], bank[6 + tt % 2][:], ACT.Copy).then_inc(gdn["keys_rows"], 1)

                    def decays(tt, g):
                        s, four = solve["decays"][g], slice(4 * g, 4 * g + 4)
                        act.wait_ge(solve["differences"][g], 2 * tt + 1)
                        act.activation(x2[:, four], x2[:, four], ACT.Exp, scale=-1.0).then_inc(s, 1)
                        act.wait_ge(solve["differences"][g], 2 * tt + 2)
                        o = qk_dec[tt % 2][:, four]
                        act.activation(o, o, ACT.Exp).then_inc(s, 1)
                        act.activation(x3[:, four], bank[2 * g][:].rearrange("p (a n) -> p a n", n=P), ACT.Exp)\
                            .then_inc(s, 1)

                    def take_step(tt, g, n):
                        four = slice(4 * g, 4 * g + 4)
                        act.wait_ge(solve["full"][g], LAST_STEP * tt + n)
                        if n == 2:
                            act.wait_ge(solve["late"][g], tt + 1)
                        dst = {1: x2, 2: x3, 3: x4, 5: x1, 6: x2, 8: x3, 10: x4, 11: x1, 12: x3, 13: x4, 15: x1,
                               16: w_t[tt % 2]}[n]
                        act.activation(dst[:, four], bank[2 * g + n % 2][:].rearrange("p (a n) -> p a n", n=P), ACT.Copy)\
                            .then_inc(solve["act"][g], 1)

                    for tt, g, turn in staggered():
                        if tt < TT and turn == 0:
                            decays(tt, g)
                        if tt < TT and turn - BUILD_TURNS + 1 in ACT_STEPS:
                            take_step(tt, g, turn - BUILD_TURNS + 1)
                        if tt and turn == RECURRENCE_TURNS[-1]:
                            act.wait_ge(solve["out_full"][g], tt)
                            act.activation(u_rows[:, tt - 1, 4 * g:4 * g + 4],
                                           bank[6 + g][:].rearrange("p (a n) -> p a n", n=P), ACT.Copy)\
                                .then_inc(solve["out_free"][g], 1)
                    for g in range(2):
                        act.wait_ge(solve["out_free"][g], TT)
                    square_tiles(st, [u_rows[:, :, h] for h in range(GDN_V)], base=8)
                    root(st, 1, norm_t[0:8])
                    for h in range(GDN_V):
                        high(st, h)
        @block.vector
        def _(dve):
            steps = [0]

            def link(ins):
                steps[0] += 1
                ins.then_inc(dve_step, 1)
                dve.wait_ge(dve_step, steps[0])

            def low(st, h):
                dve.wait_ge(gated_high, st["gated"] + h + 1)
                dve.tensor_tensor(g_lo[:, h], gated_tile(st, h)[:], g_hi[:, h].bitcast(F32), ALU.subtract).then_inc(gated_low, 1)

            def newton(u, y, t):
                link(dve.tensor_tensor(t, y, y, ALU.mult))
                link(dve.scalar_tensor_tensor(t, t, -0.5, u, ALU.mult, ALU.mult))
                return dve.scalar_tensor_tensor(y, t, 1.5, y, ALU.add, ALU.mult)

            def rsqrt(st, n, u, root_of, y, t):
                dve.tensor_copy(root_of, u).then_inc(root_in, 1)
                dve.wait_ge(root_out, st["roots"] + n + 1)
                link(dve.reciprocal(y, root_of))
                return newton(u, y, t)

            def norm_rows(st, src, n_rows, count, eps, norm=0, base=0, n_squares=16):
                dve.wait_ge(squares_used, st["squares"] + base + n_squares)
                u, y, t = norm_u[0:n_rows], norm_r[0:n_rows], norm_t[0:n_rows]
                link(dve.tensor_scalar(u, src[0:n_rows], 1.0 / count, eps, ALU.mult, ALU.add))
                rsqrt(st, norm, u, t, y, t).then_inc(rows_r, 1)

            def make_selector(counter, n=16):
                dve.tensor_copy(selector[:, 0:n], ident[:, 0:n].unsqueeze(2).to_broadcast([P, n, P]))\
                    .then_inc(counter, 1)

            def taps(y, u, weights):
                last = len(weights) - 1
                link(dve.tensor_scalar(y, u, weights[last], None, ALU.mult))
                for k in range(last):
                    s = last - k
                    link(dve.scalar_tensor_tensor(y[:, s:], u[:, :SEQ - s], weights[k], y[:, s:], ALU.mult, ALU.add))

            def prep(st):
                dve.wait_ge(mixer_loaded, 16 * st["loads"])
                n = {"fox": FOX_HEADS, "gla": GLA_RANK, "gdn": 2 * GDN_V}.get(st["layer_kind"])
                if n:
                    link(dve.tensor_copy(s_hi[:, :, 0:n], s_raw[:, :, 0:n]))
                    dve.tensor_tensor(s_lo[:, :, 0:n], s_raw[:, :, 0:n], s_hi[:, :, 0:n].bitcast(F32), ALU.subtract)\
                        .then_inc(small_split, 1)
                if st["layer_kind"] == "attn":
                    for m in range(2):
                        link(dve.tensor_tensor(lam_rows[:, 2 * m], lam_rows[:, 2 * m], lam_rows[:, 2 * m + 1], ALU.mult))
                        ins = dve.reduce_sum(lam_work[:, m:m + 1], lam_rows[:, 2 * m], AX)
                        if m == 0:
                            link(ins)
                    ins.then_inc(diff["lam_in"], 1)
                    link(dve.tensor_scalar(cols[:, 1:2], cols[:, 0:1], 1.0 - LAM_INIT, None, ALU.mult))
                if st["layer_kind"] == "fox":
                    link(dve.scalar_tensor_tensor(cols[:, 2:3], cols[:, 0:1], float(P) ** -.5, cols[:, 1:2],
                                                  ALU.mult, ALU.mult))
                    make_selector(fox["consts"])

            def by_tile(ap):
                return ap.rearrange("p (t n) -> p t n", t=TT)

            def side(st, name, four):
                last, nth = bank[4 * four + 3], st["nth_layer"]
                if name == "fox logits":
                    dve.wait_ge(small_full, st["small"])
                    link(dve.tensor_tensor(logf[:], last[:, 0:32], vec[:, 0:32], ALU.add))
                    dve.scalar_tensor_tensor(logf_e[:], logf[:], -1.0, logf[:], ALU.mult, ALU.max)\
                        .then_inc(fox["logits"], 1)
                    link(dve.tensor_scalar(logf[:], logf[:], 0.0, None, ALU.min))
                    dve.wait_ge(fox["log"], nth + 1)
                    dve.tensor_tensor(logf[:], logf_e[:], logf[:], ALU.subtract).then_inc(fox["cum_in"], 1)
                if name == "fox sums":
                    dve.wait_ge(fox["cum_full"], nth + 1)
                    dve.tensor_copy(cum_rows[0:8], last[0:8]).then_inc(fox["cum_rows"], 1)
                if name == "gla logits":
                    dve.wait_ge(small_full, st["small"])
                    dve.tensor_copy(vec[:, 0:64], last[:, 0:64]).then_inc(gla["low"], 1)
                    link(dve.memset(resets[:], 1.0))
                    link(dve.memset(resets[:].rearrange("p (c l) -> p c l", l=CHUNK)[:, :, 0:1], 0.0))
                    dve.wait_ge(gla["low_turned"], 1)
                    dve.tensor_copy(low_rank[0:GLA_RANK], bank[4 * four + 2][0:GLA_RANK]).then_inc(gla["low_rows"], 1)
                if name.startswith("gla gate"):
                    h = int(name[-1])
                    x_, a_ = gate_log[:, h % 2], gate_abs[:, h % 2]
                    dve.wait_ge(gla["gates"], h + 1)
                    if h >= 2:
                        dve.wait_ge(gla["decays"], 2 * h - 2)
                    link(dve.tensor_scalar(x_, last[:], cols[:, h:h + 1], None, ALU.add))
                    dve.scalar_tensor_tensor(a_, x_, -1.0, x_, ALU.mult, ALU.max).then_inc(gla["abs"], 1)
                    dve.wait_ge(gla["abs"], h + 1)
                    link(dve.tensor_scalar(x_, x_, 0.0, None, ALU.min))
                    dve.wait_ge(gla["log"], h + 1)
                    link(dve.tensor_tensor(a_, x_, a_, ALU.subtract))
                    dve.tensor_tensor_scan(x_, resets[:], a_, 0.0, ALU.mult, ALU.add).then_inc(gla["sums"], 1)
                if name == "gdn logits":
                    a, b = [last[:, 0:64].rearrange("p (t m n) -> p m t n", t=TT, m=2)[:, m] for m in range(2)]
                    dve.wait_ge(small_full, st["small"])
                    link(dve.tensor_tensor(by_tile(small[:, 0]), a, by_tile(vec[:, 32:64]), ALU.add))
                    link(dve.tensor_copy(by_tile(small[:, 5]), b))
                    dve.scalar_tensor_tensor(small[:, 1], small[:, 0], -1.0, small[:, 0], ALU.mult, ALU.max)\
                        .then_inc(gdn["logits"], 1)
                    dve.wait_ge(gdn["logs"], 3)
                    link(dve.scalar_tensor_tensor(small[:, 0], small[:, 0], 0.0, small[:, 1], ALU.max, ALU.add))
                    dve.scalar_tensor_tensor(small[:, 0], small[:, 0], -1.0, vec[:, 0:32], ALU.mult, ALU.mult)\
                        .then_inc(gdn["g"], 1)
                    link(dve.tensor_scalar(small[:, 6], small[:, 5], -1.0, None, ALU.mult))
                if name == "gdn sums":
                    columns = bank[4 * four + 2]
                    dve.wait_ge(gdn["sums"], 1)
                    link(dve.tensor_copy(small[:, 2], columns[:, 0:32]))
                    link(dve.tensor_copy(cum_rows[0:GDN_V], last[0:GDN_V]))
                    dve.tensor_tensor(small[:, 3], columns[:, 32:64], small[:, 2], ALU.subtract)\
                        .then_inc(gdn["columns"], 1)
                    dve.wait_ge(gdn["exps"], 2)
                    link(dve.tensor_tensor(small[:, 4], small[:, 4], small[:, 5], ALU.mult))

            norm_loads = 0
            dve.wait_ge(consts, N_CONSTS)
            for st in stages:
                kind, nth = st["kind"], st["nth"]
                if kind in ("fill", "last_norm"):
                    norm = st.get("norm", "ln2")
                    signal, s0 = (rows_ready, TT * nth) if kind == "fill" else (out_rows, 0)
                    if norm != "plain":
                        norm_loads += 1 if norm == "rms" else 2
                        dve.wait_ge(rows_loaded, 16 * norm_loads)
                    def statistics(tt):
                        if norm == "rms":
                            dve.wait_ge(sumsq, TT * st["rms"] + tt + 1)
                            s = stat[:, tt:tt + 1]
                            link(dve.tensor_scalar(s, s, 1.0 / D, RMS_EPS, ALU.mult, ALU.add))
                            dve.tensor_copy(stat[:, 12 + tt:13 + tt], s).then_inc(root_in, 1)
                        if norm in ("ln1", "ln2"):
                            dve.wait_ge(dve_freed, st["dve"] - TT + tt + 1)
                            sums, mv = stat[:, 16:28], soft[:, 2 * tt:2 * tt + 2]
                            for m in range(2):
                                link(dve.bn_stats(sums[:, 6 * m:6 * m + 6], x[:, tt, COLS * m:COLS * m + COLS]))
                            link(dve.bn_aggr(mv, sums))
                            link(dve.tensor_scalar(stat[:, tt:tt + 1], mv[:, 1:2], LN_EPS, None, ALU.add))
                            dve.tensor_copy(stat[:, 12 + tt:13 + tt], stat[:, tt:tt + 1]).then_inc(root_in, 1)

                    def normalise_rows(tt):
                        if norm == "plain":
                            if st["dve"]:
                                dve.wait_ge(dve_freed, st["dve"] - TT + tt + 1)
                            else:
                                dve.wait_ge(x_loaded[tt], 16)
                            dve.tensor_copy(stat[:, 8 + tt:9 + tt], x[:, tt, 0:1]).then_inc(signal, 1)
                            return
                        y, work = stat[:, 8 + tt:9 + tt], stat[:, 4 + tt:5 + tt]
                        dve.wait_ge(root_out, st["roots"] + tt + 1)
                        link(dve.reciprocal(y, stat[:, 12 + tt:13 + tt]))
                        link(newton(stat[:, tt:tt + 1], y, work))
                        if norm == "rms":
                            dve.scalar_tensor_tensor(xn[:, tt], x[:, tt], y, norm_w[:], ALU.mult, ALU.mult)\
                                .then_inc(signal, 1)
                        else:
                            link(dve.scalar_tensor_tensor(x[:, tt], x[:, tt], soft[:, 2 * tt:2 * tt + 1],
                                                          norm_w[:], ALU.subtract, ALU.mult))
                            dve.scalar_tensor_tensor(x[:, tt], x[:, tt], y, norm_b[:], ALU.mult, ALU.add)\
                                .then_inc(signal, 1)

                    def transposed_low(tt):
                        for n in (2 * tt, 2 * tt + 1):
                            g = n % 2
                            dve.wait_ge(xt_high, 8 * nth + n + 1)
                            at = (slice(None), slice(4 * g, 4 * g + 4), slice(tt * P, tt * P + P))
                            dve.tensor_tensor(xt_lo[at], bank[n][:].rearrange("p (k n) -> p k n", k=4),
                                              xt_hi[at].bitcast(F32), ALU.subtract).then_inc(dve_freed, 1)

                    statistics(0)
                    for tt in range(TT):
                        if tt + 1 < TT:
                            statistics(tt + 1)
                        normalise_rows(tt)
                        if kind == "fill" and tt:
                            transposed_low(tt - 1)
                    if kind == "fill":
                        transposed_low(TT - 1)
                if kind == "prep":
                    prep(st)
                if kind in ("project", "ffn_down"):
                    to = st.get("to", "residual")
                    keep = st.get("keep", ALPHA)
                    for j in range(st["panels"]):
                        if j < len(st.get("sides", ())) and st["sides"][j]:
                            side(st, st["sides"][j], j % 2)
                        for b in range(4 if st.get("by", "dve") == "dve" else 0):
                            wait_bank(dve, st, j, b)
                            four = (j + 1) % 2 if kind == "ffn_down" else j % 2
                            src = bank[4 * four + b]
                            n = 4 * j + b
                            if to in ("A", "B", "C"):
                                dst = {"A": buf_a, "B": buf_b, "C": buf_c}[to]
                                o = c_rows[:, b, COLS * j:COLS * j + COLS] if st["rows"] else dst[:, n]
                                dve.tensor_copy(o, src[:]).then_inc(dve_freed, 1)
                            if to == "residual":
                                o = x[:, b, COLS * j:COLS * j + COLS]
                                dve.scalar_tensor_tensor(o, o, keep, src[:], ALU.mult, ALU.add).then_inc(dve_freed, 1)
                            if to.startswith("rotary"):
                                scale = 64 ** -.5 if to[-1] == "A" else 1.0
                                dst = (buf_a if to[-1] == "A" else buf_b)[:, n]
                                dve.tensor_copy(rotary_in[:], src[:]).then_inc(dve_freed, 1)
                                dve.wait_ge(dve_freed, st["dve"] + n + 1)
                                link(dve.stream_shuffle(rotary_sin[:], rotary_in[:], SWAP))
                                link(dve.scalar_tensor_tensor(dst, rotary_in[:], scale, rotary[:, 0], ALU.mult, ALU.mult))
                                link(dve.scalar_tensor_tensor(rotary_sin[:], rotary_sin[:], scale, rotary[:, 1],
                                                              ALU.mult, ALU.mult))
                                link(dve.tensor_tensor(dst, dst, rotary_sin[:], ALU.add))
                            if to == "conv":
                                y = buf_a[:, n] if n < 8 else buf_b[:, n - 8]
                                link(dve.tensor_scalar(y, src[:], cols[:, 48 + n:49 + n], None, ALU.mult))
                                for k in range(3):
                                    s = 3 - k
                                    ins = dve.scalar_tensor_tensor(y[:, s:], src[:, :SEQ - s],
                                                                   cols[:, 16 * k + n:16 * k + n + 1], y[:, s:],
                                                                   ALU.mult, ALU.add)
                                    if k < 2:
                                        link(ins)
                                ins.then_inc(dve_freed, 1)
                            if to == "gated conv":
                                if n == 0:
                                    dve.wait_ge(act_freed, st["act"])
                                    dve.wait_ge(mixer_loaded, 16 * st["loads"])
                                dve.tensor_tensor(buf_a[:, n], buf_a[:, n], src[:], ALU.mult).then_inc(dve_freed, 1)
                                dve.wait_ge(dve_freed, st["dve"] + n + 1)
                                taps(buf_b[:, n], buf_a[:, n], [cols[:, 8 * k + n:8 * k + n + 1] for k in range(3)])
                            if to == "gate G":
                                if n:
                                    low(st, n - 1)
                                    dve.wait_ge(gated_low, st["gated"] + n)
                                dve.tensor_tensor(gated_conv[:], buf_b[:, n], src[:], ALU.mult).then_inc(dve_freed, 1)
                    if to == "gate G":
                        low(st, KT - 1)
                if kind == "ffn_up":
                    def up(j, four, first=False):
                        for m in range(2):
                            if m == 0:
                                dve.wait_ge(bank_full, st["full"] + 3 * j + 3)
                            else:
                                dve.wait_ge(w_used[1], st["pair"] + j + 1)
                            dve.wait_ge(act_freed, st["act"] + 2 * j + m + 1)
                            if not first:
                                dve.wait_ge(h_low, FT * nth + 2 * j + m - 1)
                            dve.tensor_tensor(hidden[:, m], gate_act[:, m], bank[4 * four + 2 + m][:], ALU.mult)\
                                .then_inc(dve_freed, 1)
                        for m in range(2):
                            dve.wait_ge(h_high, FT * nth + 2 * j + m + 1)
                            at = 2 * j + m
                            o, hi = [v[:, at] if first else v[:, bass.ds(at, 1)].rearrange("p a n -> p (a n)")
                                     for v in (h_lo, h_hi)]
                            dve.tensor_tensor(o, hidden[:, m], hi.bitcast(F32), ALU.subtract).then_inc(h_low, 1)

                    up(0, 0, True)
                    with dve.Fori(0, 5) as i:
                        for j in range(2):
                            up(2 * i + j + 1, 1 - j)
                if kind == "fox":
                    norm_rows(st, bank[2], 16, P, RMS_EPS)

                    def normalise(h):
                        dve.wait_ge(fox["norm_full"], 16 * nth + 2 * h + 2)
                        dve.scalar_tensor_tensor(q_n[:, h % 2], buf_a[:, h], cols[:, 2:3], bank[0][:],
                                                 ALU.mult, ALU.mult).then_inc(fox["qk_ready"], 1)
                        dve.tensor_tensor(k_n[:, h % 2], buf_b[:, h], bank[1][:], ALU.mult)\
                            .then_inc(fox["qk_ready"], 1)

                    def row_max(n):
                        dve.wait_ge(fox["scores"], 32 * nth + n + 1)
                        dve.tensor_reduce(soft[:, n % 4:n % 4 + 1], bank[2 + n % 3][:, 0:(n % TT + 1) * P], AX,
                                          ALU.max, negate=True).then_inc(fox["max"], 1)

                    def divide(n):
                        dve.wait_ge(fox["exps"], 32 * nth + n + 1)
                        s = soft[:, 8 + n % 4:9 + n % 4]
                        link(dve.reciprocal(s, soft[:, 4 + n % 4:5 + n % 4]))
                        p = probs[:, n % 2, 0:(n % TT + 1) * P]
                        dve.tensor_scalar(p, p, s, None, ALU.mult).then_inc(fox["normed"], 1)

                    def gate(h):
                        dve.wait_ge(fox["out_full"], 8 * nth + h + 1)
                        if h == 0:
                            dve.wait_ge(act_freed, st["act"])
                        if h:
                            dve.wait_ge(gated_low, st["gated"] + h)
                        dve.tensor_tensor(gated[:], buf_d[:, h], bank[7][:], ALU.mult).then_inc(gated_raw, 1)

                    normalise(0)
                    n_all = FOX_HEADS * TT
                    row_max(0)
                    for n in range(n_all):
                        if n + 1 < n_all:
                            row_max(n + 1)
                        divide(n)
                        if n % TT == 1 and n // TT + 1 < FOX_HEADS:
                            normalise(n // TT + 1)
                        if n % TT == 2 and n > TT:
                            gate(n // TT - 1)
                        if n % TT == 3 and n > TT:
                            low(st, n // TT - 1)
                    gate(FOX_HEADS - 1)
                    low(st, FOX_HEADS - 1)

                if kind == "attn":
                    make_selector(diff["selector"])
                    dve.wait_ge(diff["lam_out"], 1)
                    link(dve.scalar_tensor_tensor(lam_work[:, 2:3], lam_work[:, 0:1], -1.0, lam_work[:, 1:2],
                                                  ALU.mult, ALU.add))
                    link(dve.tensor_scalar(lam_work[:, 2:3], lam_work[:, 2:3], LAM_INIT, None, ALU.subtract))
                    neg_lam = lam_work[:, 2:3]

                    def pair_max(n):
                        for c in range(2):
                            k = 2 * (n % 2) + c
                            dve.wait_ge(diff["scores"], 2 * n + c + 1)
                            if n >= 2:
                                dve.wait_ge(diff["exps"], 2 * (n - 2) + c + 1)
                            dve.tensor_reduce(soft[:, k:k + 1], bank[2 * (n % 3) + c][:, 0:(n % TT + 1) * P], AX,
                                              ALU.max, negate=True).then_inc(diff["max"], 1)

                    def mix(n):
                        dve.wait_ge(diff["exps"], 2 * n + 2)
                        k = 2 * (n % 2)
                        link(dve.reciprocal(soft[:, 8 + k:10 + k], soft[:, 4 + k:6 + k]))
                        link(dve.tensor_tensor(soft[:, 12 + k:13 + k], soft[:, 9 + k:10 + k], neg_lam, ALU.mult))
                        p0, p1 = [pair_probs[:, n % 2, c, 0:(n % TT + 1) * P] for c in range(2)]
                        link(dve.tensor_scalar(p1, p1, soft[:, 12 + k:13 + k], None, ALU.mult))
                        dve.scalar_tensor_tensor(p0, p0, soft[:, 8 + k:9 + k], p1, ALU.mult, ALU.add)\
                            .then_inc(diff["mixed"], 1)

                    n_all = ATTN_HEADS * TT
                    pair_max(0)
                    for n in range(n_all):
                        if n + 1 < n_all:
                            pair_max(n + 1)
                        mix(n)
                    norm_rows(st, bank[2], 8, P, LN_EPS, n_squares=8)
                    for h in range(ATTN_HEADS):
                        dve.wait_ge(diff["spread"], h + 1)
                        if h >= 2:
                            dve.wait_ge(gated_low, st["gated"] + h - 1)
                        dve.scalar_tensor_tensor(gated_tile(st, h)[:], buf_d[:, h], cols[:, 1:2], bank[4 + h % 4][:],
                                                 ALU.mult, ALU.mult).then_inc(gated_raw, 1)
                        if h:
                            low(st, h - 1)
                    low(st, ATTN_HEADS - 1)
                if kind == "gla":
                    dve.wait_ge(w_used[1], st["pair"])
                    for h in range(GLA_HEADS):
                        dve.wait_ge(gla["decays"], 2 * h + 2)
                        link(dve.scalar_tensor_tensor(buf_b[:, h], buf_a[:, h], float(P) ** -.5, decayed[:, h],
                                                      ALU.mult, ALU.mult))
                        link(dve.tensor_tensor(buf_b[:, 4 + h], buf_a[:, 4 + h], grown[:, h], ALU.mult))
                        o, k, d_ = [v.rearrange("p (c l) -> p c l", l=CHUNK)
                                    for v in (buf_a[:, 4 + h], buf_b[:, 4 + h], decayed[:, h])]
                        dve.tensor_tensor(o, k, d_[:, :, CHUNK - 1:CHUNK].to_broadcast([P, 8, CHUNK]), ALU.mult)\
                            .then_inc(gla["keys"], 1)

                    def mask(tt):
                        dve.wait_ge(gla["inner_full"], tt + 1)
                        dve.tensor_tensor(inner[:, tt % 2], bank[2 + tt % 2][:].rearrange("p (h l) -> p h l", l=P),
                                          chunk_tri[:].unsqueeze(1).to_broadcast([P, GLA_HEADS, P]), ALU.mult)\
                            .then_inc(gla["inner"], 1)

                    mask(0)
                    for c in range(7):
                        if c % 2 == 0 and c // 2 + 1 < TT:
                            if c >= 2:
                                dve.wait_ge(gla["out_full"], c - 2)
                            mask(c // 2 + 1)
                        new, old = gla_state[:, (c + 1) % 2], gla_state[:, c % 2]
                        for g in range(2):
                            dve.wait_ge(gla["update"], 2 * c + g + 1)
                            for h in (2 * g, 2 * g + 1):
                                o = slice(h * 256, h * 256 + 256)
                                src = bank[6 + g][:, (h % 2) * 256:(h % 2) * 256 + 256]
                                if c == 0:
                                    ins = dve.tensor_copy(new[:, o], src)
                                else:
                                    ins = dve.scalar_tensor_tensor(
                                        new[:, o], old[:, o], decayed[:, h, CHUNK * (c + 1) - 1:CHUNK * (c + 1)], src,
                                        ALU.mult, ALU.add)
                                if h < 3:
                                    link(ins)
                        ins.then_inc(gla["state"], 1)
                        dve.wait_ge(gla["state"], c + 1)
                    make_selector(gla["state"])
                    norm_rows(st, bank[0], GLA_HEADS, 2 * P, RMS_EPS, n_squares=8)
                    for n in range(8):
                        h = n // 2
                        dve.wait_ge(gla["spread"], h + 1)
                        if n >= 2:
                            dve.wait_ge(gated_low, st["gated"] + n - 1)
                        o = gated_tile(st, n)[:]
                        link(dve.scalar_tensor_tensor(o, buf_a[:, n], cols[:, 4 + n % 2:5 + n % 2],
                                                      bank[4 + h][:], ALU.mult, ALU.mult))
                        dve.tensor_tensor(o, o, buf_d[:, n], ALU.mult).then_inc(gated_raw, 1)
                        if n:
                            low(st, n - 1)
                    low(st, KT - 1)
                if kind == "gdn":
                    def wide(ap, n=P):
                        return ap.unsqueeze(2).to_broadcast([P, ap.shape[1], n])

                    def four_of(b):
                        return bank[b][:].rearrange("p (a n) -> p a n", n=P)

                    dve.wait_ge(w_used[1], st["pair"])
                    link(dve.memset(delta_state[:], 0.0))
                    make_selector(gdn["selector"], GDN_V)
                    norm_rows(st, bank[1], 8, 1, RMS_EPS, n_squares=8)
                    for n in range(8):
                        dve.wait_ge(gdn["spread"], n + 1)
                        dve.scalar_tensor_tensor(buf_a[:, n], buf_a[:, n], float(P) ** -.5 if n < GDN_QK else 1.0,
                                                 bank[4 + n % 2][:], ALU.mult, ALU.mult).then_inc(gdn["qk_ready"], 1)
                    for n in range(2 * TT):
                        tt, g = divmod(n, 2)
                        dve.wait_ge(gdn["values_full"], n + 1)
                        dve.tensor_tensor(u_rows[:, tt, 4 * g:4 * g + 4], four_of(4 + g),
                                          wide(small[:, 5, tt * GDN_V + 4 * g:tt * GDN_V + 4 * g + 4]), ALU.mult)\
                            .then_inc(gdn["values_rows"], 1)
                    dve.wait_ge(gdn["keys_rows"], TT)
                    dve.tensor_copy(small[:, 7], small[:, 4]).then_inc(gdn["factors"], 1)
                    dve.wait_ge(gdn["values_rows"], 2 * TT)

                    def paired(ap):
                        return ap.unsqueeze(2).to_broadcast([P, 2, 2, P])

                    def by_pair(ap):
                        return ap.rearrange("p (a b) n -> p a b n", b=2)

                    def masked(mask):
                        return mask.unsqueeze(1).to_broadcast([P, 4, P])

                    def build(tt, g, turn):
                        four, at = slice(4 * g, 4 * g + 4), slice(tt * GDN_V + 4 * g, tt * GDN_V + 4 * g + 4)
                        kq, m = bank[2 * g + 1][:].rearrange("p (c a n) -> p c a n", c=2, n=P), tt % 2
                        if turn == 0:
                            dve.wait_ge(solve["build_full"][g], tt + 1)
                            if tt >= 2:
                                dve.wait_ge(solve["out_full"][g], tt - 1)
                            link(dve.tensor_tensor(x1[:, four], four_of(2 * g), wide(small[:, 2, at]), ALU.subtract))
                            dve.tensor_scalar(x2[:, four], x1[:, four], 0.0, None, ALU.max)\
                                .then_inc(solve["differences"][g], 1)
                            dve.tensor_scalar(qk_dec[m][:, four], x1[:, four], 0.0, None, ALU.min)\
                                .then_inc(solve["differences"][g], 1)
                        if turn == 1:
                            dve.wait_ge(solve["decays"][g], 3 * tt + 1)
                            link(dve.tensor_tensor(by_pair(x2[:, four]), by_pair(x2[:, four]), paired(kq[:, 0]), ALU.mult))
                            link(dve.tensor_tensor(x2[:, four], x2[:, four], wide(small[:, 6, at]), ALU.mult))
                        if turn == 2:
                            dve.wait_ge(solve["decays"][g], 3 * tt + 2)
                            link(dve.tensor_tensor(by_pair(qk_dec[m][:, four]), by_pair(qk_dec[m][:, four]),
                                                   paired(kq[:, 1]), ALU.mult))
                            link(dve.tensor_tensor(cross[:, four], x2[:, four], masked(across_blocks), ALU.mult))
                            dve.wait_ge(solve["differences"][g], 2 * tt + 2)
                            dve.tensor_tensor(x1[:, four], x2[:, four], masked(in_block), ALU.mult)\
                                .then_inc(solve["lower"][g], 1)
                        if turn == 3:
                            keys = key_rows[:, tt, 2 * g * P:(2 * g + 2) * P].rearrange("p (a n) -> p a n", n=P)
                            link(dve.tensor_tensor(by_pair(k_dec[m][:, four]), paired(keys),
                                                   by_pair(wide(small[:, 3, at])), ALU.mult))
                            dve.wait_ge(solve["decays"][g], 3 * tt + 3)
                            link(dve.tensor_copy(chunk_decay[:, tt, four], x3[:, four, CHUNK - 1::CHUNK]))
                            link(dve.tensor_tensor(by_pair(q_dec[m][:, four]),
                                                   paired(buf_a[:, 2 * g:2 * g + 2, tt * P:tt * P + P]),
                                                   by_pair(x3[:, four]), ALU.mult))
                            dve.tensor_tensor(qk_dec[m][:, four], qk_dec[m][:, four], masked(chunk_tri[:]), ALU.mult)\
                                .then_inc(solve["late"][g], 1)

                    def take_step(tt, g, n):
                        four = slice(4 * g, 4 * g + 4)
                        src = four_of(2 * g + n % 2)
                        dve.wait_ge(solve["full"][g], LAST_STEP * tt + n)
                        if n in ACT_STEPS:
                            solved(dve, g, tt, n, ("act",))
                        if n in (1, 11):
                            o, other = (inverse if n == 1 else x2)[:, four], masked(ident[:])
                        elif n == 14:
                            o = other = x2[:, four]
                        else:
                            o = other = inverse[:, four]
                        if n == 17:
                            ins = dve.tensor_copy(u_rows[:, tt, four], src)
                        else:
                            ins = dve.tensor_tensor(o, other, src, ALU.add)
                        ins.then_inc(solve["dve"][g], 1)
                        if n == 14:
                            at = slice(tt * GDN_V + 4 * g, tt * GDN_V + 4 * g + 4)
                            keys = key_rows[:, tt, 2 * g * P:(2 * g + 2) * P].rearrange("p (a n) -> p a n", n=P)
                            dve.tensor_tensor(by_pair(x3[:, four]), paired(keys), by_pair(wide(small[:, 4, at])), ALU.mult)\
                                .then_inc(solve["kbg"][g], 1)

                    def new_values(c, g):
                        tt, rows = c // 2, slice(CHUNK * (c % 2), CHUNK * (c % 2) + CHUNK)
                        four = slice(4 * g, 4 * g + 4)
                        solved(dve, g, tt, LAST_STEP)
                        dve.wait_ge(solve["ws"][g], c + 1)
                        dve.tensor_tensor(v_new[rows, four], u_rows[rows, tt, four], four_of(4 + g)[rows], ALU.subtract)\
                            .then_inc(solve["v_new"][g], 1)

                    def update(c, g):
                        dve.wait_ge(solve["update"][g], c + 1)
                        for i in range(4):
                            h = 4 * g + i
                            ins = dve.scalar_tensor_tensor(
                                delta_state[:, h], delta_state[:, h], chunk_decay[:, c // 2, h, c % 2:c % 2 + 1],
                                bank[4 + g][:, i * P:i * P + P], ALU.mult, ALU.add)
                            if i < 3:
                                link(ins)
                        ins.then_inc(solve["state"][g], 1)

                    for tt, g, turn in staggered():
                        if tt < TT and turn < BUILD_TURNS:
                            build(tt, g, turn)
                        if tt < TT and turn - BUILD_TURNS + 1 in DVE_STEPS:
                            take_step(tt, g, turn - BUILD_TURNS + 1)
                        if tt and turn in RECURRENCE_TURNS:
                            part = RECURRENCE_TURNS.index(turn)
                            c = 2 * (tt - 1) + part // 2
                            if part % 2 == 0:
                                new_values(c, g)
                            elif c < 2 * TT - 1:
                                update(c, g)
                    norm_rows(st, bank[0], 8, P, RMS_EPS, norm=1, base=8, n_squares=8)
                    for h in range(GDN_V):
                        dve.wait_ge(gdn["norm_spread"], h + 1)
                        if h >= 2:
                            dve.wait_ge(gated_low, st["gated"] + h - 1)
                        o = gated_tile(st, h)[:]
                        link(dve.scalar_tensor_tensor(by_tile(o), u_rows[:, :, h], cols[:, 64:65],
                                                      by_tile(bank[4 + h % 4][:]), ALU.mult, ALU.mult))
                        dve.tensor_tensor(o, o, buf_d[:, h], ALU.mult).then_inc(gated_raw, 1)
                        if h:
                            low(st, h - 1)
                    low(st, GDN_V - 1)


_INS = ["x", "norm_w", "fox_w_in", "fox_b_f", "fox_q_gain", "fox_k_gain", "fox_w_out", "gla_w_in", "gla_w_gate_up",
        "gla_b_gate", "gla_o_gain", "gla_w_out", "gdn_w_in", "gdn_conv_w", "gdn_a_log", "gdn_dt_bias", "gdn_o_gain",
        "gdn_w_out", "attn_w_qkv_2", "attn_w_o_2", "attn_lambda_q1_2", "attn_lambda_k1_2", "attn_lambda_q2_2",
        "attn_lambda_k2_2", "attn_subln_g_2", "conv_w_in_2", "conv_w_2", "conv_w_out_2", "ffn_w_gate_2",
        "ffn_w_up_2", "ffn_w_down_2", "ln1_g_2", "ln1_b_2", "ln2_g_2", "ln2_b_2"]


def kernel(**inputs):
    import concourse.bacc as _bacc
    from concourse.bass_utils import run_bass_kernel_spmd as _run

    nc = _bacc.Bacc("TRN2", target_bir_lowering=False, num_devices=1)
    arrays = {f"in_{name}_dram": np.ascontiguousarray(inputs[name]) for name in _INS}
    arrays["rotary_dram"] = rotary_tables()
    arrays["block_masks_dram"] = block_masks()
    t = {name: nc.dram_tensor(f"in_{name}_dram", arrays[f"in_{name}_dram"].shape, F32, kind="ExternalInput").ap()
         for name in _INS}
    t["rotary"] = nc.dram_tensor("rotary_dram", arrays["rotary_dram"].shape, F32, kind="ExternalInput").ap()
    t["block_masks"] = nc.dram_tensor("block_masks_dram", (3, P, P), F32, kind="ExternalInput").ap()
    out = nc.dram_tensor("out_0_dram", (1, SEQ, D), F32, kind="ExternalOutput").ap()
    six_mixer_stack(nc, t, out)
    r = _run(nc, [arrays], core_ids=[0])
    return r.results[0]["out_0_dram"]
```
